# Optimizing a Trainium2 kernel written in Bass

```python
import math
import jax
import jax.numpy as jnp
from jax import lax

D_MODEL = 1024
BATCH = 1
SEQ = 256
DEPTH = 2

CTX_LEN = 256
GRID_W = 64
D_MIX = D_MODEL
DIFF_HEADS = 4
DIFF_HEAD_DIM = 32
DIFF_V_DIM = 2 * DIFF_HEAD_DIM
DIFF_WIDTH = DIFF_HEADS * DIFF_V_DIM
HGRN_HEADS = 4
HGRN_K = 128
HGRN_V = 128
HGRN_WIDTH = HGRN_HEADS * HGRN_V
HGRN_CHUNK = 32
SWA_Q_HEADS = 4
SWA_KV_HEADS = 2
SWA_GROUP = SWA_Q_HEADS // SWA_KV_HEADS
SWA_HEAD_DIM = 64
SWA_WIDTH = SWA_Q_HEADS * SWA_HEAD_DIM
WINDOW = 128
Q_BLOCK = 128
D_FF = 2816
N_EXPERTS = 8
TOP_K = 2
ROPE_BASE = 10000.0
NORM_EPS = 1e-6
IN_SIZES = (DIFF_WIDTH,) * 3 + (HGRN_WIDTH,) * 5 + (SWA_WIDTH, SWA_KV_HEADS * SWA_HEAD_DIM, SWA_KV_HEADS * SWA_HEAD_DIM)
D_IN = sum(IN_SIZES)
N_DENSE = (DEPTH + 1) // 2
N_MOE = DEPTH // 2
F32 = jnp.float32

kernel_name = 'hymba_style_diffusion_hybrid_trunk'

def rmsnorm(x, g):
    xf = x.astype(F32)
    y = xf * lax.rsqrt(jnp.mean(xf * xf, axis=-1, keepdims=True) + NORM_EPS)
    return (y * g.astype(F32)).astype(x.dtype)

def grid_positions(n_tokens):
    rows = n_tokens // GRID_W
    row = jnp.repeat(jnp.arange(rows, dtype=jnp.int32), GRID_W)
    col = jnp.tile(jnp.arange(GRID_W, dtype=jnp.int32), rows)
    return row, col

def _rotate(xp, pos):
    nf = xp.shape[-1] // 2
    inv = ROPE_BASE ** (-jnp.arange(nf, dtype=F32) / nf)
    ang = pos.astype(F32)[:, None] * inv[None, :]
    shape = (1, pos.shape[0]) + (1,) * (xp.ndim - 3) + (nf,)
    cos = jnp.cos(ang).reshape(shape).astype(xp.dtype)
    sin = jnp.sin(ang).reshape(shape).astype(xp.dtype)
    x1, x2 = xp[..., :nf], xp[..., nf:]
    return jnp.concatenate([x1 * cos - x2 * sin, x1 * sin + x2 * cos], axis=-1)

def axial_rope(x, row, col):
    half = x.shape[-1] // 2
    return jnp.concatenate([_rotate(x[..., :half], row), _rotate(x[..., half:], col)], axis=-1)

def map_query_blocks(fn, q):
    b, n = q.shape[:2]
    nb = n // Q_BLOCK
    qb = jnp.moveaxis(q.reshape((b, nb, Q_BLOCK) + q.shape[2:]), 1, 0)
    out = lax.map(lambda a: fn(a[0], a[1]), (qb, jnp.arange(nb, dtype=jnp.int32)))
    out = jnp.moveaxis(out, 0, 1)
    return out.reshape((b, n) + out.shape[3:])

def split_projection(h, w):
    p = jnp.einsum('bld,de->ble', h, w)
    points, acc = [], 0
    for s in IN_SIZES[:-1]:
        acc += s
        points.append(acc)
    return jnp.split(p, points, axis=-1)

def _diff_core(q, k, v, lam):
    s = jnp.einsum('bqhmd,bkhmd->bhmqk', q, k, preferred_element_type=F32) * (DIFF_HEAD_DIM ** -0.5)
    p = jax.nn.softmax(s, axis=-1)
    a = p[:, :, 0] - lam * p[:, :, 1]
    return jnp.einsum('bhqk,bkhe->bqhe', a.astype(v.dtype), v)

def diff_attention_mixer(lat, ctx, row, col, qk_g, lam_vec, lam_init, sub_g, need_ctx):
    def prep(q, k, v, rotary):
        b, n, _ = q.shape
        q = rmsnorm(q.reshape(b, n, DIFF_HEADS, 2, DIFF_HEAD_DIM), qk_g[0])
        k = rmsnorm(k.reshape(b, n, DIFF_HEADS, 2, DIFF_HEAD_DIM), qk_g[1])
        if rotary:
            q, k = axial_rope(q, row, col), axial_rope(k, row, col)
        return q, k, v.reshape(b, n, DIFF_HEADS, DIFF_V_DIM)

    q_l, k_l, v_l = prep(*lat, True)
    q_c, k_c, v_c = prep(*ctx, False)
    lv = lam_vec.astype(F32)
    lam = jnp.exp(jnp.sum(lv[0] * lv[1])) - jnp.exp(jnp.sum(lv[2] * lv[3])) + lam_init
    k_all = jnp.concatenate([k_c, k_l], axis=1)
    v_all = jnp.concatenate([v_c, v_l], axis=1)

    def post(o):
        b, n = o.shape[:2]
        return (rmsnorm(o, sub_g) * (1.0 - lam_init)).reshape(b, n, DIFF_WIDTH)

    o_l = post(map_query_blocks(lambda qb, i: _diff_core(qb, k_all, v_all, lam), q_l))
    o_c = post(_diff_core(q_c, k_c, v_c, lam)) if need_ctx else None
    return o_l, o_c

def _hgrn_gates(f_logit, lb):
    lb = lb.reshape(HGRN_HEADS, HGRN_K).astype(F32)
    log_f = jnp.logaddexp(jnp.log(lb), jnp.log1p(-lb) + jax.nn.log_sigmoid(f_logit))
    return -jnp.expm1(log_f), log_f

def _hgrn2_chunkwise(q, k, v, log_f, s0):
    b, n, h, kd = q.shape
    nc = n // HGRN_CHUNK

    def to_chunks(t):
        return jnp.moveaxis(t.reshape(b, nc, HGRN_CHUNK, h, t.shape[-1]), 1, 0)

    causal = jnp.tril(jnp.ones((HGRN_CHUNK, HGRN_CHUNK), dtype=bool))[None, :, :, None, None]

    def step(s, inp):
        qc, kc, vc, lfc = inp
        cum = jnp.cumsum(lfc, axis=1)
        dec = jnp.exp(jnp.where(causal, cum[:, :, None] - cum[:, None], -jnp.inf))
        scores = jnp.sum(qc[:, :, None] * kc[:, None] * dec, axis=-1)
        o = jnp.einsum('btsh,bshv->bthv', scores, vc)
        o = o + jnp.einsum('bthk,bhkv->bthv', qc * jnp.exp(cum), s)
        last = cum[:, -1]
        k_dec = kc * jnp.exp(last[:, None] - cum)
        s_new = jnp.exp(last)[..., None] * s + jnp.einsum('bshk,bshv->bhkv', k_dec, vc)
        return s_new, o

    s_fin, o = lax.scan(step, s0, (to_chunks(q), to_chunks(k), to_chunks(v), to_chunks(log_f)))
    o = jnp.moveaxis(o, 0, 1).reshape(b, n, h, v.shape[-1])
    return o, s_fin

def hgrn2_mixer(lat, ctx, lb_fwd, lb_bwd, norm_g, need_ctx):
    def prep(q, i, f_fwd, f_bwd, g):
        b, n, _ = q.shape
        heads = lambda t: t.reshape(b, n, HGRN_HEADS, -1).astype(F32)
        return (jax.nn.silu(heads(q)), heads(i), _hgrn_gates(heads(f_fwd), lb_fwd),
                _hgrn_gates(heads(f_bwd), lb_bwd), g)

    q_l, i_l, (kf_l, lf_l), (kb_l, lb_l), g_l = prep(*lat)
    q_c, i_c, (kf_c, lf_c), (kb_c, lb_c), g_c = prep(*ctx)
    s0 = jnp.zeros((q_l.shape[0], HGRN_HEADS, HGRN_K, HGRN_V), F32)
    rev = lambda t: jnp.flip(t, axis=1)
    o_cf, s_cf = _hgrn2_chunkwise(q_c, kf_c, i_c, lf_c, s0)
    o_lf, _ = _hgrn2_chunkwise(q_l, kf_l, i_l, lf_l, s_cf)
    o_cb, s_cb = _hgrn2_chunkwise(rev(q_c), rev(kb_c), rev(i_c), rev(lb_c), s0)
    o_lb, _ = _hgrn2_chunkwise(rev(q_l), rev(kb_l), rev(i_l), rev(lb_l), s_cb)

    def post(o, g):
        b, n = o.shape[:2]
        o = rmsnorm(o, norm_g).reshape(b, n, HGRN_WIDTH)
        return (o * jax.nn.silu(g.astype(F32))).astype(g.dtype)

    out_l = post(o_lf + rev(o_lb), g_l)
    out_c = post(o_cf + rev(o_cb), g_c) if need_ctx else None
    return out_l, out_c

def _sink_softmax(logits, sink):
    m = jnp.maximum(jnp.max(logits, axis=-1, keepdims=True), sink)
    e = jnp.exp(logits - m)
    return e / (jnp.sum(e, axis=-1, keepdims=True) + jnp.exp(sink - m))

def swa_mixer(lat, ctx, row, col, qk_g, sink, need_ctx):
    def prep(q, k, v, rotary):
        b, n, _ = q.shape
        q = rmsnorm(q.reshape(b, n, SWA_Q_HEADS, SWA_HEAD_DIM), qk_g[0])
        k = rmsnorm(k.reshape(b, n, SWA_KV_HEADS, SWA_HEAD_DIM), qk_g[1])
        if rotary:
            q, k = axial_rope(q, row, col), axial_rope(k, row, col)
        return q.reshape(b, n, SWA_KV_HEADS, SWA_GROUP, SWA_HEAD_DIM), k, v.reshape(b, n, SWA_KV_HEADS, SWA_HEAD_DIM)

    q_l, k_l, v_l = prep(*lat, True)
    q_c, k_c, v_c = prep(*ctx, False)
    scale = SWA_HEAD_DIM ** -0.5
    sink_b = sink.astype(F32).reshape(1, SWA_KV_HEADS, SWA_GROUP, 1, 1)
    b, n_lat = q_l.shape[:2]
    n_ctx = k_c.shape[1]
    span = Q_BLOCK + 2 * WINDOW
    pad = ((0, 0), (WINDOW, WINDOW), (0, 0), (0, 0))
    kp, vp = jnp.pad(k_l, pad), jnp.pad(v_l, pad)

    def block(qb, i):
        start = i * Q_BLOCK
        kw = lax.dynamic_slice_in_dim(kp, start, span, axis=1)
        vw = lax.dynamic_slice_in_dim(vp, start, span, axis=1)
        s_w = jnp.einsum('bqhgd,bkhd->bhgqk', qb, kw, preferred_element_type=F32) * scale
        qpos = start + jnp.arange(Q_BLOCK)
        kpos = start - WINDOW + jnp.arange(span)
        valid = (jnp.abs(qpos[:, None] - kpos[None, :]) <= WINDOW) & (kpos[None, :] >= 0) & (kpos[None, :] < n_lat)
        s_w = jnp.where(valid, s_w, -jnp.inf)
        s_c = jnp.einsum('bqhgd,bkhd->bhgqk', qb, k_c, preferred_element_type=F32) * scale
        p = _sink_softmax(jnp.concatenate([s_c, s_w], axis=-1), sink_b).astype(v_l.dtype)
        return (jnp.einsum('bhgqk,bkhd->bqhgd', p[..., :n_ctx], v_c)
                + jnp.einsum('bhgqk,bkhd->bqhgd', p[..., n_ctx:], vw))

    o_l = map_query_blocks(block, q_l).reshape(b, n_lat, SWA_WIDTH)
    o_c = None
    if need_ctx:
        s = jnp.einsum('bqhgd,bkhd->bhgqk', q_c, k_c, preferred_element_type=F32) * scale
        p = _sink_softmax(s, sink_b).astype(v_c.dtype)
        o_c = jnp.einsum('bhgqk,bkhd->bqhgd', p, v_c).reshape(b, n_ctx, SWA_WIDTH)
    return o_l, o_c

def swiglu(h, w1, w3, w2):
    return jnp.matmul(jax.nn.silu(jnp.matmul(h, w1)) * jnp.matmul(h, w3), w2)

def moe_swiglu(h, router, w1, w3, w2):
    logits = jnp.einsum('bld,de->ble', h, router, preferred_element_type=F32)
    top_v, top_i = lax.top_k(logits, TOP_K)
    wts = jax.nn.softmax(top_v, axis=-1)
    gates = jnp.sum(jax.nn.one_hot(top_i, N_EXPERTS, dtype=F32) * wts[..., None], axis=-2)
    y = jnp.zeros_like(h)
    for e in range(N_EXPERTS):
        y = y + gates[..., e:e + 1].astype(h.dtype) * swiglu(h, w1[e], w3[e], w2[e])
    return y

def channel_mixer(h, layer, ffn_w1, ffn_w3, ffn_w2, moe_router, moe_w1, moe_w3, moe_w2):
    j = layer // 2
    if layer % 2 == 0:
        return swiglu(h, ffn_w1[j], ffn_w3[j], ffn_w2[j])
    return moe_swiglu(h, moe_router[j], moe_w1[j], moe_w3[j], moe_w2[j])

def setup_inputs(seed: int = 0) -> dict:
    key = jax.random.key(seed)
    ks = jax.random.split(key, 24)
    nrm = lambda k, shape, s: jax.random.normal(k, shape, F32) * s
    gain = lambda k, shape: 1.0 + 0.02 * jax.random.normal(k, shape, F32)
    return {
        'x': nrm(ks[0], (BATCH, SEQ, D_MODEL), 1.0),
        'c': nrm(ks[1], (BATCH, D_MODEL), 1.0),
        'ctx': nrm(ks[2], (BATCH, CTX_LEN, D_MODEL), 1.0),
        'c_ctx': nrm(ks[3], (D_MODEL,), 1.0),
        'ada_w': nrm(ks[4], (DEPTH, D_MODEL, 6 * D_MODEL), 0.5 * D_MODEL ** -0.5),
        'ada_b': nrm(ks[5], (DEPTH, 6 * D_MODEL), 0.02),
        'norm_mix_g': gain(ks[6], (DEPTH, D_MODEL)),
        'norm_ffn_g': gain(ks[7], (DEPTH, D_MODEL)),
        'w_in': nrm(ks[8], (DEPTH, D_MODEL, D_IN), D_MODEL ** -0.5),
        'w_out': nrm(ks[9], (DEPTH, D_MIX, D_MODEL), D_MIX ** -0.5),
        'diff_qk_norm_g': gain(ks[10], (DEPTH, 2, DIFF_HEAD_DIM)),
        'diff_lambda': nrm(ks[11], (DEPTH, 4, DIFF_HEAD_DIM), 0.1),
        'diff_subln_g': gain(ks[12], (DEPTH, DIFF_V_DIM)),
        'hgrn_lb_logits': nrm(ks[13], (2, DEPTH, HGRN_WIDTH), 0.5),
        'hgrn_norm_g': gain(ks[14], (DEPTH, HGRN_V)),
        'swa_qk_norm_g': gain(ks[15], (DEPTH, 2, SWA_HEAD_DIM)),
        'swa_sink': nrm(ks[16], (DEPTH, SWA_Q_HEADS), 0.5),
        'ffn_w1': nrm(ks[17], (N_DENSE, D_MODEL, D_FF), D_MODEL ** -0.5),
        'ffn_w3': nrm(ks[18], (N_DENSE, D_MODEL, D_FF), D_MODEL ** -0.5),
        'ffn_w2': nrm(ks[19], (N_DENSE, D_FF, D_MODEL), D_FF ** -0.5),
        'moe_router': nrm(ks[20], (N_MOE, D_MODEL, N_EXPERTS), D_MODEL ** -0.5),
        'moe_w1': nrm(ks[21], (N_MOE, N_EXPERTS, D_MODEL, D_FF), D_MODEL ** -0.5),
        'moe_w3': nrm(ks[22], (N_MOE, N_EXPERTS, D_MODEL, D_FF), D_MODEL ** -0.5),
        'moe_w2': nrm(ks[23], (N_MOE, N_EXPERTS, D_FF, D_MODEL), D_FF ** -0.5),
    }

def reference(x, c, ctx, c_ctx, ada_w, ada_b, norm_mix_g, norm_ffn_g, w_in, w_out,
              diff_qk_norm_g, diff_lambda, diff_subln_g, hgrn_lb_logits, hgrn_norm_g,
              swa_qk_norm_g, swa_sink, ffn_w1, ffn_w3, ffn_w2, moe_router, moe_w1, moe_w3, moe_w2):
    row, col = grid_positions(x.shape[1])
    lb = jnp.cumsum(jax.nn.softmax(hgrn_lb_logits.astype(F32), axis=1), axis=1)
    lb = lb - lb[:, :1]
    silu_c = jax.nn.silu(c)
    silu_cc = jax.nn.silu(c_ctx)
    for layer in range(DEPTH):
        need_ctx = layer < DEPTH - 1
        m_l = [m[:, None, :] for m in jnp.split(silu_c @ ada_w[layer] + ada_b[layer], 6, axis=-1)]
        m_c = jnp.split(silu_cc @ ada_w[layer] + ada_b[layer], 6, axis=-1)
        h_l = rmsnorm(x, norm_mix_g[layer]) * (1 + m_l[1]) + m_l[0]
        h_c = rmsnorm(ctx, norm_mix_g[layer]) * (1 + m_c[1]) + m_c[0]
        p_l = split_projection(h_l, w_in[layer])
        p_c = split_projection(h_c, w_in[layer])
        lam_init = 0.8 - 0.6 * math.exp(-0.3 * layer)
        a_l, a_c = diff_attention_mixer(tuple(p_l[0:3]), tuple(p_c[0:3]), row, col, diff_qk_norm_g[layer],
                                        diff_lambda[layer], lam_init, diff_subln_g[layer], need_ctx)
        b_l, b_c = hgrn2_mixer(tuple(p_l[3:8]), tuple(p_c[3:8]), lb[0, layer], lb[1, layer],
                               hgrn_norm_g[layer], need_ctx)
        c_l, c_c = swa_mixer(tuple(p_l[8:11]), tuple(p_c[8:11]), row, col, swa_qk_norm_g[layer],
                             swa_sink[layer], need_ctx)
        x = x + m_l[2] * (jnp.concatenate([a_l, b_l, c_l], axis=-1) @ w_out[layer])
        if need_ctx:
            ctx = ctx + m_c[2] * (jnp.concatenate([a_c, b_c, c_c], axis=-1) @ w_out[layer])
        h2 = rmsnorm(x, norm_ffn_g[layer]) * (1 + m_l[4]) + m_l[3]
        x = x + m_l[5] * channel_mixer(h2, layer, ffn_w1, ffn_w3, ffn_w2, moe_router, moe_w1, moe_w3, moe_w2)
        if need_ctx:
            h2c = rmsnorm(ctx, norm_ffn_g[layer]) * (1 + m_c[4]) + m_c[3]
            ctx = ctx + m_c[5] * channel_mixer(h2c, layer, ffn_w1, ffn_w3, ffn_w2, moe_router, moe_w1, moe_w3, moe_w2)
    return x


_drawn_inputs = setup_inputs


def setup_inputs(seed=0):
    import zlib

    import numpy as np

    out = dict(_drawn_inputs(seed))
    spreads = {}
    factors = {'norm_mix_g': 6.389,
     'norm_ffn_g': 3.872,
     'diff_qk_norm_g': 8.0,
     'diff_lambda': 2.712,
     'diff_subln_g': 50.52,
     'hgrn_lb_logits': 8.0,
     'hgrn_norm_g': 6.904,
     'swa_qk_norm_g': 8.0,
     'swa_sink': 8.0}
    for name, (base, spread) in spreads.items():
        noise = np.random.default_rng([zlib.crc32(name.encode()), seed]).standard_normal(out[name].shape)
        drawn = base * np.exp(spread * noise) if base else spread * noise
        out[name] = jnp.asarray(drawn.astype(out[name].dtype))
    for name, factor in factors.items():
        out[name] = (out[name] * factor).astype(out[name].dtype)
    return out
```

```python
from contextlib import ExitStack
import math

import numpy as np
import concourse.bass as bass
import concourse.mybir as mybir

F32 = mybir.dt.float32
U8 = mybir.dt.uint8
I32 = mybir.dt.int32
ALU = mybir.AluOpType
ACT = mybir.ActivationFunctionType
AX = mybir.AxisListType

P = 128
D = 1024
KC = D // P
NT = 4
CTX_TILES, LAT_TILES = (0, 1), (2, 3)
DEPTH = 2
D_IN = 3840
D_FF = 2816
FC = D_FF // P
N_EXP = 8
EPS = 1e-6
GRID_W = 64
WINDOW = 128
NH = 4
C_AQK, C_AV, C_BQ, C_BI, C_BFF, C_BFB, C_BG, C_C = 0, 512, 768, 1280, 1792, 2304, 2816, 3328
LEVELS = [1, 2, 4, 8, 16, 32, 64]
FT = [(0, 512), (512, 512), (1024, 512), (1536, 512), (2048, 512), (2560, 256)]
SLOT = KC * 512

K_ID, K_TRI, K_ONE, K_IOTA, K_C32, K_S32, K_C64, K_S64, K_SWA, K_REV, K_SELT, K_E12 = range(12)
K_WIDTH = {K_ID: 128, K_TRI: 128, K_ONE: 128, K_IOTA: 128, K_C32: 64, K_S32: 64, K_C64: 128,
           K_S64: 128, K_SWA: 256, K_REV: 16, K_SELT: 256, K_E12: 24}
K_AT = {k: sum(K_WIDTH[j] for j in range(k)) for k in K_WIDTH}
K_ALL = sum(K_WIDTH.values())


def constants():
    k = np.zeros((P, K_ALL), np.float32)

    def put(name, a):
        a = np.asarray(a, np.float32)
        k[:a.shape[0], K_AT[name]:K_AT[name] + a.shape[1]] = a

    i = np.arange(P)
    put(K_ID, np.eye(P))
    put(K_TRI, i[:, None] < i[None, :])
    put(K_ONE, np.ones((P, P)))
    put(K_IOTA, np.broadcast_to(i, (P, P)))
    tok = np.arange(2 * P)
    row, col = tok // GRID_W, tok % GRID_W
    for dim, kc, ks in ((32, K_C32, K_S32), (64, K_C64, K_S64)):
        nf = dim // 4
        inv = (np.float32(10000.0) ** (-np.arange(nf, dtype=np.float32) / np.float32(nf))).astype(np.float32)
        c, s = np.zeros((2 * P, dim)), np.zeros((2 * P, dim))
        for half, pos in enumerate((row, col)):
            ang = (pos.astype(np.float32)[:, None] * inv[None, :]).astype(np.float32).astype(np.float64)
            a = half * 2 * nf
            c[:, a:a + nf] = c[:, a + nf:a + 2 * nf] = np.cos(ang)
            s[:, a:a + nf] = -np.sin(ang)
            s[:, a + nf:a + 2 * nf] = np.sin(ang)
        put(kc, c.reshape(2, P, dim).transpose(1, 0, 2).reshape(P, 2 * dim))
        put(ks, s.reshape(2, P, dim).transpose(1, 0, 2).reshape(P, 2 * dim))
    swa = np.zeros((P, 2, P), np.float32)
    for b in range(2):
        swa[:, b] = np.where(np.abs((b * P + i)[:, None] - ((1 - b) * P + i)[None, :]) <= WINDOW, 0.0, -1e30)
    put(K_SWA, swa.reshape(P, -1))
    put(K_REV, np.broadcast_to(np.tile(8.0 - np.arange(8), 2), (P, 16)))
    sel = np.zeros((2, 2, P))
    sel[0, 0] = sel[1, 1] = 1
    put(K_SELT, sel.reshape(2, -1))
    e12 = np.zeros((12, 12, 2))
    e12[np.arange(12), np.arange(12)] = 1
    put(K_E12, e12.reshape(12, -1))
    m8 = np.zeros((P, 2, len(LEVELS), P), np.float32)
    s, t = i[:, None], i[None, :]
    for n, m in enumerate(LEVELS):
        same = s // (2 * m) == t // (2 * m)
        m8[:, 0, n] = same & (s % (2 * m) < m) & (t % (2 * m) >= m)
        m8[:, 1, n] = same & (s % (2 * m) >= m) & (t % (2 * m) < m)
    return k, m8.reshape(P, -1)


def bc(ap, axis, n):
    ap = ap.unsqueeze(axis)
    shape = list(ap.shape)
    shape[axis] = n
    return ap.to_broadcast(shape)


def trunk(nc, t):
    ctx = ExitStack()
    with ctx:
        def sb(name, shape, dt=F32):
            return ctx.enter_context(nc.sbuf_tensor(name, shape, dt))

        sems = {}

        def S(name):
            if name not in sems:
                sems[name] = ctx.enter_context(nc.semaphore(name))
            return sems[name]

        X = sb("X", [P, NT, D])
        GATE = sb("GATE", [P, 2, 2, D])
        K = sb("K", [P, K_ALL])
        M8 = sb("M8", [P, 2, len(LEVELS), P], U8)
        ARENA = sb("ARENA", [P, 161 * 256])
        MT = sb("MT", [P, 6, KC, 2])
        SC = sb("SC", [P, KC, 2])
        CIN = sb("CIN", [P, KC, 2])
        GMIX = sb("GMIX", [P, DEPTH, KC])
        GFFN = sb("GFFN", [P, DEPTH, KC])
        QKG = sb("QKG", [P, DEPTH, 2, 32])
        SUBG = sb("SUBG", [P, DEPTH, 64])
        HNG = sb("HNG", [P, DEPTH, 128])
        SQKG = sb("SQKG", [P, DEPTH, 2, 64])
        SINK = sb("SINK", [P, DEPTH, NH])
        NSINK = sb("NSINK", [P, DEPTH, NH])
        LBL = sb("LBL", [P, 2, DEPTH, NH])
        LBT = sb("LBT", [P, 6, 2, NH])
        LAM = sb("LAM", [P, DEPTH, 6])
        ROUT = sb("ROUT", [P, KC, N_EXP])
        NEGH = sb("NEGH", [P, 64])
        STAT = sb("STAT", [P, 4, 96])
        PS = ctx.enter_context(nc.psum_tensor("PS", [P, 8, 512], F32))

        def B(i):
            return PS[:, i, :]

        def kc(name, w=None):
            return K[:, K_AT[name]:K_AT[name] + (w or K_WIDTH[name])]

        ident = kc(K_ID)

        def A(at, *shape):
            n = int(np.prod(shape))
            a = int(at * 256)
            v = ARENA[:, a:a + n]
            names = "abcde"[:len(shape)]
            if len(shape) == 1:
                return v
            return v.rearrange(f"p ({' '.join(names)}) -> p {' '.join(names)}", **dict(zip(names[1:], shape[1:])))

        HT = A(0, KC, 512)
        ST = [A(0, NH, 512), A(8, NH, 512)]
        Q = A(16, NH, 512)
        QP = [A(24, NH, 512), A(32, NH, 512)]
        KE = [A(40, NH, 512), A(48, NH, 512)]
        FG = [A(56, NH, 512), A(64, NH, 512)]
        TB = [A(108, 1024), A(112, 1024)]
        SST = A(56, 3, 2, NH, P)
        KDT = A(68, 2, NH, P)
        V = A(72, NT, 512)
        G = A(80, NT, 512)
        AQK = A(88, NT, 512)
        AV = A(96, NT, 256)
        CQKV = A(100, NT, 512)
        MIX = A(108, NT, D)
        XN = A(24, NT, D)
        TMP = A(108, NT, 512)
        TMP2 = A(116, NT, 512)
        RING = [A(129, KC, 512), A(145, KC, 512)]
        QKT = A(0, 4, 512)
        CT = A(8, 3, 512)
        EX = A(24, 2, 2, 512)
        AT = A(32, 2, 512)
        MSK = A(36, 2, 512)
        OT = A(40, NT, 512)
        AST = A(48, 6, 32, 2)
        LAMV = A(0, DEPTH, 4, 32)
        MASKF = A(60, 2 * len(LEVELS) * P)
        YT = A(24, 2, 512)
        ADAB = A(0, 512)
        MROW = A(2, 2, 512)
        ACTT = A(16, FC, 512)
        FTMP = A(61, 8, 512)

        in_layer0 = {
            "adab_loaded": 16, "ada_mm": 12, "ada_row": 12, "ada_spread": 12, "ada_cp": 12,
            "proj_mm": 8 * NT, "proj_act": 4 * NT, "proj_dve": 4 * NT,
            "qk_sq": 2, "qk_ss": 2, "qk_ms": 2, "qk_rstd": 2, "qk_x": 1 + NT, "qk_gained": 4, "qk_turned": 12,
            "qk_rotated": 4,
            "s_kt": 6, "s_kd": 6, "s_kv": 6, "s_st": 6 * NH, "s_o": NT, "t_tp": 7,
            "a_msk": 2 * 2 * NH, "o_tp": KC, "o_mt_act": KC // 2, "o_mt_dve": KC // 2, "o_gated": 2 * NT,
            "o_added": 2 * NT, "out_mm": 2 * NT}
        for d in range(2):
            in_layer0.update({f"h{d}_f": 0, f"h{d}_qp": 1, f"h{d}_mm": 1 + len(LEVELS), f"h{d}_taken": 1 + len(LEVELS),
                              f"h{d}_upd": 3 * len(LEVELS)})
        for step in ("s", "mx", "nb", "exp", "r", "ratio", "p", "pt", "at", "pv", "o"):
            in_layer0["a_" + step] = 2 * NH * NT

        def since(L, name):
            return L * in_layer0[name]

        plan, index = [], {}

        def item(key, pieces, release):
            index[key] = len(plan)
            plan.append((pieces, release))

        def cols(w, a, n):
            return w.rearrange("(k p) n -> p k n", p=P)[:, :, a:a + n]

        def proj_units(L):
            out = []
            lat = LAT_TILES if L == DEPTH - 1 else range(NT)
            for key, kind, c0, w, eng in (
                    ("bq", "T", C_BQ, 512, "act"), ("aqk", "N", C_AQK, 512, "dve"),
                    ("bff", "T", C_BFF, 512, "act"), ("c", "N", C_C, 512, "dve"),
                    ("bfb", "T", C_BFB, 512, "act"), ("bi", "N", C_BI, 512, "dve"),
                    ("bg", "N", C_BG, 512, "act"), ("av", "N", C_AV, 256, "dve")):
                for u in (lat if key == "bg" else range(4)):
                    out.append((key, u, kind, c0, w, eng))
            return out

        for L in range(DEPTH):
            for j in range(12):
                item(("ada", L, j), [(slice(0, 512), cols(t["ada_w"][L], 512 * j, 512))], ("ada_mm", since(L, "ada_mm") + j + 1))
            units = proj_units(L)
            for key in dict.fromkeys(u[0] for u in units):
                c0, w = next((u[3], u[4]) for u in units if u[0] == key)
                last = max(i for i, u in enumerate(units) if u[0] == key)
                if key == "c":
                    pieces = [(slice(64 * n, 64 * n + 64), cols(t["w_in"][L], C_C + 64 * h, 64))
                              for n, h in enumerate((0, 2, 1, 3))]
                    pieces.append((slice(256, 512), cols(t["w_in"][L], C_C + 256, 256)))
                else:
                    pieces = [(slice(0, w), cols(t["w_in"][L], c0, w))]
                item((key, L), pieces, ("proj_mm", since(L, "proj_mm") + last + 1))
            n_out = NT if L == 0 else 2
            for h in range(2):
                item(("out", L, h), [(slice(0, 512), cols(t["w_out"][L], 512 * h, 512))],
                     ("out_mm", since(L, "out_mm") + n_out * (h + 1)))
            if L == 0:
                for n, (f0, w) in enumerate(FT):
                    item(("w1", n), [(slice(0, w), cols(t["ffn_w1"][0], f0, w))], ("ffn_u_mm", 4 * n + w // P))
                    item(("w3", n), [(slice(0, w), cols(t["ffn_w3"][0], f0, w))], ("ffn_v_mm", 4 * n + w // P))
                for n in range(6):
                    item(("w2", n), [(None, n)], ("ffn_y_mm", n + 1))

        full = []
        count = [0, 0]
        for n, (pieces, _) in enumerate(plan):
            count[n % 2] += 16 * len(pieces)
            full.append(count[n % 2])

        def slot_full(eng, key):
            n = index[key]
            eng.wait_ge(S(f"ring_full{n % 2}"), full[n])
            return RING[n % 2]

        ENG = ("pe", "act", "dve", "pool")
        stage_count = {e: 0 for e in ENG}

        def stage_end(eng, me):
            eng.drain().then_inc(S(f"{me}_stage_done"), 1)
            stage_count[me] += 1
            for other in ENG:
                if other != me:
                    eng.wait_ge(S(f"{other}_stage_done"), stage_count[me])

        def rng(L):
            return (0, 1) if L < DEPTH - 1 else (1,)

        def tiles(L):
            return range(NT) if L < DEPTH - 1 else LAT_TILES

        block = ctx.enter_context(nc.Block())

        def pe_ada(pe, L):
            for j in range(13):
                if j < 12:
                    slot = slot_full(pe, ("ada", L, j))
                    if j == 0:
                        pe.wait_ge(S("adab_loaded"), since(L, "adab_loaded") + 16)
                    if j >= 2:
                        pe.wait_ge(S("ada_row"), since(L, "ada_row") + j - 1)
                    ps = B(j % 2)[0:2, :]
                    e12 = K[0:12, K_AT[K_E12] + 2 * j:K_AT[K_E12] + 2 * j + 2]
                    pe.matmul(ps, e12, ADAB[0:12, :], start=True, stop=False)
                    for k in range(KC):
                        mm = pe.matmul(ps, SC[:, k, :], slot[:, k, :], start=False, stop=k == KC - 1)
                    mm.then_inc(S("ada_mm"), 1)
                if j >= 1:
                    i = j - 1
                    pe.wait_ge(S("ada_row"), since(L, "ada_row") + i + 1)
                    if i >= 1:
                        pe.wait_ge(S("ada_cp"), since(L, "ada_cp") + i)
                    if i // 2 in (2, 5):
                        for r in range(2):
                            sel = K[0:2, K_AT[K_SELT] + P * r:K_AT[K_SELT] + P * r + P]
                            mm = pe.matmul(B(2 + r), sel, MROW[0:2, i % 2, :], start=True, stop=True)
                    else:
                        for c in range(4):
                            mm = pe.matmul(B(4)[:, 2 * c:2 * c + 2], MROW[0:2, i % 2, P * c:P * c + P],
                                           ident[0:2, 0:2], start=True, stop=True)
                    mm.then_inc(S("ada_spread"), 1)

        def act_ada(act, L):
            for j in range(12):
                act.wait_ge(S("ada_mm"), since(L, "ada_mm") + j + 1)
                if j >= 2:
                    act.wait_ge(S("ada_spread"), since(L, "ada_spread") + j - 1)
                act.activation(MROW[0:2, j % 2, :], B(j % 2)[0:2, :], ACT.Copy).then_inc(S("ada_row"), 1)

        def dve_ada(dve, L):
            for j in range(12):
                m, half = j // 2, j % 2
                dve.wait_ge(S("ada_spread"), since(L, "ada_spread") + j + 1)
                if m in (2, 5):
                    dve.tensor_copy(GATE[:, m // 3, :, 512 * half:512 * half + 512],
                                    PS[:, 2:4, :]).then_inc(S("ada_cp"), 1)
                else:
                    dve.tensor_copy(MT[:, m, 4 * half:4 * half + 4, :],
                                    B(4)[:, 0:8].rearrange("p (c r) -> p c r", r=2)).then_inc(S("ada_cp"), 1)
            dve.wait_ge(S("ada_cp"), since(L, "ada_cp") + 12)
            for m, g in ((1, GMIX), (4, GFFN)):
                dve.scalar_tensor_tensor(out=MT[:, m, :, :], in0=MT[:, m, :, :], scalar=1.0,
                                         in1=bc(g[:, L, :], 2, 2), op0=ALU.add, op1=ALU.mult)

        def norm_tiles(L, which):
            return list(range(NT)) if which == 0 else list(tiles(L))

        def act_norm(act, L, which):
            n, tt, v = "norm_", norm_tiles(L, which), 2 * L + which
            for x in tt:
                act.activation(A(0, D), X[:, x, :], ACT.Square,
                               accum_out=STAT[:, 0, x:x + 1]).then_inc(S(n + "ss"), 1)
                act.wait_ge(S(n + "ss"), 4 * v + tt.index(x) + 1)
            for k in range(1, KC, 2):
                act.wait_ge(S(n + "tp"), KC * v + k + 1)
                for r in sorted({x // 2 for x in tt}):
                    act.activation(HT[:, k, 256 * r:256 * r + 256], B(k % 4)[:, 256 * r:256 * r + 256], ACT.Identity,
                                   bias=MT[:, 3 * which, k, r:r + 1],
                                   scale=MT[:, 3 * which + 1, k, r:r + 1]).then_inc(S(n + "ht_act"), 1)

        def pool_norm(pool, L, which):
            n, tt, v = "norm_", norm_tiles(L, which), 2 * L + which
            a, b = tt[0], tt[-1] + 1
            pool.wait_ge(S(n + "ss"), 4 * v + len(tt))
            pool.tensor_scalar(STAT[:, 1, a:b], STAT[:, 0, a:b], 1.0 / D, EPS, ALU.mult, ALU.add).then_inc(S(n + "ms"), 1)
            pool.wait_ge(S(n + "ms"), v + 1)
            pool.tensor_tensor(STAT[:, 2, a:b], STAT[:, 1, a:b], NEGH[:, 0:b - a], ALU.pow).then_inc(S(n + "rstd"), 1)

        def dve_norm(dve, L, which):
            n, tt, v = "norm_", norm_tiles(L, which), 2 * L + which
            dve.wait_ge(S(n + "rstd"), v + 1)
            for x in tt:
                dve.tensor_scalar(XN[:, x, :], X[:, x, :], STAT[:, 2, x:x + 1], None, ALU.mult).then_inc(S(n + "xn"), 1)
            for k in range(0, KC, 2):
                dve.wait_ge(S(n + "tp"), KC * v + k + 1)
                for r in sorted({x // 2 for x in tt}):
                    dve.tensor_scalar(HT[:, k, 256 * r:256 * r + 256], B(k % 4)[:, 256 * r:256 * r + 256],
                                      MT[:, 3 * which + 1, k, r:r + 1], MT[:, 3 * which, k, r:r + 1],
                                      ALU.mult, ALU.add).then_inc(S(n + "ht_dve"), 1)

        def pe_norm(pe, L, which):
            n, tt, v = "norm_", norm_tiles(L, which), 2 * L + which
            nr = len({x // 2 for x in tt})
            pe.wait_ge(S(n + "xn"), 4 * v + len(tt))
            for k in range(KC):
                if k >= 4:
                    pe.wait_ge(S(n + ("ht_act" if k % 2 else "ht_dve")), 8 * v + nr * ((k - 4) // 2 + 1))
                for x in tt:
                    mm = pe.transpose(B(k % 4)[:, P * x:P * x + P], XN[:, x, P * k:P * k + P], ident)
                mm.then_inc(S(n + "tp"), 1)

        def proj_places(L):
            seen = {"act": 0, "dve": 0}
            for key, u, kind, c0, w, eng in proj_units(L):
                i = seen[eng]
                seen[eng] += 1
                yield key, u, kind, w, eng, (0 if eng == "act" else 4) + i % 4, i

        def pe_proj(pe, L):
            last = None
            for key, u, kind, w, eng, bank, i in proj_places(L):
                if key != last:
                    slot = slot_full(pe, (key, L))
                    last = key
                if i >= 4:
                    pe.wait_ge(S(f"proj_{eng}"), since(L, f"proj_{eng}") + i - 3)
                for k in range(KC):
                    if kind == "T":
                        mm = pe.matmul(B(bank), slot[:, k, P * u:P * u + P], HT[:, k, :], start=k == 0, stop=k == KC - 1)
                    else:
                        mm = pe.matmul(B(bank)[:, 0:w], HT[:, k, P * u:P * u + P], slot[:, k, 0:w],
                                       start=k == 0, stop=k == KC - 1)
                mm.then_inc(S("proj_mm"), 1)

        def act_proj(act, L):
            for n, (key, u, kind, w, eng, bank, i) in enumerate(proj_places(L)):
                if eng != "act":
                    continue
                act.wait_ge(S("proj_mm"), since(L, "proj_mm") + n + 1)
                if key == "bq":
                    act.activation(Q[:, u, :], B(bank), ACT.Silu).then_inc(S("proj_act"), 1)
                elif key == "bg":
                    act.activation(G[:, u, :], B(bank), ACT.Silu).then_inc(S("proj_act"), 1)
                else:
                    d = 0 if key == "bff" else 1
                    act.activation(FG[d][:, u, :], B(bank), ACT.Sigmoid)
                    act.activation(KE[d][:, u, :], B(bank), ACT.Sigmoid, scale=-1.0).then_inc(S("proj_act"), 1)

        def dve_proj(dve, L):
            dst = {"aqk": AQK, "c": CQKV, "bi": V, "av": AV}
            for n, (key, u, kind, w, eng, bank, i) in enumerate(proj_places(L)):
                if eng != "dve":
                    continue
                dve.wait_ge(S("proj_mm"), since(L, "proj_mm") + n + 1)
                dve.tensor_copy(dst[key][:, u, :], B(bank)[:, 0:w]).then_inc(S("proj_dve"), 1)

        def dve_qk(dve, L):
            n = "qk_"
            c3 = CQKV[:, :, 0:384]
            a3 = AQK.rearrange("p a (g d) -> p (a g) d", d=32)
            dve.tensor_tensor(TMP, AQK, AQK, ALU.mult).then_inc(S(n + "sq"), 1)
            dve.tensor_tensor(TMP2[:, :, 0:384], c3, c3, ALU.mult).then_inc(S(n + "sq"), 1)
            dve.wait_ge(S(n + "sq"), since(L, n + "sq") + 2)
            dve.tensor_reduce(STAT[:, 0, 0:64], TMP.rearrange("p a (g d) -> p (a g) d", d=32), AX.X, ALU.add).then_inc(S(n + "ss"), 1)
            dve.tensor_reduce(STAT[:, 0, 64:88].rearrange("p (a g) -> p a g", g=6),
                              TMP2[:, :, 0:384].rearrange("p a (g d) -> p a g d", d=64), AX.X, ALU.add).then_inc(S(n + "ss"), 1)
            dve.wait_ge(S(n + "rstd"), since(L, n + "rstd") + 2)
            dve.tensor_tensor(a3, a3, bc(STAT[:, 2, 0:64], 2, 32), ALU.mult).then_inc(S(n + "x"), 1)
            for x in range(NT):
                v = CQKV[:, x, 0:384].rearrange("p (g d) -> p g d", d=64)
                dve.tensor_tensor(v, v, bc(STAT[:, 2, 64 + 6 * x:70 + 6 * x], 2, 64), ALU.mult).then_inc(S(n + "x"), 1)
            dve.wait_ge(S(n + "x"), since(L, n + "x") + 1 + NT)
            for j in range(2):
                v = AQK[:, :, 256 * j:256 * j + 256].rearrange("p a (g d) -> p a g d", d=32)
                g = bc(bc(QKG[:, L, j, :], 1, 8), 1, NT)
                dve.tensor_tensor(v, v, g, ALU.mult).then_inc(S(n + "gained"), 1)
            for j, (a, b) in enumerate(((0, 256), (256, 384))):
                v = CQKV[:, :, a:b].rearrange("p a (g d) -> p a g d", d=64)
                g = bc(bc(SQKG[:, L, j, :], 1, (b - a) // 64), 1, NT)
                dve.tensor_tensor(v, v, g, ALU.mult).then_inc(S(n + "gained"), 1)

        def pool_qk(pool, L):
            n = "qk_"
            pool.wait_ge(S(n + "ss"), since(L, n + "ss") + 2)
            pool.tensor_scalar(STAT[:, 1, 0:64], STAT[:, 0, 0:64], 1.0 / 32, EPS, ALU.mult, ALU.add).then_inc(S(n + "ms"), 1)
            pool.tensor_scalar(STAT[:, 1, 64:88], STAT[:, 0, 64:88], 1.0 / 64, EPS, ALU.mult, ALU.add).then_inc(S(n + "ms"), 1)
            pool.wait_ge(S(n + "ms"), since(L, n + "ms") + 2)
            pool.tensor_tensor(STAT[:, 2, 0:64], STAT[:, 1, 0:64], NEGH[:, :], ALU.pow).then_inc(S(n + "rstd"), 1)
            pool.tensor_tensor(STAT[:, 2, 64:88], STAT[:, 1, 64:88], NEGH[:, 0:24], ALU.pow).then_inc(S(n + "rstd"), 1)
            pool.wait_ge(S(n + "gained"), since(L, n + "gained") + 4)
            for x in LAT_TILES:
                for src, dim, g, kcos, ksin in ((AQK[:, x, :], 32, 16, K_C32, K_S32),
                                                (CQKV[:, x, 0:384], 64, 6, K_C64, K_S64)):
                    c = kc(kcos)[:, dim * (x - 2):dim * (x - 1)]
                    s = kc(ksin)[:, dim * (x - 2):dim * (x - 1)]
                    nf = dim // 4
                    w = g * dim
                    v = src.rearrange("p (g d) -> p g d", d=dim)
                    turned = TMP2[:, x, 0:w].rearrange("p (g h b f) -> p g h b f", h=2, b=2, f=nf)
                    halves = src.rearrange("p (g h b f) -> p g h b f", h=2, b=2, f=nf)
                    sh = s.rearrange("p (h b f) -> p h b f", h=2, b=2)
                    for b in range(2):
                        pool.tensor_tensor(turned[:, :, :, b, :], halves[:, :, :, 1 - b, :],
                                           bc(sh[:, :, b, :], 1, g), ALU.mult).then_inc(S(n + "turned"), 1)
                    pool.tensor_tensor(TMP[:, x, 0:w].rearrange("p (g d) -> p g d", d=dim), v, bc(c, 1, g),
                                       ALU.mult).then_inc(S(n + "turned"), 1)
                    k = 3 * (2 * (x - 2) + (0 if dim == 32 else 1) + 1)
                    pool.wait_ge(S(n + "turned"), since(L, n + "turned") + k)
                    pool.tensor_tensor(src, TMP[:, x, 0:w], TMP2[:, x, 0:w], ALU.add).then_inc(S(n + "rotated"), 1)
                    pool.wait_ge(S(n + "rotated"), since(L, n + "rotated") + k // 3)

        def hgrn_gates(eng, L, d):
            n = f"h{d}_"
            if L > 0:
                for h in range(NH):
                    eng.tensor_scalar(FG[d][:, h, :], FG[d][:, h, :], LBT[:, 5, d, h:h + 1], LBT[:, 4, d, h:h + 1],
                                      ALU.mult, ALU.add).then_inc(S(n + "f"), 1)
                    eng.tensor_scalar(KE[d][:, h, :], KE[d][:, h, :], LBT[:, 5, d, h:h + 1], None,
                                      ALU.mult).then_inc(S(n + "f"), 1)
                eng.wait_ge(S(n + "f"), since(L, n + "f") + 2 * NH)
            eng.tensor_tensor(QP[d], Q, FG[d], ALU.mult).then_inc(S(n + "qp"), 1)
            eng.wait_ge(S(n + "qp"), since(L, n + "qp") + 1)

        def hgrn_double(eng, L, d, n_level):
            n = f"h{d}_"
            m = LEVELS[n_level]
            nb = NH * 512 // m
            tot = FG[d].rearrange("p a b -> p (a b)") if n_level == 0 else (
                TB[d][:, 0:nb] if n_level % 2 else FG[d].rearrange("p a b -> p (a b)")[:, 0:nb])
            new = TB[d][:, 0:nb // 2] if n_level % 2 == 0 else FG[d].rearrange("p a b -> p (a b)")[:, 0:nb // 2]
            tv = tot.rearrange("p (b h) -> p b h", h=2)
            early, late = (0, 1) if d == 0 else (1, 0)
            qv = QP[d].rearrange("p a b -> p (a b)").rearrange("p (b h m) -> p b h m", h=2, m=m)
            kv = KE[d].rearrange("p a b -> p (a b)").rearrange("p (b h m) -> p b h m", h=2, m=m)
            eng.wait_ge(S(n + "mm"), since(L, n + "mm") + n_level + 2)
            eng.tensor_tensor(qv[:, :, late, :], qv[:, :, late, :], bc(tv[:, :, early], 2, m), ALU.mult).then_inc(S(n + "upd"), 1)
            eng.tensor_tensor(kv[:, :, early, :], kv[:, :, early, :], bc(tv[:, :, late], 2, m), ALU.mult).then_inc(S(n + "upd"), 1)
            eng.tensor_tensor(new, tv[:, :, 0], tv[:, :, 1], ALU.mult).then_inc(S(n + "upd"), 1)
            eng.wait_ge(S(n + "upd"), since(L, n + "upd") + 3 * (n_level + 1))

        def pe_levels(pe, L):
            ts = list(tiles(L))
            for n_level in range(-1, len(LEVELS)):
                for d in range(2):
                    n = f"h{d}_"
                    pe.wait_ge(S(n + "qp"), since(L, n + "qp") + 1)
                    if n_level >= 1:
                        pe.wait_ge(S(n + "upd"), since(L, n + "upd") + 3 * n_level)
                    if n_level >= 0:
                        pe.wait_ge(S(n + "taken"), since(L, n + "taken") + n_level + 1)
                    for h in range(NH):
                        for x in ts:
                            c = slice(P * x, P * x + P)
                            q = Q if n_level < 0 else QP[d]
                            mm = pe.matmul(B(4 * d + h)[:, c], KE[d][:, h, c], q[:, h, c], start=True, stop=True)
                    mm.then_inc(S(n + "mm"), 1)

        def dve_take(dve, L, d, n_level):
            n = f"h{d}_"
            ts = list(tiles(L))
            a, nt = P * ts[0], len(ts)
            dve.wait_ge(S(n + "mm"), since(L, n + "mm") + n_level + 2)
            if n_level < 0:
                for h in range(NH):
                    src = B(4 * d + h)[:, a:].rearrange("p (x t) -> p x t", t=P)
                    dst = ST[d][:, h, a:].rearrange("p (x t) -> p x t", t=P)
                    ins = dve.tensor_tensor(dst, src, bc(ident, 1, nt), ALU.mult)
            else:
                for h in range(NH):
                    src = B(4 * d + h)[:, a:].rearrange("p (x t) -> p x t", t=P)
                    dst = ST[d][:, h, a:].rearrange("p (x t) -> p x t", t=P)
                    dve.wait_ge(S(n + "taken"), since(L, n + "taken") + n_level + 1)
                    ins = dve.copy_predicated(dst, bc(M8[:, d, n_level, :], 1, nt), src)
            ins.then_inc(S(n + "taken"), 1)

        def dve_levels(dve, L):
            hgrn_gates(dve, L, 0)
            dve_take(dve, L, 0, -1)
            dve_take(dve, L, 1, -1)
            for n_level in range(len(LEVELS)):
                dve_take(dve, L, 0, n_level)
                hgrn_double(dve, L, 0, n_level)
                dve_take(dve, L, 1, n_level)

        def pool_levels(pool, L):
            hgrn_gates(pool, L, 1)
            for n_level in range(len(LEVELS)):
                hgrn_double(pool, L, 1, n_level)

        ORDER = [(0, 1, 2, 3), (1, 0, 3, 2)]

        def pe_states(pe, L):
            n = "s_"
            for i in range(3):
                b0 = 4 * (i % 2)
                for d in range(2):
                    x = ORDER[d][i]
                    for h in range(NH):
                        mm = pe.transpose(B(b0 + d)[:, P * h:P * h + P], KE[d][:, h, P * x:P * x + P], ident)
                    mm.then_inc(S(n + "kt"), 1)
                for d in range(2):
                    x = ORDER[d][i]
                    pe.wait_ge(S(n + "kd"), since(L, n + "kd") + 2 * i + d + 1)
                    if i >= 2:
                        pe.wait_ge(S(n + "st"), since(L, n + "st") + 2 * NH * (i - 1))
                    for h in range(NH):
                        mm = pe.matmul(B(b0 + 2 + d)[:, P * h:P * h + P], KDT[:, d, h, :], V[:, x, P * h:P * h + P],
                                       start=True, stop=True)
                    mm.then_inc(S(n + "kv"), 1)
            pe.wait_ge(S(n + "st"), since(L, n + "st") + 6 * NH)
            for j, x in enumerate(tiles(L)):
                c = slice(P * x, P * x + P)
                for h in range(NH):
                    o = B(j)[:, P * h:P * h + P]
                    v = V[:, x, P * h:P * h + P]
                    pairs = [(ST[0][:, h, c], v), (ST[1][:, h, c], v)]
                    for d in range(2):
                        i = ORDER[d].index(x)
                        if i:
                            pairs.append((QP[d][:, h, c], SST[:, i - 1, d, h, :]))
                    for k, (a, b) in enumerate(pairs):
                        mm = pe.matmul(o, a, b, start=k == 0, stop=k == len(pairs) - 1)
                mm.then_inc(S(n + "o"), 1)

        def act_states(act, L):
            n = "s_"
            for i in range(3):
                for d in range(2):
                    act.wait_ge(S(n + "kt"), since(L, n + "kt") + 2 * i + d + 1)
                    if i:
                        act.wait_ge(S(n + "kv"), since(L, n + "kv") + 2 * (i - 1) + d + 1)
                    act.activation(KDT[:, d, :, :], B(4 * (i % 2) + d).rearrange("p (h k) -> p h k", k=P),
                                   ACT.Copy).then_inc(S(n + "kd"), 1)

        def dve_states(dve, L):
            n = "s_"
            for i in range(3):
                for d in range(2):
                    x = ORDER[d][i]
                    dve.wait_ge(S(n + "kv"), since(L, n + "kv") + 2 * i + d + 1)
                    if i:
                        dve.wait_ge(S(n + "st"), since(L, n + "st") + 2 * NH * i)
                    for h in range(NH):
                        ps = B(4 * (i % 2) + 2 + d)[:, P * h:P * h + P]
                        if i == 0:
                            dve.tensor_copy(SST[:, 0, d, h, :], ps).then_inc(S(n + "st"), 1)
                        else:
                            total = TB[d][:, NT * h + x:NT * h + x + 1]
                            dve.scalar_tensor_tensor(out=SST[:, i, d, h, :], in0=SST[:, i - 1, d, h, :], scalar=total,
                                                     in1=ps, op0=ALU.mult, op1=ALU.add).then_inc(S(n + "st"), 1)
            for j, x in enumerate(tiles(L)):
                dve.wait_ge(S(n + "o"), since(L, n + "o") + j + 1)
                dve.tensor_copy(MIX[:, x, 256:768], B(j)).then_inc(S(n + "mix"), 1)

        def out_rows(L):
            ts = list(tiles(L))
            return slice(ts[0], ts[-1] + 1), len(ts)

        def dve_post(dve, L, name, c0, dim, gain, extra):
            n, v = "post_", 2 * L + (name == "dp")
            rows, nt = out_rows(L)
            hs = 512 // dim if name == "hp" else 256 // dim
            w = hs * dim
            o = MIX[:, rows, c0:c0 + w]
            sq = OT[:, rows, 0:w]
            dve.tensor_tensor(sq, o, o, ALU.mult).then_inc(S(n + "sq"), 1)
            dve.wait_ge(S(n + "sq"), v + 1)
            st = STAT[:, 0, 0:nt * hs]
            dve.tensor_reduce(st.rearrange("p (a g) -> p a g", g=hs), sq.rearrange("p a (g d) -> p a g d", d=dim),
                              AX.X, ALU.add).then_inc(S(n + "ss"), 1)
            dve.wait_ge(S(n + "rstd"), v + 1)
            for j, x in enumerate(tiles(L)):
                mv = MIX[:, x, c0:c0 + w].rearrange("p (g d) -> p g d", d=dim)
                dve.tensor_tensor(mv, mv, bc(STAT[:, 2, hs * j:hs * j + hs], 2, dim), ALU.mult).then_inc(S(n + "x"), 1)
            dve.wait_ge(S(n + "x"), (0, 4, 8, 10)[v] + nt)
            ov = o.rearrange("p a (g d) -> p a g d", d=dim)
            dve.tensor_tensor(ov, ov, bc(bc(gain, 1, hs), 1, nt), ALU.mult).then_inc(S(n + "g"), 1)
            dve.wait_ge(S(n + "g"), v + 1)
            if name == "hp":
                dve.tensor_tensor(o, o, G[:, rows, :], ALU.mult)
            else:
                dve.tensor_scalar(o, o, extra, None, ALU.mult)

        def pool_post(pool, L, name, dim):
            n, v = "post_", 2 * L + (name == "dp")
            nt = out_rows(L)[1]
            w = nt * ((512 if name == "hp" else 256) // dim)
            pool.wait_ge(S(n + "ss"), v + 1)
            pool.tensor_scalar(STAT[:, 1, 0:w], STAT[:, 0, 0:w], 1.0 / dim, EPS, ALU.mult, ALU.add).then_inc(S(n + "ms"), 1)
            pool.wait_ge(S(n + "ms"), v + 1)
            pool.tensor_tensor(STAT[:, 2, 0:w], STAT[:, 1, 0:w], NEGH[:, 0:w], ALU.pow).then_inc(S(n + "rstd"), 1)

        def units(L):
            return [(kind, h, x) for x in tiles(L) for h in range(NH) for kind in "DW"]

        def keys(x):
            return 256 if x in CTX_TILES else 512

        def masked(L, u):
            return sum(k == "W" and x in LAT_TILES for k, _, x in units(L)[:u])

        def pe_qkt(pe, L):
            n = "t_"
            for b in range(7):
                for x in range(NT):
                    src = AQK[:, x, P * b:P * b + P] if b < 4 else CQKV[:, x, P * (b - 4):P * (b - 3)]
                    mm = pe.transpose(B(b)[:, P * x:P * x + P], src, ident)
                mm.then_inc(S(n + "tp"), 1)

        def act_qkt(act, L):
            for b in range(0, 7, 2):
                act.wait_ge(S("t_tp"), since(L, "t_tp") + b + 1)
                act.activation(QKT[:, b, :] if b < 4 else CT[:, b - 4, :], B(b), ACT.Copy)

        def dve_qkt(dve, L):
            for b in range(1, 7, 2):
                dve.wait_ge(S("t_tp"), since(L, "t_tp") + b + 1)
                dve.tensor_copy(QKT[:, b, :] if b < 4 else CT[:, b - 4, :], B(b))

        def pe_att(pe, L):
            n, us = "a_", units(L)
            for s in range(len(us) + 2):
                if s < len(us):
                    kind, h, x = us[s]
                    if s >= 2:
                        pe.wait_ge(S(n + "exp"), since(L, n + "exp") + s - 1)
                    c, nk = slice(P * x, P * x + P), keys(x)
                    if kind == "D":
                        for m in range(2):
                            g = 2 * h + m
                            r = slice(32 * (g % 4), 32 * (g % 4) + 32)
                            mm = pe.matmul(B(2 * (s % 2) + m)[:, 0:nk], QKT[r, g // 4, c], QKT[r, 2 + g // 4, 0:nk],
                                           start=True, stop=True)
                    else:
                        r = slice(64 * (h // 2), 64 * (h // 2) + 64)
                        mm = pe.matmul(B(2 * (s % 2))[:, 0:nk], CT[r, h % 2, c], CT[r, 2, 0:nk], start=True, stop=True)
                    mm.then_inc(S(n + "s"), 1)
                if 1 <= s <= len(us):
                    u = s - 1
                    pe.wait_ge(S(n + "p"), since(L, n + "p") + u + 1)
                    if u >= 2:
                        pe.wait_ge(S(n + "at"), since(L, n + "at") + u - 1)
                    for k in range(keys(us[u][2]) // P):
                        mm = pe.transpose(B(4 + u % 2)[:, P * k:P * k + P], EX[:, u % 2, 0, P * k:P * k + P], ident)
                    mm.then_inc(S(n + "pt"), 1)
                if s >= 2:
                    u = s - 2
                    kind, h, x = us[u]
                    pe.wait_ge(S(n + "at"), since(L, n + "at") + u + 1)
                    if u >= 2:
                        pe.wait_ge(S(n + "o"), since(L, n + "o") + u - 1)
                    nk = keys(x) // P
                    for k in range(nk):
                        v = AV[:, k, 64 * h:64 * h + 64] if kind == "D" else CQKV[:, k, 384 + 64 * (h // 2):448 + 64 * (h // 2)]
                        mm = pe.matmul(B(6 + u % 2)[:, 0:64], AT[:, u % 2, P * k:P * k + P], v, start=k == 0, stop=k == nk - 1)
                    mm.then_inc(S(n + "pv"), 1)

        def act_att(act, L):
            n, us = "a_", units(L)
            for s in range(len(us) + 1):
                if s < len(us):
                    kind, h, x = us[s]
                    nk = keys(x)
                    act.wait_ge(S(n + "nb"), since(L, n + "nb") + s + 1)
                    if s >= 2:
                        act.wait_ge(S(n + "pt"), since(L, n + "pt") + s - 1)
                    if kind == "D":
                        for m in range(2):
                            ins = act.activation(EX[:, s % 2, m, 0:nk], B(2 * (s % 2) + m)[:, 0:nk], ACT.Exp,
                                                 bias=AST[:, 1, s, m:m + 1], scale=32 ** -0.5,
                                                 accum_out=AST[:, 2, s, m:m + 1])
                    else:
                        src = MSK[:, masked(L, s) % 2, :] if x in LAT_TILES else B(2 * (s % 2))[:, 0:nk]
                        act.activation(AST[:, 3, s, 0:1], SINK[:, L, h:h + 1], ACT.Exp, bias=AST[:, 1, s, 0:1])
                        ins = act.activation(EX[:, s % 2, 0, 0:nk], src, ACT.Exp, bias=AST[:, 1, s, 0:1],
                                             scale=64 ** -0.5, accum_out=AST[:, 2, s, 0:1])
                    ins.then_inc(S(n + "exp"), 1)
                if s >= 1:
                    u = s - 1
                    nk = keys(us[u][2])
                    act.wait_ge(S(n + "pt"), since(L, n + "pt") + u + 1)
                    if u >= 2:
                        act.wait_ge(S(n + "pv"), since(L, n + "pv") + u - 1)
                    act.activation(AT[:, u % 2, 0:nk], B(4 + u % 2)[:, 0:nk], ACT.Copy).then_inc(S(n + "at"), 1)

        def dve_att(dve, L):
            n, us = "a_", units(L)
            for s in range(len(us) + 3):
                if s < len(us):
                    kind, h, x = us[s]
                    nk = keys(x)
                    dve.wait_ge(S(n + "s"), since(L, n + "s") + s + 1)
                    if kind == "D":
                        dve.tensor_reduce(AST[:, 0, s, :], PS[:, 2 * (s % 2):2 * (s % 2) + 2, 0:nk], AX.X,
                                          ALU.max).then_inc(S(n + "mx"), 1)
                        dve.wait_ge(S(n + "mx"), since(L, n + "mx") + s + 1)
                        dve.tensor_scalar(AST[:, 1, s, :], AST[:, 0, s, :], -(32 ** -0.5), None,
                                          ALU.mult).then_inc(S(n + "nb"), 1)
                    else:
                        src = B(2 * (s % 2))[:, 0:nk]
                        if x in LAT_TILES:
                            w = masked(L, s)
                            if w >= 2:
                                before = [i for i, (k, _, y) in enumerate(us) if k == "W" and y in LAT_TILES][w - 2]
                                dve.wait_ge(S(n + "exp"), since(L, n + "exp") + before + 1)
                            dst = MSK[:, w % 2, :]
                            o = 384 if x == 2 else 256
                            dve.tensor_tensor(dst[:, o:o + P], src[:, o:o + P], kc(K_SWA)[:, P * (x - 2):P * (x - 1)],
                                              ALU.add).then_inc(S(n + "msk"), 1)
                            if x == 2:
                                dve.tensor_copy(dst[:, 0:384], src[:, 0:384]).then_inc(S(n + "msk"), 1)
                            else:
                                dve.tensor_copy(dst[:, 0:256], src[:, 0:256])
                                dve.tensor_copy(dst[:, 384:512], src[:, 384:512]).then_inc(S(n + "msk"), 1)
                            dve.wait_ge(S(n + "msk"), since(L, n + "msk") + 2 * (w + 1))
                            src = dst
                        dve.tensor_reduce(AST[:, 0, s, 0:1], src, AX.X, ALU.max).then_inc(S(n + "mx"), 1)
                        dve.wait_ge(S(n + "mx"), since(L, n + "mx") + s + 1)
                        dve.tensor_scalar(AST[:, 1, s, 0:1], AST[:, 0, s, 0:1], -(64 ** -0.5), NSINK[:, L, h:h + 1],
                                          ALU.mult, ALU.min).then_inc(S(n + "nb"), 1)
                if 1 <= s <= len(us):
                    u = s - 1
                    kind, h, x = us[u]
                    nk = keys(x)
                    dve.wait_ge(S(n + "exp"), since(L, n + "exp") + u + 1)
                    if kind == "D":
                        dve.reciprocal(AST[:, 4, u, :], AST[:, 2, u, :]).then_inc(S(n + "r"), 1)
                        dve.wait_ge(S(n + "r"), since(L, n + "r") + u + 1)
                        dve.tensor_scalar(AST[:, 5, u, 0:1], AST[:, 4, u, 1:2], AST[:, 2, u, 0:1], LAM[:, L, 5:6],
                                          ALU.mult, ALU.mult).then_inc(S(n + "ratio"), 1)
                        dve.wait_ge(S(n + "ratio"), since(L, n + "ratio") + u + 1)
                        e = EX[:, u % 2, 0, 0:nk]
                        dve.scalar_tensor_tensor(out=e, in0=EX[:, u % 2, 1, 0:nk], scalar=AST[:, 5, u, 0:1], in1=e,
                                                 op0=ALU.mult, op1=ALU.add).then_inc(S(n + "p"), 1)
                    else:
                        dve.tensor_tensor(AST[:, 5, u, 0:1], AST[:, 2, u, 0:1], AST[:, 3, u, 0:1], ALU.add).then_inc(S(n + "ratio"), 1)
                        dve.wait_ge(S(n + "ratio"), since(L, n + "ratio") + u + 1)
                        dve.reciprocal(AST[:, 4, u, 0:1], AST[:, 5, u, 0:1]).then_inc(S(n + "r"), 1)
                        dve.wait_ge(S(n + "r"), since(L, n + "r") + u + 1)
                        dve.tensor_copy(AST[:, 3, u, 1:2], AST[:, 4, u, 0:1]).then_inc(S(n + "p"), 1)
                if s >= 3:
                    u = s - 3
                    kind, h, x = us[u]
                    dve.wait_ge(S(n + "pv"), since(L, n + "pv") + u + 1)
                    c = (0 if kind == "D" else 768) + 64 * h
                    dve.tensor_scalar(MIX[:, x, c:c + 64], B(6 + u % 2)[:, 0:64], AST[:, 4, u, 0:1], None,
                                      ALU.mult).then_inc(S(n + "o"), 1)

        def pe_out(pe, L):
            n, ts = "o_", list(tiles(L))
            for k in range(KC):
                if k >= 4:
                    pe.wait_ge(S(n + ("mt_act" if k % 2 else "mt_dve")), since(L, n + ("mt_act" if k % 2 else "mt_dve")) + (k - 4) // 2 + 1)
                for x in ts:
                    mm = pe.transpose(B(k % 4)[:, P * x:P * x + P], MIX[:, x, P * k:P * k + P], ident)
                mm.then_inc(S(n + "tp"), 1)
            pe.wait_ge(S(n + "mt_act"), since(L, n + "mt_act") + 4)
            pe.wait_ge(S(n + "mt_dve"), since(L, n + "mt_dve") + 4)
            for h in range(2):
                slot = slot_full(pe, ("out", L, h))
                for j, x in enumerate(ts):
                    i = len(ts) * h + j
                    for k in range(KC):
                        mm = pe.matmul(B(i), HT[:, k, P * x:P * x + P], slot[:, k, :], start=k == 0, stop=k == KC - 1)
                    mm.then_inc(S("out_mm"), 1)

        def act_out(act, L):
            n, ts = "o_", list(tiles(L))
            for k in range(1, KC, 2):
                act.wait_ge(S(n + "tp"), since(L, n + "tp") + k + 1)
                act.activation(HT[:, k, P * ts[0]:], B(k % 4)[:, P * ts[0]:], ACT.Copy).then_inc(S(n + "mt_act"), 1)

        def dve_out(dve, L):
            n, ts = "o_", list(tiles(L))
            for k in range(0, KC, 2):
                dve.wait_ge(S(n + "tp"), since(L, n + "tp") + k + 1)
                dve.tensor_copy(HT[:, k, P * ts[0]:], B(k % 4)[:, P * ts[0]:]).then_inc(S(n + "mt_dve"), 1)
            for h in range(2):
                for j, x in enumerate(ts):
                    i = len(ts) * h + j
                    dve.wait_ge(S("out_mm"), since(L, "out_mm") + i + 1)
                    if i >= 2:
                        dve.wait_ge(S(n + "added"), since(L, n + "added") + i - 1)
                    c = slice(512 * h, 512 * h + 512)
                    dve.tensor_tensor(YT[:, i % 2, :], B(i), GATE[:, 0, x // 2, c], ALU.mult).then_inc(S(n + "gated"), 1)
                    dve.wait_ge(S(n + "gated"), since(L, n + "gated") + i + 1)
                    dve.tensor_tensor(X[:, x, c], X[:, x, c], YT[:, i % 2, :], ALU.add).then_inc(S(n + "added"), 1)

        def pe_ffn(pe):
            for n, (f0, w) in enumerate(FT):
                for key, b0, sem, ev in (("w1", 0, "ffn_u_mm", "ffn_u"), ("w3", 4, "ffn_v_mm", "ffn_act")):
                    slot = slot_full(pe, (key, n))
                    for c in range(w // P):
                        if n:
                            pe.wait_ge(S(ev), 4 * (n - 1) + c + 1)
                        for k in range(KC):
                            mm = pe.matmul(B(b0 + c), slot[:, k, P * c:P * c + P], HT[:, k, :], start=k == 0, stop=k == KC - 1)
                        mm.then_inc(S(sem), 1)
            pe.wait_ge(S("ffn_act"), FC)
            for n in range(6):
                slot = slot_full(pe, ("w2", n)).rearrange("p k n -> p (k n)")
                for c in range(4 * n, min(4 * n + 4, FC)):
                    for x in range(NT):
                        for h in range(2):
                            a = D * (c - 4 * n) + 512 * h
                            mm = pe.matmul(B(2 * x + h), ACTT[:, c, P * x:P * x + P], slot[:, a:a + 512],
                                           start=c == 0, stop=c == FC - 1)
                mm.then_inc(S("ffn_y_mm"), 1)

        def act_ffn(act):
            for c in range(FC):
                act.wait_ge(S("ffn_u_mm"), c + 1)
                act.activation(ACTT[:, c, :], B(c % 4), ACT.Silu).then_inc(S("ffn_u"), 1)

        def dve_ffn(dve):
            for c in range(FC):
                dve.wait_ge(S("ffn_u"), c + 1)
                dve.wait_ge(S("ffn_v_mm"), c + 1)
                dve.tensor_tensor(ACTT[:, c, :], B(4 + c % 4), ACTT[:, c, :], ALU.mult).then_inc(S("ffn_act"), 1)
            dve.wait_ge(S("ffn_y_mm"), 6)
            for i in range(8):
                x, h = i // 2, i % 2
                dve.tensor_tensor(FTMP[:, i, :], B(i), GATE[:, 1, x // 2, 512 * h:512 * h + 512],
                                  ALU.mult).then_inc(S("ffn_gated"), 1)
            for i in range(8):
                x, c = i // 2, slice(512 * (i % 2), 512 * (i % 2) + 512)
                dve.wait_ge(S("ffn_gated"), i + 1)
                dve.tensor_tensor(X[:, x, c], X[:, x, c], FTMP[:, i, :], ALU.add)

        WA = [A(11 * s, D_FF) for s in range(8)]
        WB = [A(88 + 4 * s, D) for s in range(11)]
        UA = A(132, D_FF)
        AE = A(143, FC, P)
        HE = A(154, KC, P)
        YE = HE.rearrange("p a b -> p (a b)")
        PG = A(158, 2, P)
        PT = A(159, 2, P)
        PH = A(160, 2, P)
        XL = GATE[:, 0, :, :]
        Y = X[:, 0:2, :]
        RT = A(16, 9, 2, N_EXP)
        RV = A(17, 8, 2)
        POS = sb("POS", [P, 2, 2, N_EXP])
        GT = sb("GT", [P, 2, 2, N_EXP])
        CNT = sb("CNT", [P, 4])
        NROUND = sb("NROUND", [P, 1], I32)

        def pe_route(pe):
            for x in range(2):
                for k in range(KC):
                    mm = pe.matmul(B(0)[:, 8 * x:8 * x + 8], HT[:, k, 256 + P * x:384 + P * x], ROUT[:, k, :],
                                   start=k == 0, stop=k == KC - 1)
            mm.then_inc(S("r_logits"), 1)
            pe.wait_ge(S("r_sel"), 1)
            one, tri = kc(K_ONE), kc(K_TRI)
            pe.matmul(B(1)[:, 0:8], tri, RT[:, 8, 0, :], start=True, stop=True)
            pe.matmul(B(1)[:, 8:16], one, RT[:, 8, 0, :], start=True, stop=False)
            pe.matmul(B(1)[:, 8:16], tri, RT[:, 8, 1, :], start=False, stop=True)
            pe.matmul(B(1)[:, 16:24], one, RT[:, 8, 0, :], start=True, stop=False)
            pe.matmul(B(1)[:, 16:24], one, RT[:, 8, 1, :], start=False, stop=True).then_inc(S("r_pos"), 1)

        def dve_route(dve):
            step = [0]

            def then(ins):
                step[0] += 1
                ins.then_inc(S("r_step"), 1)
                dve.wait_ge(S("r_step"), step[0])

            dve.wait_ge(S("r_logits"), 1)
            lg, rev = RT[:, 0, :, :], kc(K_REV).rearrange("p (x e) -> p x e", e=8)
            then(dve.tensor_copy(lg, B(0)[:, 0:16].rearrange("p (x e) -> p x e", e=8)))
            for r in range(2):
                then(dve.tensor_reduce(RV[:, r, :], lg, AX.X, ALU.max))
                then(dve.tensor_tensor(RT[:, 1, :, :], lg, bc(RV[:, r, :], 2, 8), ALU.is_equal))
                then(dve.tensor_tensor(RT[:, 2, :, :], RT[:, 1, :, :], rev, ALU.mult))
                then(dve.tensor_reduce(RV[:, 2 + r, :], RT[:, 2, :, :], AX.X, ALU.max))
                then(dve.tensor_tensor(RT[:, 3 + r, :, :], RT[:, 2, :, :], bc(RV[:, 2 + r, :], 2, 8), ALU.is_equal))
                if r == 0:
                    then(dve.scalar_tensor_tensor(out=lg, in0=RT[:, 3, :, :], scalar=-3.0e38, in1=lg,
                                                  op0=ALU.mult, op1=ALU.add))
            then(dve.tensor_tensor(RV[:, 4, :], RV[:, 1, :], RV[:, 0, :], ALU.subtract))
            dve.tensor_tensor(RT[:, 8, :, :], RT[:, 3, :, :], RT[:, 4, :, :], ALU.add).then_inc(S("r_sel"), 1)
            dve.wait_ge(S("r_exp"), 1)
            then(dve.tensor_scalar(RV[:, 6, :], RV[:, 5, :], 1.0, None, ALU.add))
            then(dve.reciprocal(RV[:, 6, :], RV[:, 6, :]))
            then(dve.tensor_tensor(RV[:, 7, :], RV[:, 5, :], RV[:, 6, :], ALU.mult))
            then(dve.tensor_tensor(RT[:, 5, :, :], RT[:, 3, :, :], bc(RV[:, 6, :], 2, 8), ALU.mult))
            then(dve.tensor_tensor(RT[:, 6, :, :], RT[:, 4, :, :], bc(RV[:, 7, :], 2, 8), ALU.mult))
            for c in range(2):
                then(dve.tensor_tensor(GT[:, c, :, :], RT[:, 5, :, :], RT[:, 6, :, :], ALU.add))
            dve.wait_ge(S("r_pos"), 1)
            pos = B(1)[:, 0:16].rearrange("p (x e) -> p x e", e=8)
            then(dve.scalar_tensor_tensor(out=RT[:, 7, :, :], in0=pos, scalar=1.0, in1=RT[:, 8, :, :],
                                          op0=ALU.add, op1=ALU.mult))
            for c in range(2):
                then(dve.tensor_scalar(POS[:, c, :, :], RT[:, 7, :, :], -1.0 - P * c, None, ALU.add))
            then(dve.tensor_reduce(CNT[:, 0:1], B(1)[:, 16:24], AX.X, ALU.max))
            then(dve.tensor_scalar(CNT[:, 1:2], CNT[:, 0:1], float(P), None, ALU.is_gt))
            then(dve.tensor_scalar(CNT[:, 2:3], CNT[:, 1:2], 1.0, None, ALU.add))
            then(dve.tensor_copy(NROUND[:, :], CNT[:, 2:3]))
            then(dve.tensor_copy(XL, XN[:, 2:4, :]))
            dve.memset(Y, 0.0)

        def act_route(act):
            act.wait_ge(S("r_sel"), 1)
            act.activation(RV[:, 5, :], RV[:, 4, :], ACT.Exp).then_inc(S("r_exp"), 1)

        VB = [6, 7, 0, 1, 2, 3]
        TBK = [4, 5, 6, 7, 0, 1]
        SB = [5, 6, 7, 0]

        def rounds(eng, body):
            n = eng.value_load(NROUND[0:1, 0:1], min_val=1, max_val=2)
            with eng.Fori(0, n) as c:
                with eng.Fori(0, N_EXP) as e:
                    body(c * N_EXP + e, e, c)

        def sp_moe(sp):
            for other in ENG:
                sp.wait_ge(S(f"{other}_stage_done"), MOE_STAGE)

            def body(i, e, c):
                for w, off in ((t["moe_w1"], 0), (t["moe_w3"], 8)):
                    for k in range(KC):
                        sp.wait_ge(S("m_wa_used"), 16 * i + off + k + 1)
                        sp.dma_start(WA[k], w[0, bass.ds(e, 1), P * k:P * k + P, :].rearrange("a p n -> p (a n)")
                                     ).then_inc(S(f"m_wa{k}"), 16)
                for f in range(FC):
                    sp.wait_ge(S("m_wb_used"), FC * i + f + 1)
                    sp.dma_start(WB[f % 11], t["moe_w2"][0, bass.ds(e, 1), P * f:P * f + P, :].rearrange("a p n -> p (a n)")
                                 ).then_inc(S(f"m_wb{f % 11}"), 16)
            rounds(sp, body)

        def pe_moe(pe):
            pe.sem_inc(S("m_wa_used"), 8)
            pe.sem_inc(S("m_wb_used"), 11)
            pe.sem_inc(S("m_scattered"), 1)

            def body(i, e, c):
                pe.wait_ge(S("m_onehot"), i * 2 + 2)
                for k in range(KC):
                    for x in range(2):
                        mm = pe.matmul(B(6 + k // 4)[:, P * (k % 4):P * (k % 4) + P], XL[:, x, P * k:P * k + P],
                                       PH[:, x, :], start=x == 0, stop=x == 1)
                    if k % 4 == 3:
                        mm.then_inc(S("m_gathered"), 1)
                for k in range(KC):
                    if k % 4 == 0:
                        pe.wait_ge(S("m_he_dve" if k == 0 else "m_he_act"), i * 4 + 4)
                    pe.wait_ge(S(f"m_wa{k}"), i * 32 + 16)
                    for j, (f0, w) in enumerate(FT):
                        if k == 0 and j == 0:
                            pe.wait_ge(S("m_added"), i * 4 + 1)
                        mm = pe.matmul(B(j)[:, 0:w], HE[:, k, :], WA[k][:, f0:f0 + w], start=k == 0, stop=k == KC - 1)
                    mm.then_inc(S("m_wa_used"), 1)
                for k in range(KC):
                    pe.wait_ge(S(f"m_wa{k}"), i * 32 + 32)
                    for j, (f0, w) in enumerate(FT):
                        if k == 0 and j >= 2:
                            pe.wait_ge(S("m_u"), i * 6 + j - 1)
                        mm = pe.matmul(B(VB[j])[:, 0:w], HE[:, k, :], WA[k][:, f0:f0 + w], start=k == 0, stop=k == KC - 1)
                    mm.then_inc(S("m_wa_used"), 1)
                for g in range(6 + 1):
                    if g < 6:
                        if g == 0:
                            pe.wait_ge(S("m_u"), i * 6 + 6)
                        pe.wait_ge(S("m_hidden"), i * 6 + g + 1)
                        if g >= 2:
                            pe.wait_ge(S("m_hidden"), i * 6 + [0, 0, 1, 2, 3, 4][g])
                        for f in range(4 * g, min(4 * g + 4, FC)):
                            mm = pe.transpose(B(TBK[g])[:, P * (f % 4):P * (f % 4) + P], UA[:, P * f:P * f + P], ident)
                        mm.then_inc(S("m_turned"), 1)
                    if g >= 1:
                        if g == 1:
                            pe.wait_ge(S("m_hidden"), i * 6 + 6)
                        pe.wait_ge(S("m_ae"), i * 6 + g)
                        for f in range(4 * g - 4, min(4 * g, FC)):
                            pe.wait_ge(S(f"m_wb{f % 11}"), i * 32 + 16 * (f // 11) + 16)
                            for h in range(2):
                                mm = pe.matmul(B(2 + h), AE[:, f, :], WB[f % 11][:, 512 * h:512 * h + 512],
                                               start=f == 0, stop=f == FC - 1)
                            mm.then_inc(S("m_wb_used"), 1)
                pe.wait_ge(S("m_gated"), i * 2 + 2)
                for x in range(2):
                    mm = pe.transpose(B(4)[:, P * x:P * x + P], PG[:, x, :], ident)
                mm.then_inc(S("m_gt"), 1)
                pe.wait_ge(S("m_pt"), i + 1)
                pe.wait_ge(S("m_ye"), i * 2 + 2)
                pe.wait_ge(S("m_ae"), i * 6 + 6)
                for j in range(4):
                    x, h = j // 2, j % 2
                    pe.matmul(B(SB[j]), PT[:, x, :], YE[:, 512 * h:512 * h + 512], start=True,
                              stop=True).then_inc(S("m_scattered"), 1)
            rounds(pe, body)

        def act_moe(act):
            def body(i, e, c):
                for k in range(4, KC):
                    if k == 4:
                        act.wait_ge(S("m_gathered"), i * 2 + 2)
                        act.wait_ge(S("m_scattered"), i * 4 + 1)
                    act.activation(HE[:, k, :], B(6 + k // 4)[:, P * (k % 4):P * (k % 4) + P], ACT.Identity,
                                   bias=MT[:, 3, k, 1:2], scale=MT[:, 4, k, 1:2]).then_inc(S("m_he_act"), 1)
                act.wait_ge(S("m_wa_used"), i * 16 + 16)
                for j, (f0, w) in enumerate(FT):
                    act.activation(UA[:, f0:f0 + w], B(j)[:, 0:w], ACT.Silu).then_inc(S("m_u"), 1)
                for g in range(0, 6, 2):
                    act.wait_ge(S("m_turned"), i * 6 + g + 1)
                    if g:
                        act.wait_ge(S("m_ae"), i * 6 + g)
                    act.activation(AE[:, 4 * g:4 * g + 4, :], B(TBK[g]).rearrange("p (a b) -> p a b", b=P),
                                   ACT.Copy).then_inc(S("m_ae"), 1)
                act.wait_ge(S("m_wb_used"), i * FC + FC + 11)
                act.activation(YE[:, 0:512], B(2), ACT.Copy).then_inc(S("m_ye"), 1)
                act.activation(YE[:, 512:1024], B(3), ACT.Copy).then_inc(S("m_ye"), 1)
            rounds(act, body)

        def dve_moe(dve):
            def body(i, e, c):
                for x in range(2):
                    at = bass.ds(c * 16 + 8 * x + e, 1)
                    dve.tensor_scalar(PH[:, x, :], kc(K_IOTA), POS.rearrange("p c x e -> p (c x e)")[:, at], None,
                                      ALU.is_equal).then_inc(S("m_onehot"), 1)
                dve.wait_ge(S("m_onehot"), i * 2 + 2)
                for x in range(2):
                    at = bass.ds(c * 16 + 8 * x + e, 1)
                    dve.tensor_scalar(PG[:, x, :], PH[:, x, :], GT.rearrange("p c x e -> p (c x e)")[:, at], None,
                                      ALU.mult).then_inc(S("m_gated"), 1)
                for k in range(4):
                    if k == 0:
                        dve.wait_ge(S("m_gathered"), i * 2 + 1)
                    dve.tensor_scalar(HE[:, k, :], B(6)[:, P * k:P * k + P], MT[:, 4, k, 1:2], MT[:, 3, k, 1:2],
                                      ALU.mult, ALU.add).then_inc(S("m_he_dve"), 1)
                dve.wait_ge(S("m_wa_used"), i * 16 + 24)
                for j, (f0, w) in enumerate(FT):
                    dve.wait_ge(S("m_u"), i * 6 + j + 1)
                    dve.tensor_tensor(UA[:, f0:f0 + w], B(VB[j])[:, 0:w], UA[:, f0:f0 + w], ALU.mult).then_inc(S("m_hidden"), 1)
                for g in range(1, 6, 2):
                    n = min(4, FC - 4 * g)
                    dve.wait_ge(S("m_turned"), i * 6 + g + 1)
                    dve.wait_ge(S("m_ae"), i * 6 + g)
                    dve.tensor_copy(AE[:, 4 * g:4 * g + n, :], B(TBK[g])[:, 0:n * P].rearrange("p (a b) -> p a b", b=P)
                                    ).then_inc(S("m_ae"), 1)
                dve.wait_ge(S("m_gt"), i + 1)
                dve.tensor_copy(PT, B(4)[:, 0:256].rearrange("p (a b) -> p a b", b=P)).then_inc(S("m_pt"), 1)
                for j in range(4):
                    x, h = j // 2, j % 2
                    dve.wait_ge(S("m_scattered"), i * 4 + j + 2)
                    v = Y[:, x, 512 * h:512 * h + 512]
                    dve.tensor_tensor(v, B(SB[j]), v, ALU.add).then_inc(S("m_added"), 1)
                dve.wait_ge(S("m_added"), i * 4 + 5)
            dve.sem_inc(S("m_added"), 1)
            rounds(dve, body)

        def dve_last(dve):
            dve.tensor_tensor(Y, Y, GATE[:, 1, 1:2, :].to_broadcast([P, 2, D]), ALU.mult).then_inc(S("y_gated"), 1)
            dve.wait_ge(S("y_gated"), 1)
            dve.tensor_tensor(X[:, 2:4, :], X[:, 2:4, :], Y, ALU.add).then_inc(S("x_done"), 1)

        SMALL = [(K[:, :], t["consts"]), (MASKF, t["masks"]),
                 (X[:, 0:2, :], t["ctx"][0].rearrange("(a p) n -> p a n", p=P)),
                 (X[:, 2:4, :], t["x"][0].rearrange("(a p) n -> p a n", p=P)),
                 (CIN[:, :, 0:1], t["c_ctx"].rearrange("(k p a) -> p k a", p=P, a=1)),
                 (CIN[:, :, 1:2], t["c"].rearrange("a (k p) -> p k a", p=P)),
                 (ROUT[:, :, :], t["moe_router"][0].rearrange("(k p) e -> p k e", p=P)),
                 (QKG[:, :, :, :], t["diff_qk_norm_g"].partition_broadcast(P)),
                 (LAMV[:, :, :, :], t["diff_lambda"].partition_broadcast(P)),
                 (SUBG[:, :, :], t["diff_subln_g"].partition_broadcast(P)),
                 (HNG[:, :, :], t["hgrn_norm_g"].partition_broadcast(P)),
                 (SQKG[:, :, :, :], t["swa_qk_norm_g"].partition_broadcast(P)),
                 (SINK[:, :, :], t["swa_sink"].partition_broadcast(P))]
        for L in range(DEPTH):
            SMALL.append((GMIX[:, L, :].unsqueeze(2), t["norm_mix_g"][L].rearrange("(k p a) -> p k a", p=P, a=1)))
            SMALL.append((GFFN[:, L, :].unsqueeze(2), t["norm_ffn_g"][L].rearrange("(k p a) -> p k a", p=P, a=1)))
            for d in range(2):
                SMALL.append((LBL[:, d, L, :].unsqueeze(2),
                              t["hgrn_lb_logits"][d, L].rearrange("(k p a) -> p k a", p=P, a=1)))

        def dve_setup(dve):
            step = [0]

            def then(ins):
                step[0] += 1
                ins.then_inc(S("setup_step"), 1)
                dve.wait_ge(S("setup_step"), step[0])

            then(dve.memset(NEGH[:, :], -0.5))
            dve.wait_ge(S("small_loaded"), 16 * len(SMALL))
            then(dve.tensor_copy(M8.rearrange("p a b c -> p (a b c)"), MASKF))
            then(dve.tensor_scalar(NSINK[:, :, :], SINK[:, :, :], -1.0, None, ALU.mult))
            l0, l1 = LBL[:, :, 0, :], LBL[:, :, 1, :]
            then(dve.tensor_tensor(LBT[:, 0, :, :], l0, l1, ALU.max))
            then(dve.tensor_tensor(LBT[:, 1, :, :], l0, LBT[:, 0, :, :], ALU.subtract))
            dve.tensor_tensor(LBT[:, 2, :, :], l1, LBT[:, 0, :, :], ALU.subtract).then_inc(S("lb_ready"), 1)
            for L in range(DEPTH):
                for j in range(2):
                    then(dve.tensor_tensor(LAMV[:, L, 2 * j, :], LAMV[:, L, 2 * j, :], LAMV[:, L, 2 * j + 1, :], ALU.mult))
                    then(dve.tensor_reduce(LAM[:, L, j:j + 1], LAMV[:, L, 2 * j, :], AX.X, ALU.add))
            dve.sem_inc(S("lam_ready"), 1)
            dve.wait_ge(S("setup_exp"), 1)
            then(dve.tensor_tensor(LBT[:, 3, :, :], LBT[:, 1, :, :], LBT[:, 2, :, :], ALU.add))
            then(dve.reciprocal(LBT[:, 3, :, :], LBT[:, 3, :, :]))
            then(dve.tensor_tensor(LBT[:, 1, :, :], LBT[:, 1, :, :], LBT[:, 3, :, :], ALU.mult))
            then(dve.tensor_tensor(LBT[:, 2, :, :], LBT[:, 2, :, :], LBT[:, 3, :, :], ALU.mult))
            then(dve.tensor_tensor(LBT[:, 2, :, :], LBT[:, 2, :, :], LBT[:, 1, :, :], ALU.add))
            then(dve.tensor_tensor(LBT[:, 4, :, :], LBT[:, 2, :, :], LBT[:, 1, :, :], ALU.subtract))
            then(dve.tensor_scalar(LBT[:, 5, :, :], LBT[:, 4, :, :], -1.0, 1.0, ALU.mult, ALU.add))
            for L in range(DEPTH):
                lam_init = 0.8 - 0.6 * math.exp(-0.3 * L)
                then(dve.tensor_tensor(LAM[:, L, 4:5], LAM[:, L, 3:4], LAM[:, L, 2:3], ALU.subtract))
                then(dve.tensor_scalar(LAM[:, L, 5:6], LAM[:, L, 4:5], -lam_init, None, ALU.add))

        def act_setup(act):
            act.wait_ge(S("small_loaded"), 16 * len(SMALL))
            act.activation(SC[:, :, :], CIN[:, :, :], ACT.Silu)
            act.wait_ge(S("lb_ready"), 1)
            act.wait_ge(S("lam_ready"), 1)
            act.activation(LAM[:, :, 2:4], LAM[:, :, 0:2], ACT.Exp)
            act.activation(LBT[:, 1:3, :, :], LBT[:, 1:3, :, :], ACT.Exp).then_inc(S("setup_exp"), 1)

        def ADA_STAGE(L):
            return 1 + 11 * L

        MOE_STAGE = 1 + 11 * DEPTH

        @block.sync
        def _(sp):
            for dst, src in SMALL:
                sp.dma_start(dst, src, allow_slow_non_contiguous=True).then_inc(S("small_loaded"), 16)
            for n, (pieces, _) in enumerate(plan):
                key = next(k for k, v in index.items() if v == n)
                if key[0] == "ada" and key[2] == 0:
                    L = key[1]
                    for other in ENG:
                        sp.wait_ge(S(f"{other}_stage_done"), ADA_STAGE(L))
                    sp.dma_start(ADAB[0:12, :], t["ada_b"][L].rearrange("(a n) -> a n", n=512)).then_inc(
                        S("adab_loaded"), 16)
                if n >= 2:
                    sp.wait_ge(S(plan[n - 2][1][0]), plan[n - 2][1][1])
                for where, src in pieces:
                    if where is None:
                        rows = min(4, FC - 4 * src)
                        dst = RING[n % 2].rearrange("p k n -> p (k n)")[:, 0:rows * D].rearrange("p (c n) -> p c n", n=D)
                        w = t["ffn_w2"][0][4 * P * src:4 * P * src + rows * P, :].rearrange("(c p) n -> p c n", p=P)
                    else:
                        dst, w = RING[n % 2][:, :, where], src
                    sp.dma_start(dst, w).then_inc(S(f"ring_full{n % 2}"), 16)
            sp_moe(sp)
            sp.wait_ge(S("x_done"), 1)
            sp.dma_start(t["out"][0].rearrange("(a p) n -> p a n", p=P), X[:, 2:4, :]).then_inc(S("stored"), 16)
            sp.wait_ge(S("stored"), 16)

        @block.tensor
        def _(pe):
            stage_end(pe, "pe")
            for L in range(DEPTH):
                for stage in (pe_ada, lambda e, l: pe_norm(e, l, 0), pe_proj, None, pe_levels, pe_states, pe_qkt,
                              pe_att, None, pe_out):
                    if stage:
                        stage(pe, L)
                    stage_end(pe, "pe")
                pe_norm(pe, L, 1)
                if L == 0:
                    pe.wait_ge(S("norm_ht_act"), 16)
                    pe.wait_ge(S("norm_ht_dve"), 16)
                    pe_ffn(pe)
                else:
                    pe.wait_ge(S("norm_ht_act"), 28)
                    pe.wait_ge(S("norm_ht_dve"), 28)
                    pe_route(pe)
                stage_end(pe, "pe")
            pe_moe(pe)

        @block.scalar
        def _(act):
            act_setup(act)
            stage_end(act, "act")
            for L in range(DEPTH):
                for stage in (act_ada, lambda e, l: act_norm(e, l, 0), act_proj, None, None, act_states, act_qkt,
                              act_att, None, act_out):
                    if stage:
                        stage(act, L)
                    stage_end(act, "act")
                act_norm(act, L, 1)
                if L == 0:
                    act_ffn(act)
                else:
                    act_route(act)
                stage_end(act, "act")
            act_moe(act)

        @block.gpsimd
        def _(pool):
            stage_end(pool, "pool")
            for L in range(DEPTH):
                for stage in (None, lambda e, l: pool_norm(e, l, 0), None, pool_qk, pool_levels, None,
                              lambda e, l: pool_post(e, l, "hp", 128), None, lambda e, l: pool_post(e, l, "dp", 64), None):
                    if stage:
                        stage(pool, L)
                    stage_end(pool, "pool")
                pool_norm(pool, L, 1)
                stage_end(pool, "pool")

        @block.vector
        def _(dve):
            dve_setup(dve)
            stage_end(dve, "dve")
            for L in range(DEPTH):
                lam_init = 0.8 - 0.6 * math.exp(-0.3 * L)
                dve_ada(dve, L)
                stage_end(dve, "dve")
                dve_norm(dve, L, 0)
                stage_end(dve, "dve")
                dve_proj(dve, L)
                stage_end(dve, "dve")
                dve_qk(dve, L)
                stage_end(dve, "dve")
                dve_levels(dve, L)
                stage_end(dve, "dve")
                dve_states(dve, L)
                stage_end(dve, "dve")
                dve_qkt(dve, L)
                dve_post(dve, L, "hp", 256, 128, HNG[:, L, :], None)
                stage_end(dve, "dve")
                dve_att(dve, L)
                stage_end(dve, "dve")
                dve_post(dve, L, "dp", 0, 64, SUBG[:, L, :], 1.0 - lam_init)
                stage_end(dve, "dve")
                dve_out(dve, L)
                stage_end(dve, "dve")
                dve_norm(dve, L, 1)
                if L == 0:
                    dve_ffn(dve)
                else:
                    dve_route(dve)
                stage_end(dve, "dve")
            dve_moe(dve)
            dve.drain()
            dve_last(dve)


_INS = ['x', 'c', 'ctx', 'c_ctx', 'ada_w', 'ada_b', 'norm_mix_g', 'norm_ffn_g', 'w_in', 'w_out',
        'diff_qk_norm_g', 'diff_lambda', 'diff_subln_g', 'hgrn_lb_logits', 'hgrn_norm_g',
        'swa_qk_norm_g', 'swa_sink', 'ffn_w1', 'ffn_w3', 'ffn_w2', 'moe_router', 'moe_w1', 'moe_w3', 'moe_w2']


def kernel(**inputs):
    import concourse.bacc as bacc
    from concourse.bass_utils import run_bass_kernel_spmd

    nc = bacc.Bacc("TRN2", target_bir_lowering=False, num_devices=1)
    arrays, t = {}, {}
    k, masks = constants()
    for name, a in [(n, inputs[n]) for n in _INS] + [("consts", k), ("masks", masks)]:
        a = np.ascontiguousarray(a)
        arrays["in_" + name] = a
        t[name] = nc.dram_tensor("in_" + name, a.shape, mybir.dt.from_np(a.dtype), kind="ExternalInput").ap()
    t["out"] = nc.dram_tensor("out_x", (1, 256, D), F32, kind="ExternalOutput").ap()
    trunk(nc, t)
    r = run_bass_kernel_spmd(nc, [arrays], core_ids=[0])
    return r.results[0]["out_x"]
```

```python
from contextlib import ExitStack
import math

import numpy as np
import concourse.bass as bass
import concourse.mybir as mybir

F32 = mybir.dt.float32
U8 = mybir.dt.uint8
BF16 = mybir.dt.bfloat16
I32 = mybir.dt.int32
ALU = mybir.AluOpType
ACT = mybir.ActivationFunctionType
AX = mybir.AxisListType

P = 128
D = 1024
KC = D // P
NT = 4
CTX_TILES, LAT_TILES = (0, 1), (2, 3)
DEPTH = 2
D_IN = 3840
D_FF = 2816
FC = D_FF // P
N_EXP = 8
EPS = 1e-6
GRID_W = 64
WINDOW = 128
NH = 4
C_AQK, C_AV, C_BQ, C_BI, C_BFF, C_BFB, C_BG, C_C = 0, 512, 768, 1280, 1792, 2304, 2816, 3328
LEVELS = [1, 2, 4, 8, 16, 32, 64]
FT = [(0, 512), (512, 512), (1024, 512), (1536, 512), (2048, 512), (2560, 256)]

K_ID, K_TRI, K_ONE, K_IOTA, K_C32, K_S32, K_C64, K_S64, K_SWA, K_REV, K_SELT, K_E12 = range(12)
K_WIDTH = {K_ID: 128, K_TRI: 128, K_ONE: 128, K_IOTA: 128, K_C32: 64, K_S32: 64, K_C64: 128,
           K_S64: 128, K_SWA: 256, K_REV: 16, K_SELT: 256, K_E12: 24}
K_AT = {k: sum(K_WIDTH[j] for j in range(k)) for k in K_WIDTH}
K_ALL = sum(K_WIDTH.values())


def constants():
    k = np.zeros((P, K_ALL), np.float32)

    def put(name, a):
        a = np.asarray(a, np.float32)
        k[:a.shape[0], K_AT[name]:K_AT[name] + a.shape[1]] = a

    i = np.arange(P)
    put(K_ID, np.eye(P))
    put(K_TRI, i[:, None] < i[None, :])
    put(K_ONE, np.ones((P, P)))
    put(K_IOTA, np.broadcast_to(i, (P, P)))
    tok = np.arange(2 * P)
    row, col = tok // GRID_W, tok % GRID_W
    for dim, kc, ks in ((32, K_C32, K_S32), (64, K_C64, K_S64)):
        nf = dim // 4
        inv = (np.float32(10000.0) ** (-np.arange(nf, dtype=np.float32) / np.float32(nf))).astype(np.float32)
        c, s = np.zeros((2 * P, dim)), np.zeros((2 * P, dim))
        for half, pos in enumerate((row, col)):
            ang = (pos.astype(np.float32)[:, None] * inv[None, :]).astype(np.float32).astype(np.float64)
            a = half * 2 * nf
            c[:, a:a + nf] = c[:, a + nf:a + 2 * nf] = np.cos(ang)
            s[:, a:a + nf] = -np.sin(ang)
            s[:, a + nf:a + 2 * nf] = np.sin(ang)
        put(kc, c.reshape(2, P, dim).transpose(1, 0, 2).reshape(P, 2 * dim))
        put(ks, s.reshape(2, P, dim).transpose(1, 0, 2).reshape(P, 2 * dim))
    swa = np.zeros((P, 2, P), np.float32)
    for b in range(2):
        swa[:, b] = np.where(np.abs((b * P + i)[:, None] - ((1 - b) * P + i)[None, :]) <= WINDOW, 0.0, -1e30)
    put(K_SWA, swa.reshape(P, -1))
    put(K_REV, np.broadcast_to(np.tile(8.0 - np.arange(8), 2), (P, 16)))
    sel = np.zeros((2, 2, P))
    sel[0, 0] = sel[1, 1] = 1
    put(K_SELT, sel.reshape(2, -1))
    e12 = np.zeros((12, 12, 2))
    e12[np.arange(12), np.arange(12)] = 1
    put(K_E12, e12.reshape(12, -1))
    m8 = np.zeros((P, 2, len(LEVELS), P), np.float32)
    s, t = i[:, None], i[None, :]
    for n, m in enumerate(LEVELS):
        same = s // (2 * m) == t // (2 * m)
        m8[:, 0, n] = same & (s % (2 * m) < m) & (t % (2 * m) >= m)
        m8[:, 1, n] = same & (s % (2 * m) >= m) & (t % (2 * m) < m)
    return k, m8.reshape(P, -1)


def bc(ap, axis, n):
    ap = ap.unsqueeze(axis)
    shape = list(ap.shape)
    shape[axis] = n
    return ap.to_broadcast(shape)


def trunk(nc, t):
    ctx = ExitStack()
    with ctx:
        def sb(name, shape, dt=F32):
            return ctx.enter_context(nc.sbuf_tensor(name, shape, dt))

        sems = {}

        def S(name):
            if name not in sems:
                sems[name] = ctx.enter_context(nc.semaphore(name))
            return sems[name]

        X = sb("X", [P, NT, D])
        GATE = sb("GATE", [P, 2, 2, D])
        K = sb("K", [P, K_ALL])
        M8 = sb("M8", [P, 2, len(LEVELS), P], U8)
        ARENA = sb("ARENA", [P, 161 * 256])
        MT = sb("MT", [P, 6, KC, 2])
        SC = sb("SC", [P, KC, 2])
        CIN = sb("CIN", [P, KC, 2])
        GMIX = sb("GMIX", [P, DEPTH, KC])
        GFFN = sb("GFFN", [P, DEPTH, KC])
        QKG = sb("QKG", [P, DEPTH, 2, 32])
        SUBG = sb("SUBG", [P, DEPTH, 64])
        HNG = sb("HNG", [P, DEPTH, 128])
        SQKG = sb("SQKG", [P, DEPTH, 2, 64])
        SINK = sb("SINK", [P, DEPTH, NH])
        NSINK = sb("NSINK", [P, DEPTH, NH])
        LBL = sb("LBL", [P, 2, DEPTH, NH])
        LBT = sb("LBT", [P, 6, 2, NH])
        LAM = sb("LAM", [P, DEPTH, 6])
        ROUT = sb("ROUT", [P, KC, N_EXP])
        NEGH = sb("NEGH", [P, 64])
        STAT = sb("STAT", [P, 4, 96])
        PS = ctx.enter_context(nc.psum_tensor("PS", [P, 8, 512], F32))

        def B(i):
            return PS[:, i, :]

        def kc(name, w=None):
            return K[:, K_AT[name]:K_AT[name] + (w or K_WIDTH[name])]

        ident = kc(K_ID)

        def A(at, *shape):
            n = int(np.prod(shape))
            a = int(at * 256)
            v = ARENA[:, a:a + n]
            names = "abcde"[:len(shape)]
            if len(shape) == 1:
                return v
            return v.rearrange(f"p ({' '.join(names)}) -> p {' '.join(names)}", **dict(zip(names[1:], shape[1:])))

        HT = A(0, KC, 512)
        ST = [A(0, NH, 512), A(8, NH, 512)]
        Q = A(16, NH, 512)
        QP = [A(24, NH, 512), A(32, NH, 512)]
        KE = [A(40, NH, 512), A(48, NH, 512)]
        FG = [A(56, NH, 512), A(64, NH, 512)]
        TB = [A(108, 1024), A(112, 1024)]
        SST = A(56, 3, 2, NH, P)
        KDT = A(68, 2, NH, P)
        V = A(72, NT, 512)
        G = A(80, NT, 512)
        AQK = A(88, NT, 512)
        AV = A(96, NT, 256)
        CQKV = A(100, NT, 512)
        MIX = A(108, NT, D)
        XN = A(24, NT, D)
        TMP = A(108, NT, 512)
        TMP2 = A(116, NT, 512)
        RING = [A(129, KC, 512), A(145, KC, 512)]
        QKT = A(0, 4, 512)
        CT = A(8, 3, 512)
        EX = A(24, 4, 2, 512)
        AT = A(40, 2, 512)
        MSK = A(44, 2, 512)
        OT = A(48, NT, 512)
        AST = A(56, 6, 32, 2)
        LAMV = A(0, DEPTH, 4, 32)
        MASKF = A(60, 2 * len(LEVELS) * P)
        YT = A(24, 2, 512)
        ADAB = A(0, 512)
        MROW = A(2, 2, 512)
        ACTT = A(16, FC, 512)
        FTMP = A(61, 8, 512)

        in_layer0 = {
            "adab_loaded": 16, "ada_mm": 12, "ada_row": 12, "ada_spread": 12, "ada_cp": 12,
            "proj_mm": 8 * NT, "proj_act": 4 * NT, "proj_dve": 4 * NT,
            "qk_sq": 2, "qk_ss": 2, "qk_ms": 2, "qk_rstd": 2, "qk_x": 1 + NT, "qk_gained": 4, "qk_turned": 12,
            "qk_rotated": 4,
            "s_kt": 6, "s_kd": 6, "s_kv": 6, "s_st": 6 * NH, "s_o": NT, "t_tp": 7,
            "a_msk": 2 * 2 * NH, "o_tp": KC, "o_mt_act": KC // 2, "o_mt_dve": KC // 2, "o_gated": 2 * NT,
            "o_added": 2 * NT, "out_mm": 2 * NT}
        for d in range(2):
            in_layer0.update({f"h{d}_f": 0, f"h{d}_qp": 1, f"h{d}_mm": 1 + len(LEVELS), f"h{d}_taken": 1 + len(LEVELS),
                              f"h{d}_upd": 3 * len(LEVELS)})
        for step in ("s", "mx", "nb", "exp", "r", "ratio", "p", "pt", "at", "pv", "o"):
            in_layer0["a_" + step] = 2 * NH * NT

        def since(L, name):
            return L * in_layer0[name]

        plan, index = [], {}

        def item(key, pieces, release):
            index[key] = len(plan)
            plan.append((pieces, release))

        def cols(w, a, n):
            return w.rearrange("(k p) n -> p k n", p=P)[:, :, a:a + n]

        def proj_units(L):
            out = []
            lat = LAT_TILES if L == DEPTH - 1 else range(NT)
            for key, kind, c0, w, eng in (
                    ("bff", "T", C_BFF, 512, "act"), ("aqk", "N", C_AQK, 512, "dve"),
                    ("bfb", "T", C_BFB, 512, "act"), ("c", "N", C_C, 512, "dve"),
                    ("bq", "T", C_BQ, 512, "act"), ("bi", "N", C_BI, 512, "dve"),
                    ("bg", "N", C_BG, 512, "act"), ("av", "N", C_AV, 256, "dve")):
                for u in (lat if key == "bg" else range(4)):
                    out.append((key, u, kind, c0, w, eng))
            return out

        for L in range(DEPTH):
            for j in range(12):
                item(("ada", L, j), [(slice(0, 512), cols(t["ada_w"][L], 512 * j, 512))], ("ada_mm", since(L, "ada_mm") + j + 1))
            units = proj_units(L)
            for key in dict.fromkeys(u[0] for u in units):
                c0, w = next((u[3], u[4]) for u in units if u[0] == key)
                last = max(i for i, u in enumerate(units) if u[0] == key)
                if key == "c":
                    pieces = [(slice(64 * n, 64 * n + 64), cols(t["w_in"][L], C_C + 64 * h, 64))
                              for n, h in enumerate((0, 2, 1, 3))]
                    pieces.append((slice(256, 512), cols(t["w_in"][L], C_C + 256, 256)))
                else:
                    pieces = [(slice(0, w), cols(t["w_in"][L], c0, w))]
                item((key, L), pieces, ("proj_mm", since(L, "proj_mm") + last + 1))
            n_out = NT if L == 0 else 2
            for h in range(2):
                item(("out", L, h), [(slice(0, 512), cols(t["w_out"][L], 512 * h, 512))],
                     ("out_mm", since(L, "out_mm") + n_out * (h + 1)))
            if L == 0:
                for n, (f0, w) in enumerate(FT):
                    item(("w1", n), [(slice(0, w), cols(t["ffn_w1"][0], f0, w))], ("ffn_u_mm", 4 * n + w // P))
                    item(("w3", n), [(slice(0, w), cols(t["ffn_w3"][0], f0, w))], ("ffn_v_mm", 4 * n + w // P))
                for n in range(6):
                    item(("w2", n), [(None, n)], ("ffn_y_mm", n + 1))

        full = []
        count = [0, 0]
        for n, (pieces, _) in enumerate(plan):
            count[n % 2] += 16 * len(pieces)
            full.append(count[n % 2])

        def slot_full(eng, key):
            n = index[key]
            eng.wait_ge(S(f"ring_full{n % 2}"), full[n])
            return RING[n % 2]

        ENG = ("pe", "act", "dve", "pool")
        stage_count = {e: 0 for e in ENG}

        def stage_end(eng, me):
            eng.drain().then_inc(S(f"{me}_stage_done"), 1)
            stage_count[me] += 1
            for other in ENG:
                if other != me:
                    eng.wait_ge(S(f"{other}_stage_done"), stage_count[me])

        def rng(L):
            return (0, 1) if L < DEPTH - 1 else (1,)

        def tiles(L):
            return range(NT) if L < DEPTH - 1 else LAT_TILES

        block = ctx.enter_context(nc.Block())

        def pe_ada(pe, L):
            for j in range(13):
                if j < 12:
                    slot = slot_full(pe, ("ada", L, j))
                    if j == 0:
                        pe.wait_ge(S("adab_loaded"), since(L, "adab_loaded") + 16)
                    if j >= 2:
                        pe.wait_ge(S("ada_row"), since(L, "ada_row") + j - 1)
                    ps = B(j % 2)[0:2, :]
                    e12 = K[0:12, K_AT[K_E12] + 2 * j:K_AT[K_E12] + 2 * j + 2]
                    pe.matmul(ps, e12, ADAB[0:12, :], start=True, stop=False)
                    for k in range(KC):
                        mm = pe.matmul(ps, SC[:, k, :], slot[:, k, :], start=False, stop=k == KC - 1)
                    mm.then_inc(S("ada_mm"), 1)
                if j >= 1:
                    i = j - 1
                    pe.wait_ge(S("ada_row"), since(L, "ada_row") + i + 1)
                    if i >= 1:
                        pe.wait_ge(S("ada_cp"), since(L, "ada_cp") + i)
                    if i // 2 in (2, 5):
                        for r in range(2):
                            sel = K[0:2, K_AT[K_SELT] + P * r:K_AT[K_SELT] + P * r + P]
                            mm = pe.matmul(B(2 + r), sel, MROW[0:2, i % 2, :], start=True, stop=True)
                    else:
                        for c in range(4):
                            mm = pe.matmul(B(4)[:, 2 * c:2 * c + 2], MROW[0:2, i % 2, P * c:P * c + P],
                                           ident[0:2, 0:2], start=True, stop=True)
                    mm.then_inc(S("ada_spread"), 1)

        def act_ada(act, L):
            for j in range(12):
                act.wait_ge(S("ada_mm"), since(L, "ada_mm") + j + 1)
                if j >= 2:
                    act.wait_ge(S("ada_spread"), since(L, "ada_spread") + j - 1)
                act.activation(MROW[0:2, j % 2, :], B(j % 2)[0:2, :], ACT.Copy).then_inc(S("ada_row"), 1)

        def dve_ada(dve, L):
            for j in range(12):
                m, half = j // 2, j % 2
                dve.wait_ge(S("ada_spread"), since(L, "ada_spread") + j + 1)
                if m in (2, 5):
                    dve.tensor_copy(GATE[:, m // 3, :, 512 * half:512 * half + 512],
                                    PS[:, 2:4, :]).then_inc(S("ada_cp"), 1)
                else:
                    dve.tensor_copy(MT[:, m, 4 * half:4 * half + 4, :],
                                    B(4)[:, 0:8].rearrange("p (c r) -> p c r", r=2)).then_inc(S("ada_cp"), 1)
            dve.wait_ge(S("ada_cp"), since(L, "ada_cp") + 12)
            for m, g in ((1, GMIX), (4, GFFN)):
                dve.scalar_tensor_tensor(out=MT[:, m, :, :], in0=MT[:, m, :, :], scalar=1.0,
                                         in1=bc(g[:, L, :], 2, 2), op0=ALU.add, op1=ALU.mult)

        def norm_tiles(L, which):
            return list(range(NT)) if which == 0 else list(tiles(L))

        def act_norm(act, L, which):
            n, tt, v = "norm_", norm_tiles(L, which), 2 * L + which
            for x in tt:
                act.activation(A(0, D), X[:, x, :], ACT.Square,
                               accum_out=STAT[:, 0, x:x + 1]).then_inc(S(n + "ss"), 1)
                act.wait_ge(S(n + "ss"), 4 * v + tt.index(x) + 1)
            for k in range(1, KC, 2):
                act.wait_ge(S(n + "tp"), KC * v + k + 1)
                for r in sorted({x // 2 for x in tt}):
                    act.activation(HT[:, k, 256 * r:256 * r + 256], B(k % 4)[:, 256 * r:256 * r + 256], ACT.Identity,
                                   bias=MT[:, 3 * which, k, r:r + 1],
                                   scale=MT[:, 3 * which + 1, k, r:r + 1]).then_inc(S(n + "ht_act"), 1)

        def pool_norm(pool, L, which):
            n, tt, v = "norm_", norm_tiles(L, which), 2 * L + which
            a, b = tt[0], tt[-1] + 1
            pool.wait_ge(S(n + "ss"), 4 * v + len(tt))
            pool.tensor_scalar(STAT[:, 1, a:b], STAT[:, 0, a:b], 1.0 / D, EPS, ALU.mult, ALU.add).then_inc(S(n + "ms"), 1)
            pool.wait_ge(S(n + "ms"), v + 1)
            pool.tensor_tensor(STAT[:, 2, a:b], STAT[:, 1, a:b], NEGH[:, 0:b - a], ALU.pow).then_inc(S(n + "rstd"), 1)

        def dve_norm(dve, L, which):
            n, tt, v = "norm_", norm_tiles(L, which), 2 * L + which
            dve.wait_ge(S(n + "rstd"), v + 1)
            for x in tt:
                dve.tensor_scalar(XN[:, x, :], X[:, x, :], STAT[:, 2, x:x + 1], None, ALU.mult).then_inc(S(n + "xn"), 1)
            for k in range(0, KC, 2):
                dve.wait_ge(S(n + "tp"), KC * v + k + 1)
                for r in sorted({x // 2 for x in tt}):
                    dve.tensor_scalar(HT[:, k, 256 * r:256 * r + 256], B(k % 4)[:, 256 * r:256 * r + 256],
                                      MT[:, 3 * which + 1, k, r:r + 1], MT[:, 3 * which, k, r:r + 1],
                                      ALU.mult, ALU.add).then_inc(S(n + "ht_dve"), 1)

        def pe_norm(pe, L, which):
            n, tt, v = "norm_", norm_tiles(L, which), 2 * L + which
            nr = len({x // 2 for x in tt})
            pe.wait_ge(S(n + "xn"), 4 * v + len(tt))
            for k in range(KC):
                if k >= 4:
                    pe.wait_ge(S(n + ("ht_act" if k % 2 else "ht_dve")), 8 * v + nr * ((k - 4) // 2 + 1))
                for x in tt:
                    mm = pe.transpose(B(k % 4)[:, P * x:P * x + P], XN[:, x, P * k:P * k + P], ident)
                mm.then_inc(S(n + "tp"), 1)

        def proj_places(L):
            seen = {"act": 0, "dve": 0}
            for key, u, kind, c0, w, eng in proj_units(L):
                i = seen[eng]
                seen[eng] += 1
                yield key, u, kind, w, eng, (0 if eng == "act" else 4) + i % 4, i

        def pe_proj(pe, L):
            last = None
            for key, u, kind, w, eng, bank, i in proj_places(L):
                if key != last:
                    slot = slot_full(pe, (key, L))
                    last = key
                if i >= 4:
                    pe.wait_ge(S(f"proj_{eng}"), since(L, f"proj_{eng}") + i - 3)
                for k in range(KC):
                    if kind == "T":
                        mm = pe.matmul(B(bank), slot[:, k, P * u:P * u + P], HT[:, k, :], start=k == 0, stop=k == KC - 1)
                    else:
                        mm = pe.matmul(B(bank)[:, 0:w], HT[:, k, P * u:P * u + P], slot[:, k, 0:w],
                                       start=k == 0, stop=k == KC - 1)
                mm.then_inc(S("proj_mm"), 1)

        def act_proj(act, L):
            for n, (key, u, kind, w, eng, bank, i) in enumerate(proj_places(L)):
                if eng != "act":
                    continue
                act.wait_ge(S("proj_mm"), since(L, "proj_mm") + n + 1)
                if key == "bq":
                    act.activation(Q[:, u, :], B(bank), ACT.Silu).then_inc(S("proj_act"), 1)
                elif key == "bg":
                    act.activation(G[:, u, :], B(bank), ACT.Silu).then_inc(S("proj_act"), 1)
                else:
                    d = 0 if key == "bff" else 1
                    act.activation(FG[d][:, u, :], B(bank), ACT.Sigmoid)
                    act.activation(KE[d][:, u, :], B(bank), ACT.Sigmoid, scale=-1.0).then_inc(S("proj_act"), 1)

        def dve_proj(dve, L, keys):
            dst = {"aqk": AQK, "c": CQKV, "bi": V, "av": AV}
            for n, (key, u, kind, w, eng, bank, i) in enumerate(proj_places(L)):
                if key not in keys:
                    continue
                dve.wait_ge(S("proj_mm"), since(L, "proj_mm") + n + 1)
                dve.tensor_copy(dst[key][:, u, :], B(bank)[:, 0:w]).then_inc(S("proj_dve"), 1)

        def dve_qk(dve, L):
            n = "qk_"
            c3 = CQKV[:, :, 0:384]
            a3 = AQK.rearrange("p a (g d) -> p (a g) d", d=32)
            dve.wait_ge(S("proj_dve"), since(L, "proj_dve") + 2 * NT)
            dve.tensor_tensor(TMP, AQK, AQK, ALU.mult).then_inc(S(n + "sq"), 1)
            dve.tensor_tensor(TMP2[:, :, 0:384], c3, c3, ALU.mult).then_inc(S(n + "sq"), 1)
            dve.wait_ge(S(n + "sq"), since(L, n + "sq") + 2)
            dve.tensor_reduce(STAT[:, 0, 0:64], TMP.rearrange("p a (g d) -> p (a g) d", d=32), AX.X, ALU.add).then_inc(S(n + "ss"), 1)
            dve.tensor_reduce(STAT[:, 0, 64:88].rearrange("p (a g) -> p a g", g=6),
                              TMP2[:, :, 0:384].rearrange("p a (g d) -> p a g d", d=64), AX.X, ALU.add).then_inc(S(n + "ss"), 1)
            dve.wait_ge(S(n + "rstd"), since(L, n + "rstd") + 2)
            dve.tensor_tensor(a3, a3, bc(STAT[:, 2, 0:64], 2, 32), ALU.mult).then_inc(S(n + "x"), 1)
            for x in range(NT):
                v = CQKV[:, x, 0:384].rearrange("p (g d) -> p g d", d=64)
                dve.tensor_tensor(v, v, bc(STAT[:, 2, 64 + 6 * x:70 + 6 * x], 2, 64), ALU.mult).then_inc(S(n + "x"), 1)
            dve.wait_ge(S(n + "x"), since(L, n + "x") + 1 + NT)
            for j in range(2):
                v = AQK[:, :, 256 * j:256 * j + 256].rearrange("p a (g d) -> p a g d", d=32)
                g = bc(bc(QKG[:, L, j, :], 1, 8), 1, NT)
                dve.tensor_tensor(v, v, g, ALU.mult).then_inc(S(n + "gained"), 1)
            for j, (a, b) in enumerate(((0, 256), (256, 384))):
                v = CQKV[:, :, a:b].rearrange("p a (g d) -> p a g d", d=64)
                g = bc(bc(SQKG[:, L, j, :], 1, (b - a) // 64), 1, NT)
                dve.tensor_tensor(v, v, g, ALU.mult).then_inc(S(n + "gained"), 1)

        def pool_qk(pool, L):
            n = "qk_"
            pool.wait_ge(S(n + "ss"), since(L, n + "ss") + 2)
            pool.tensor_scalar(STAT[:, 1, 0:64], STAT[:, 0, 0:64], 1.0 / 32, EPS, ALU.mult, ALU.add).then_inc(S(n + "ms"), 1)
            pool.tensor_scalar(STAT[:, 1, 64:88], STAT[:, 0, 64:88], 1.0 / 64, EPS, ALU.mult, ALU.add).then_inc(S(n + "ms"), 1)
            pool.wait_ge(S(n + "ms"), since(L, n + "ms") + 2)
            pool.tensor_tensor(STAT[:, 2, 0:64], STAT[:, 1, 0:64], NEGH[:, :], ALU.pow).then_inc(S(n + "rstd"), 1)
            pool.tensor_tensor(STAT[:, 2, 64:88], STAT[:, 1, 64:88], NEGH[:, 0:24], ALU.pow).then_inc(S(n + "rstd"), 1)
            pool.wait_ge(S(n + "gained"), since(L, n + "gained") + 4)
            for x in LAT_TILES:
                for src, dim, g, kcos, ksin in ((AQK[:, x, :], 32, 16, K_C32, K_S32),
                                                (CQKV[:, x, 0:384], 64, 6, K_C64, K_S64)):
                    c = kc(kcos)[:, dim * (x - 2):dim * (x - 1)]
                    s = kc(ksin)[:, dim * (x - 2):dim * (x - 1)]
                    nf = dim // 4
                    w = g * dim
                    v = src.rearrange("p (g d) -> p g d", d=dim)
                    turned = TMP2[:, x, 0:w].rearrange("p (g h b f) -> p g h b f", h=2, b=2, f=nf)
                    halves = src.rearrange("p (g h b f) -> p g h b f", h=2, b=2, f=nf)
                    sh = s.rearrange("p (h b f) -> p h b f", h=2, b=2)
                    for b in range(2):
                        pool.tensor_tensor(turned[:, :, :, b, :], halves[:, :, :, 1 - b, :],
                                           bc(sh[:, :, b, :], 1, g), ALU.mult).then_inc(S(n + "turned"), 1)
                    pool.tensor_tensor(TMP[:, x, 0:w].rearrange("p (g d) -> p g d", d=dim), v, bc(c, 1, g),
                                       ALU.mult).then_inc(S(n + "turned"), 1)
                    k = 3 * (2 * (x - 2) + (0 if dim == 32 else 1) + 1)
                    pool.wait_ge(S(n + "turned"), since(L, n + "turned") + k)
                    pool.tensor_tensor(src, TMP[:, x, 0:w], TMP2[:, x, 0:w], ALU.add).then_inc(S(n + "rotated"), 1)
                    pool.wait_ge(S(n + "rotated"), since(L, n + "rotated") + k // 3)

        def hgrn_gates(eng, L, d):
            n = f"h{d}_"
            eng.wait_ge(S("proj_act"), since(L, "proj_act") + 3 * NH)
            if L > 0:
                for h in range(NH):
                    eng.tensor_scalar(FG[d][:, h, :], FG[d][:, h, :], LBT[:, 5, d, h:h + 1], LBT[:, 4, d, h:h + 1],
                                      ALU.mult, ALU.add).then_inc(S(n + "f"), 1)
                    eng.tensor_scalar(KE[d][:, h, :], KE[d][:, h, :], LBT[:, 5, d, h:h + 1], None,
                                      ALU.mult).then_inc(S(n + "f"), 1)
                eng.wait_ge(S(n + "f"), since(L, n + "f") + 2 * NH)
            eng.tensor_tensor(QP[d], Q, FG[d], ALU.mult).then_inc(S(n + "qp"), 1)
            eng.wait_ge(S(n + "qp"), since(L, n + "qp") + 1)

        def hgrn_double(eng, L, d, n_level):
            n = f"h{d}_"
            m = LEVELS[n_level]
            nb = NH * 512 // m
            tot = FG[d].rearrange("p a b -> p (a b)") if n_level == 0 else (
                TB[d][:, 0:nb] if n_level % 2 else FG[d].rearrange("p a b -> p (a b)")[:, 0:nb])
            new = TB[d][:, 0:nb // 2] if n_level % 2 == 0 else FG[d].rearrange("p a b -> p (a b)")[:, 0:nb // 2]
            tv = tot.rearrange("p (b h) -> p b h", h=2)
            early, late = (0, 1) if d == 0 else (1, 0)
            qv = QP[d].rearrange("p a b -> p (a b)").rearrange("p (b h m) -> p b h m", h=2, m=m)
            kv = KE[d].rearrange("p a b -> p (a b)").rearrange("p (b h m) -> p b h m", h=2, m=m)
            eng.wait_ge(S(n + "mm"), since(L, n + "mm") + n_level + 2)
            eng.tensor_tensor(qv[:, :, late, :], qv[:, :, late, :], bc(tv[:, :, early], 2, m), ALU.mult).then_inc(S(n + "upd"), 1)
            eng.tensor_tensor(kv[:, :, early, :], kv[:, :, early, :], bc(tv[:, :, late], 2, m), ALU.mult).then_inc(S(n + "upd"), 1)
            eng.tensor_tensor(new, tv[:, :, 0], tv[:, :, 1], ALU.mult).then_inc(S(n + "upd"), 1)
            eng.wait_ge(S(n + "upd"), since(L, n + "upd") + 3 * (n_level + 1))

        def pe_levels(pe, L):
            ts = list(tiles(L))
            pe.wait_ge(S("proj_act"), since(L, "proj_act") + 3 * NH + len(ts))
            pe.wait_ge(S("proj_dve"), since(L, "proj_dve") + 4 * NT)
            for n_level in range(-1, len(LEVELS)):
                for d in range(2):
                    n = f"h{d}_"
                    pe.wait_ge(S(n + "qp"), since(L, n + "qp") + 1)
                    if n_level >= 1:
                        pe.wait_ge(S(n + "upd"), since(L, n + "upd") + 3 * n_level)
                    if n_level >= 0:
                        pe.wait_ge(S(n + "taken"), since(L, n + "taken") + n_level + 1)
                    for h in range(NH):
                        for x in ts:
                            c = slice(P * x, P * x + P)
                            q = Q if n_level < 0 else QP[d]
                            mm = pe.matmul(B(4 * d + h)[:, c], KE[d][:, h, c], q[:, h, c], start=True, stop=True)
                    mm.then_inc(S(n + "mm"), 1)

        def dve_take(dve, L, d, n_level):
            n = f"h{d}_"
            ts = list(tiles(L))
            a, nt = P * ts[0], len(ts)
            dve.wait_ge(S(n + "mm"), since(L, n + "mm") + n_level + 2)
            if n_level < 0:
                for h in range(NH):
                    src = B(4 * d + h)[:, a:].rearrange("p (x t) -> p x t", t=P)
                    dst = ST[d][:, h, a:].rearrange("p (x t) -> p x t", t=P)
                    ins = dve.tensor_tensor(dst, src, bc(ident, 1, nt), ALU.mult)
            else:
                for h in range(NH):
                    src = B(4 * d + h)[:, a:].rearrange("p (x t) -> p x t", t=P)
                    dst = ST[d][:, h, a:].rearrange("p (x t) -> p x t", t=P)
                    dve.wait_ge(S(n + "taken"), since(L, n + "taken") + n_level + 1)
                    ins = dve.copy_predicated(dst, bc(M8[:, d, n_level, :], 1, nt), src)
            ins.then_inc(S(n + "taken"), 1)

        def dve_levels(dve, L):
            dve.wait_ge(S("qk_rotated"), since(L, "qk_rotated") + 4)
            dve_take(dve, L, 0, -1)
            dve_take(dve, L, 1, -1)
            for n_level in range(len(LEVELS)):
                dve_take(dve, L, 0, n_level)
                hgrn_double(dve, L, 0, n_level)
                dve_take(dve, L, 1, n_level)

        def pool_levels(pool, L):
            hgrn_gates(pool, L, 1)
            for n_level in range(len(LEVELS)):
                hgrn_double(pool, L, 1, n_level)

        def pe_mix_in(pe, L):
            pe_proj(pe, L)
            pe_levels(pe, L)

        def pool_mix_in(pool, L):
            pool_qk(pool, L)
            pool_levels(pool, L)

        ORDER = [(0, 1, 2, 3), (1, 0, 3, 2)]

        def pe_states(pe, L):
            n = "s_"
            for i in range(3):
                b0 = 4 * (i % 2)
                for d in range(2):
                    x = ORDER[d][i]
                    for h in range(NH):
                        mm = pe.transpose(B(b0 + d)[:, P * h:P * h + P], KE[d][:, h, P * x:P * x + P], ident)
                    mm.then_inc(S(n + "kt"), 1)
                for d in range(2):
                    x = ORDER[d][i]
                    pe.wait_ge(S(n + "kd"), since(L, n + "kd") + 2 * i + d + 1)
                    if i >= 2:
                        pe.wait_ge(S(n + "st"), since(L, n + "st") + 2 * NH * (i - 1))
                    for h in range(NH):
                        mm = pe.matmul(B(b0 + 2 + d)[:, P * h:P * h + P], KDT[:, d, h, :], V[:, x, P * h:P * h + P],
                                       start=True, stop=True)
                    mm.then_inc(S(n + "kv"), 1)
            pe.wait_ge(S(n + "st"), since(L, n + "st") + 6 * NH)
            for j, x in enumerate(tiles(L)):
                c = slice(P * x, P * x + P)
                for h in range(NH):
                    o = B(j)[:, P * h:P * h + P]
                    v = V[:, x, P * h:P * h + P]
                    pairs = [(ST[0][:, h, c], v), (ST[1][:, h, c], v)]
                    for d in range(2):
                        i = ORDER[d].index(x)
                        if i:
                            pairs.append((QP[d][:, h, c], SST[:, i - 1, d, h, :]))
                    for k, (a, b) in enumerate(pairs):
                        mm = pe.matmul(o, a, b, start=k == 0, stop=k == len(pairs) - 1)
                mm.then_inc(S(n + "o"), 1)

        def act_states(act, L):
            n = "s_"
            for i in range(3):
                for d in range(2):
                    act.wait_ge(S(n + "kt"), since(L, n + "kt") + 2 * i + d + 1)
                    if i:
                        act.wait_ge(S(n + "kv"), since(L, n + "kv") + 2 * (i - 1) + d + 1)
                    act.activation(KDT[:, d, :, :], B(4 * (i % 2) + d).rearrange("p (h k) -> p h k", k=P),
                                   ACT.Copy).then_inc(S(n + "kd"), 1)

        def dve_states(dve, L):
            n = "s_"
            for i in range(3):
                for d in range(2):
                    x = ORDER[d][i]
                    dve.wait_ge(S(n + "kv"), since(L, n + "kv") + 2 * i + d + 1)
                    if i:
                        dve.wait_ge(S(n + "st"), since(L, n + "st") + 2 * NH * i)
                    for h in range(NH):
                        ps = B(4 * (i % 2) + 2 + d)[:, P * h:P * h + P]
                        if i == 0:
                            dve.tensor_copy(SST[:, 0, d, h, :], ps).then_inc(S(n + "st"), 1)
                        else:
                            total = TB[d][:, NT * h + x:NT * h + x + 1]
                            dve.scalar_tensor_tensor(out=SST[:, i, d, h, :], in0=SST[:, i - 1, d, h, :], scalar=total,
                                                     in1=ps, op0=ALU.mult, op1=ALU.add).then_inc(S(n + "st"), 1)
            for j, x in enumerate(tiles(L)):
                dve.wait_ge(S(n + "o"), since(L, n + "o") + j + 1)
                dve.tensor_copy(MIX[:, x, 256:768], B(j)).then_inc(S(n + "mix"), 1)

        def out_rows(L):
            ts = list(tiles(L))
            return slice(ts[0], ts[-1] + 1), len(ts)

        def dve_post(dve, L, name, c0, dim, gain, extra):
            n, v = "post_", 2 * L + (name == "dp")
            rows, nt = out_rows(L)
            hs = 512 // dim if name == "hp" else 256 // dim
            w = hs * dim
            o = MIX[:, rows, c0:c0 + w]
            sq = OT[:, rows, 0:w]
            dve.tensor_tensor(sq, o, o, ALU.mult).then_inc(S(n + "sq"), 1)
            dve.wait_ge(S(n + "sq"), v + 1)
            st = STAT[:, 0, 0:nt * hs]
            dve.tensor_reduce(st.rearrange("p (a g) -> p a g", g=hs), sq.rearrange("p a (g d) -> p a g d", d=dim),
                              AX.X, ALU.add).then_inc(S(n + "ss"), 1)
            dve.wait_ge(S(n + "rstd"), v + 1)
            for j, x in enumerate(tiles(L)):
                mv = MIX[:, x, c0:c0 + w].rearrange("p (g d) -> p g d", d=dim)
                dve.tensor_tensor(mv, mv, bc(STAT[:, 2, hs * j:hs * j + hs], 2, dim), ALU.mult).then_inc(S(n + "x"), 1)
            dve.wait_ge(S(n + "x"), (0, 4, 8, 10)[v] + nt)
            ov = o.rearrange("p a (g d) -> p a g d", d=dim)
            dve.tensor_tensor(ov, ov, bc(bc(gain, 1, hs), 1, nt), ALU.mult).then_inc(S(n + "g"), 1)
            dve.wait_ge(S(n + "g"), v + 1)
            if name == "hp":
                dve.tensor_tensor(o, o, G[:, rows, :], ALU.mult)
            else:
                dve.tensor_scalar(o, o, extra, None, ALU.mult)

        def pool_post(pool, L, name, dim):
            n, v = "post_", 2 * L + (name == "dp")
            nt = out_rows(L)[1]
            w = nt * ((512 if name == "hp" else 256) // dim)
            pool.wait_ge(S(n + "ss"), v + 1)
            pool.tensor_scalar(STAT[:, 1, 0:w], STAT[:, 0, 0:w], 1.0 / dim, EPS, ALU.mult, ALU.add).then_inc(S(n + "ms"), 1)
            pool.wait_ge(S(n + "ms"), v + 1)
            pool.tensor_tensor(STAT[:, 2, 0:w], STAT[:, 1, 0:w], NEGH[:, 0:w], ALU.pow).then_inc(S(n + "rstd"), 1)

        def units(L):
            return [(kind, h, x) for x in tiles(L) for h in range(NH) for kind in "DW"]

        def keys(x):
            return 256 if x in CTX_TILES else 512

        def masked(L, u):
            return sum(k == "W" and x in LAT_TILES for k, _, x in units(L)[:u])

        def pe_qkt(pe, L):
            n = "t_"
            for b in range(7):
                for x in range(NT):
                    src = AQK[:, x, P * b:P * b + P] if b < 4 else CQKV[:, x, P * (b - 4):P * (b - 3)]
                    mm = pe.transpose(B(b)[:, P * x:P * x + P], src, ident)
                mm.then_inc(S(n + "tp"), 1)

        def act_qkt(act, L):
            for b in range(0, 7, 2):
                act.wait_ge(S("t_tp"), since(L, "t_tp") + b + 1)
                act.activation(QKT[:, b, :] if b < 4 else CT[:, b - 4, :], B(b), ACT.Copy)

        def dve_qkt(dve, L):
            for b in range(1, 7, 2):
                dve.wait_ge(S("t_tp"), since(L, "t_tp") + b + 1)
                dve.tensor_copy(QKT[:, b, :] if b < 4 else CT[:, b - 4, :], B(b))

        def pe_att(pe, L):
            n, us = "a_", units(L)
            for s in range(len(us) + 3):
                if s < len(us):
                    kind, h, x = us[s]
                    if s >= 2:
                        pe.wait_ge(S(n + "exp"), since(L, n + "exp") + s - 1)
                    c, nk = slice(P * x, P * x + P), keys(x)
                    if kind == "D":
                        for m in range(2):
                            g = 2 * h + m
                            r = slice(32 * (g % 4), 32 * (g % 4) + 32)
                            mm = pe.matmul(B(2 * (s % 2) + m)[:, 0:nk], QKT[r, g // 4, c], QKT[r, 2 + g // 4, 0:nk],
                                           start=True, stop=True)
                    else:
                        r = slice(64 * (h // 2), 64 * (h // 2) + 64)
                        mm = pe.matmul(B(2 * (s % 2))[:, 0:nk], CT[r, h % 2, c], CT[r, 2, 0:nk], start=True, stop=True)
                    mm.then_inc(S(n + "s"), 1)
                if 2 <= s < len(us) + 2:
                    u = s - 2
                    pe.wait_ge(S(n + "p"), since(L, n + "p") + u + 1)
                    if u >= 2:
                        pe.wait_ge(S(n + "at"), since(L, n + "at") + u - 1)
                    for k in range(keys(us[u][2]) // P):
                        mm = pe.transpose(B(4 + u % 2)[:, P * k:P * k + P], EX[:, u % 4, 0, P * k:P * k + P], ident)
                    mm.then_inc(S(n + "pt"), 1)
                if s >= 3:
                    u = s - 3
                    kind, h, x = us[u]
                    pe.wait_ge(S(n + "at"), since(L, n + "at") + u + 1)
                    if u >= 2:
                        pe.wait_ge(S(n + "o"), since(L, n + "o") + u - 1)
                    nk = keys(x) // P
                    for k in range(nk):
                        v = AV[:, k, 64 * h:64 * h + 64] if kind == "D" else CQKV[:, k, 384 + 64 * (h // 2):448 + 64 * (h // 2)]
                        mm = pe.matmul(B(6 + u % 2)[:, 0:64], AT[:, u % 2, P * k:P * k + P], v, start=k == 0, stop=k == nk - 1)
                    mm.then_inc(S(n + "pv"), 1)

        def act_att(act, L):
            n, us = "a_", units(L)
            for s in range(len(us) + 2):
                if s < len(us):
                    kind, h, x = us[s]
                    nk = keys(x)
                    act.wait_ge(S(n + "nb"), since(L, n + "nb") + s + 1)
                    if s >= 4:
                        act.wait_ge(S(n + "pt"), since(L, n + "pt") + s - 3)
                    if kind == "D":
                        for m in range(2):
                            ins = act.activation(EX[:, s % 4, m, 0:nk], B(2 * (s % 2) + m)[:, 0:nk], ACT.Exp,
                                                 bias=AST[:, 1, s, m:m + 1], scale=32 ** -0.5,
                                                 accum_out=AST[:, 2, s, m:m + 1])
                    else:
                        src = MSK[:, masked(L, s) % 2, :] if x in LAT_TILES else B(2 * (s % 2))[:, 0:nk]
                        act.activation(AST[:, 3, s, 0:1], SINK[:, L, h:h + 1], ACT.Exp, bias=AST[:, 1, s, 0:1])
                        ins = act.activation(EX[:, s % 4, 0, 0:nk], src, ACT.Exp, bias=AST[:, 1, s, 0:1],
                                             scale=64 ** -0.5, accum_out=AST[:, 2, s, 0:1])
                    ins.then_inc(S(n + "exp"), 1)
                if s >= 2:
                    u = s - 2
                    nk = keys(us[u][2])
                    act.wait_ge(S(n + "pt"), since(L, n + "pt") + u + 1)
                    if u >= 2:
                        act.wait_ge(S(n + "pv"), since(L, n + "pv") + u - 1)
                    act.activation(AT[:, u % 2, 0:nk], B(4 + u % 2)[:, 0:nk], ACT.Copy).then_inc(S(n + "at"), 1)

        def dve_att(dve, L):
            n, us = "a_", units(L)
            for s in range(len(us) + 4):
                if s < len(us):
                    kind, h, x = us[s]
                    nk = keys(x)
                    dve.wait_ge(S(n + "s"), since(L, n + "s") + s + 1)
                    if kind == "D":
                        dve.tensor_reduce(AST[:, 0, s, :], PS[:, 2 * (s % 2):2 * (s % 2) + 2, 0:nk], AX.X,
                                          ALU.max).then_inc(S(n + "mx"), 1)
                        dve.wait_ge(S(n + "mx"), since(L, n + "mx") + s + 1)
                        dve.tensor_scalar(AST[:, 1, s, :], AST[:, 0, s, :], -(32 ** -0.5), None,
                                          ALU.mult).then_inc(S(n + "nb"), 1)
                    else:
                        src = B(2 * (s % 2))[:, 0:nk]
                        if x in LAT_TILES:
                            w = masked(L, s)
                            if w >= 2:
                                before = [i for i, (k, _, y) in enumerate(us) if k == "W" and y in LAT_TILES][w - 2]
                                dve.wait_ge(S(n + "exp"), since(L, n + "exp") + before + 1)
                            dst = MSK[:, w % 2, :]
                            o = 384 if x == 2 else 256
                            dve.tensor_tensor(dst[:, o:o + P], src[:, o:o + P], kc(K_SWA)[:, P * (x - 2):P * (x - 1)],
                                              ALU.add).then_inc(S(n + "msk"), 1)
                            if x == 2:
                                dve.tensor_copy(dst[:, 0:384], src[:, 0:384]).then_inc(S(n + "msk"), 1)
                            else:
                                dve.tensor_copy(dst[:, 0:256], src[:, 0:256])
                                dve.tensor_copy(dst[:, 384:512], src[:, 384:512]).then_inc(S(n + "msk"), 1)
                            dve.wait_ge(S(n + "msk"), since(L, n + "msk") + 2 * (w + 1))
                            src = dst
                        dve.tensor_reduce(AST[:, 0, s, 0:1], src, AX.X, ALU.max).then_inc(S(n + "mx"), 1)
                        dve.wait_ge(S(n + "mx"), since(L, n + "mx") + s + 1)
                        dve.tensor_scalar(AST[:, 1, s, 0:1], AST[:, 0, s, 0:1], -(64 ** -0.5), NSINK[:, L, h:h + 1],
                                          ALU.mult, ALU.min).then_inc(S(n + "nb"), 1)
                if 1 <= s <= len(us):
                    u = s - 1
                    kind, h, x = us[u]
                    nk = keys(x)
                    dve.wait_ge(S(n + "exp"), since(L, n + "exp") + u + 1)
                    if kind == "D":
                        dve.reciprocal(AST[:, 4, u, :], AST[:, 2, u, :]).then_inc(S(n + "r"), 1)
                        dve.wait_ge(S(n + "r"), since(L, n + "r") + u + 1)
                        dve.tensor_scalar(AST[:, 5, u, 0:1], AST[:, 4, u, 1:2], AST[:, 2, u, 0:1], LAM[:, L, 5:6],
                                          ALU.mult, ALU.mult).then_inc(S(n + "ratio"), 1)
                        dve.wait_ge(S(n + "ratio"), since(L, n + "ratio") + u + 1)
                        e = EX[:, u % 4, 0, 0:nk]
                        dve.scalar_tensor_tensor(out=e, in0=EX[:, u % 4, 1, 0:nk], scalar=AST[:, 5, u, 0:1], in1=e,
                                                 op0=ALU.mult, op1=ALU.add).then_inc(S(n + "p"), 1)
                    else:
                        dve.tensor_tensor(AST[:, 5, u, 0:1], AST[:, 2, u, 0:1], AST[:, 3, u, 0:1], ALU.add).then_inc(S(n + "ratio"), 1)
                        dve.wait_ge(S(n + "ratio"), since(L, n + "ratio") + u + 1)
                        dve.reciprocal(AST[:, 4, u, 0:1], AST[:, 5, u, 0:1]).then_inc(S(n + "r"), 1)
                        dve.wait_ge(S(n + "r"), since(L, n + "r") + u + 1)
                        dve.tensor_copy(AST[:, 3, u, 1:2], AST[:, 4, u, 0:1]).then_inc(S(n + "p"), 1)
                if s >= 4:
                    u = s - 4
                    kind, h, x = us[u]
                    dve.wait_ge(S(n + "pv"), since(L, n + "pv") + u + 1)
                    c = (0 if kind == "D" else 768) + 64 * h
                    dve.tensor_scalar(MIX[:, x, c:c + 64], B(6 + u % 2)[:, 0:64], AST[:, 4, u, 0:1], None,
                                      ALU.mult).then_inc(S(n + "o"), 1)

        def pe_out(pe, L):
            n, ts = "o_", list(tiles(L))
            for k in range(KC):
                if k >= 4:
                    pe.wait_ge(S(n + ("mt_act" if k % 2 else "mt_dve")), since(L, n + ("mt_act" if k % 2 else "mt_dve")) + (k - 4) // 2 + 1)
                for x in ts:
                    mm = pe.transpose(B(k % 4)[:, P * x:P * x + P], MIX[:, x, P * k:P * k + P], ident)
                mm.then_inc(S(n + "tp"), 1)
            pe.wait_ge(S(n + "mt_act"), since(L, n + "mt_act") + 4)
            pe.wait_ge(S(n + "mt_dve"), since(L, n + "mt_dve") + 4)
            for h in range(2):
                slot = slot_full(pe, ("out", L, h))
                for j, x in enumerate(ts):
                    i = len(ts) * h + j
                    for k in range(KC):
                        mm = pe.matmul(B(i), HT[:, k, P * x:P * x + P], slot[:, k, :], start=k == 0, stop=k == KC - 1)
                    mm.then_inc(S("out_mm"), 1)

        def act_out(act, L):
            n, ts = "o_", list(tiles(L))
            for k in range(1, KC, 2):
                act.wait_ge(S(n + "tp"), since(L, n + "tp") + k + 1)
                act.activation(HT[:, k, P * ts[0]:], B(k % 4)[:, P * ts[0]:], ACT.Copy).then_inc(S(n + "mt_act"), 1)

        def dve_out(dve, L):
            n, ts = "o_", list(tiles(L))
            for k in range(0, KC, 2):
                dve.wait_ge(S(n + "tp"), since(L, n + "tp") + k + 1)
                dve.tensor_copy(HT[:, k, P * ts[0]:], B(k % 4)[:, P * ts[0]:]).then_inc(S(n + "mt_dve"), 1)
            for h in range(2):
                for j, x in enumerate(ts):
                    i = len(ts) * h + j
                    dve.wait_ge(S("out_mm"), since(L, "out_mm") + i + 1)
                    if i >= 2:
                        dve.wait_ge(S(n + "added"), since(L, n + "added") + i - 1)
                    c = slice(512 * h, 512 * h + 512)
                    dve.tensor_tensor(YT[:, i % 2, :], B(i), GATE[:, 0, x // 2, c], ALU.mult).then_inc(S(n + "gated"), 1)
                    dve.wait_ge(S(n + "gated"), since(L, n + "gated") + i + 1)
                    dve.tensor_tensor(X[:, x, c], X[:, x, c], YT[:, i % 2, :], ALU.add).then_inc(S(n + "added"), 1)

        def pe_ffn(pe):
            for n, (f0, w) in enumerate(FT):
                for key, b0, sem, ev in (("w1", 0, "ffn_u_mm", "ffn_u"), ("w3", 4, "ffn_v_mm", "ffn_act")):
                    slot = slot_full(pe, (key, n))
                    for c in range(w // P):
                        if n:
                            pe.wait_ge(S(ev), 4 * (n - 1) + c + 1)
                        for k in range(KC):
                            mm = pe.matmul(B(b0 + c), slot[:, k, P * c:P * c + P], HT[:, k, :], start=k == 0, stop=k == KC - 1)
                        mm.then_inc(S(sem), 1)
            pe.wait_ge(S("ffn_act"), FC)
            for n in range(6):
                slot = slot_full(pe, ("w2", n)).rearrange("p k n -> p (k n)")
                for c in range(4 * n, min(4 * n + 4, FC)):
                    for x in range(NT):
                        for h in range(2):
                            a = D * (c - 4 * n) + 512 * h
                            mm = pe.matmul(B(2 * x + h), ACTT[:, c, P * x:P * x + P], slot[:, a:a + 512],
                                           start=c == 0, stop=c == FC - 1)
                mm.then_inc(S("ffn_y_mm"), 1)

        def act_ffn(act):
            for c in range(FC):
                act.wait_ge(S("ffn_u_mm"), c + 1)
                act.activation(ACTT[:, c, :], B(c % 4), ACT.Silu).then_inc(S("ffn_u"), 1)

        def dve_ffn(dve):
            for c in range(FC):
                dve.wait_ge(S("ffn_u"), c + 1)
                dve.wait_ge(S("ffn_v_mm"), c + 1)
                dve.tensor_tensor(ACTT[:, c, :], B(4 + c % 4), ACTT[:, c, :], ALU.mult).then_inc(S("ffn_act"), 1)
            dve.wait_ge(S("ffn_y_mm"), 6)
            for i in range(8):
                x, h = i // 2, i % 2
                dve.tensor_tensor(FTMP[:, i, :], B(i), GATE[:, 1, x // 2, 512 * h:512 * h + 512],
                                  ALU.mult).then_inc(S("ffn_gated"), 1)
            for i in range(8):
                x, c = i // 2, slice(512 * (i % 2), 512 * (i % 2) + 512)
                dve.wait_ge(S("ffn_gated"), i + 1)
                dve.tensor_tensor(X[:, x, c], X[:, x, c], FTMP[:, i, :], ALU.add)

        NPIECE, NRAW, NSPLIT = 24, 4, 8
        RAW = [A(11 * s, D_FF) for s in range(NRAW)]
        SPLIT = [ARENA[:, 256 * (44 + 11 * s):256 * (55 + 11 * s)].bitcast(BF16) for s in range(NSPLIT)]
        WHI = [v[:, 0:D_FF] for v in SPLIT]
        WLO = [v[:, D_FF:2 * D_FF] for v in SPLIT]
        UA = A(132, D_FF)
        AEP = ARENA[:, 256 * 143:256 * 154].bitcast(BF16).rearrange("p (h c s) -> p h c s", h=2, c=FC)
        AEH, AEL = AEP[:, 0], AEP[:, 1]
        HEP = ARENA[:, 256 * 154:256 * 158].bitcast(BF16).rearrange("p (h k s) -> p h k s", h=2, k=KC)
        HEH, HEL = HEP[:, 0], HEP[:, 1]
        PG = A(158, 2, P)
        PT = A(159, 2, P)
        PH = ARENA[:, 256 * 160:256 * 160 + P].bitcast(BF16).rearrange("p (x s) -> p x s", x=2)
        XLP = GATE[:, 0, :, :].rearrange("p a n -> p (a n)").bitcast(BF16).rearrange("p (h x n) -> p h x n", h=2, x=2)
        XLH, XLL = XLP[:, 0], XLP[:, 1]
        YE = GATE[:, 1, 0, :]
        Y = X[:, 0:2, :]
        RT = A(16, 9, 2, N_EXP)
        RV = A(17, 8, 2)
        NIT = 2 * N_EXP + 1
        POS = sb("POS", [P, 2, NIT])
        GT = sb("GT", [P, 2, NIT])
        CNT = sb("CNT", [P, 4])
        NROUND = sb("NROUND", [P, 1], I32)

        def pe_route(pe):
            for x in range(2):
                for k in range(KC):
                    mm = pe.matmul(B(0)[:, 8 * x:8 * x + 8], HT[:, k, 256 + P * x:384 + P * x], ROUT[:, k, :],
                                   start=k == 0, stop=k == KC - 1)
            mm.then_inc(S("r_logits"), 1)
            for x in range(2):
                for k in range(KC):
                    mm = pe.transpose(B(4 + 2 * x + k // 4)[:, P * (k % 4):P * (k % 4) + P],
                                      HT[:, k, 256 + P * x:384 + P * x], ident)
            mm.then_inc(S("r_rows"), 1)
            pe.wait_ge(S("r_sel"), 1)
            one, tri = kc(K_ONE), kc(K_TRI)
            pe.matmul(B(1)[:, 0:8], tri, RT[:, 8, 0, :], start=True, stop=True)
            pe.matmul(B(1)[:, 8:16], one, RT[:, 8, 0, :], start=True, stop=False)
            pe.matmul(B(1)[:, 8:16], tri, RT[:, 8, 1, :], start=False, stop=True)
            pe.matmul(B(1)[:, 16:24], one, RT[:, 8, 0, :], start=True, stop=False)
            pe.matmul(B(1)[:, 16:24], one, RT[:, 8, 1, :], start=False, stop=True).then_inc(S("r_pos"), 1)

        def dve_route(dve):
            step = [0]

            def then(ins):
                step[0] += 1
                ins.then_inc(S("r_step"), 1)
                dve.wait_ge(S("r_step"), step[0])

            dve.wait_ge(S("r_logits"), 1)
            lg, rev = RT[:, 0, :, :], kc(K_REV).rearrange("p (x e) -> p x e", e=8)
            then(dve.tensor_copy(lg, B(0)[:, 0:16].rearrange("p (x e) -> p x e", e=8)))
            for r in range(2):
                then(dve.tensor_reduce(RV[:, r, :], lg, AX.X, ALU.max))
                then(dve.tensor_tensor(RT[:, 1, :, :], lg, bc(RV[:, r, :], 2, 8), ALU.is_equal))
                then(dve.tensor_tensor(RT[:, 2, :, :], RT[:, 1, :, :], rev, ALU.mult))
                then(dve.tensor_reduce(RV[:, 2 + r, :], RT[:, 2, :, :], AX.X, ALU.max))
                then(dve.tensor_tensor(RT[:, 3 + r, :, :], RT[:, 2, :, :], bc(RV[:, 2 + r, :], 2, 8), ALU.is_equal))
                if r == 0:
                    then(dve.scalar_tensor_tensor(out=lg, in0=RT[:, 3, :, :], scalar=-3.0e38, in1=lg,
                                                  op0=ALU.mult, op1=ALU.add))
            then(dve.tensor_tensor(RV[:, 4, :], RV[:, 1, :], RV[:, 0, :], ALU.subtract))
            dve.tensor_tensor(RT[:, 8, :, :], RT[:, 3, :, :], RT[:, 4, :, :], ALU.add).then_inc(S("r_sel"), 1)
            dve.wait_ge(S("r_exp"), 1)
            then(dve.tensor_scalar(RV[:, 6, :], RV[:, 5, :], 1.0, None, ALU.add))
            then(dve.reciprocal(RV[:, 6, :], RV[:, 6, :]))
            then(dve.tensor_tensor(RV[:, 7, :], RV[:, 5, :], RV[:, 6, :], ALU.mult))
            then(dve.tensor_tensor(RT[:, 5, :, :], RT[:, 3, :, :], bc(RV[:, 6, :], 2, 8), ALU.mult))
            then(dve.tensor_tensor(RT[:, 6, :, :], RT[:, 4, :, :], bc(RV[:, 7, :], 2, 8), ALU.mult))
            then(dve.memset(POS[:, :, 2 * N_EXP:NIT], -1.0))
            for c in range(2):
                then(dve.tensor_tensor(GT[:, :, N_EXP * c:N_EXP * c + N_EXP], RT[:, 5, :, :], RT[:, 6, :, :], ALU.add))
            dve.wait_ge(S("r_pos"), 1)
            pos = B(1)[:, 0:16].rearrange("p (x e) -> p x e", e=8)
            then(dve.scalar_tensor_tensor(out=RT[:, 7, :, :], in0=pos, scalar=1.0, in1=RT[:, 8, :, :],
                                          op0=ALU.add, op1=ALU.mult))
            for c in range(2):
                then(dve.tensor_scalar(POS[:, :, N_EXP * c:N_EXP * c + N_EXP], RT[:, 7, :, :], -1.0 - P * c, None, ALU.add))
            then(dve.tensor_reduce(CNT[:, 0:1], B(1)[:, 16:24], AX.X, ALU.max))
            then(dve.tensor_scalar(CNT[:, 1:2], CNT[:, 0:1], float(P), None, ALU.is_gt))
            then(dve.tensor_scalar(CNT[:, 2:3], CNT[:, 1:2], 1.0, None, ALU.add))
            then(dve.tensor_copy(NROUND[:, :], CNT[:, 2:3]))
            dve.wait_ge(S("r_high"), 4)
            for j in range(4):
                x, c = j // 2, slice(512 * (j % 2), 512 * (j % 2) + 512)
                dve.tensor_tensor(XLL[:, x, c], B(4 + j), XLH[:, x, c], ALU.subtract)
            dve.memset(Y, 0.0)
            dve.memset(PT, 0.0)

        def act_route(act):
            act.wait_ge(S("r_sel"), 1)
            act.activation(RV[:, 5, :], RV[:, 4, :], ACT.Exp).then_inc(S("r_exp"), 1)
            act.wait_ge(S("r_rows"), 1)
            for j in range(4):
                act.activation(XLH[:, j // 2, 512 * (j % 2):512 * (j % 2) + 512], B(4 + j),
                               ACT.Copy).then_inc(S("r_high"), 1)

        VB = [6, 7, 0, 1, 2, 3]
        TBK = [4, 5, 6, 7, 0, 1]
        UORD = [0, 1, 4, 5, 2, 3]
        YSEG = []
        for blk in range(2 * FC):
            a, left = 512 * blk, 512
            while left:
                w = min(left, D_FF - a % D_FF)
                YSEG.append((16 + a // D_FF, a % D_FF, blk // 2, blk % 2, 512 - left, w))
                a, left = a + w, left - w
        NEXT_AFTER = 20
        INSERT_U, INSERT_V, INSERT_NEXT, INSERT_ONEHOT = 9, 17, 22, 12

        def rounds(eng, body):
            n = eng.value_load(NROUND[0:1, 0:1], min_val=1, max_val=2)
            with eng.Fori(0, n) as c:
                with eng.Fori(0, N_EXP) as e:
                    body(c * N_EXP + e, e)

        def sp_moe(sp):
            for other in ENG:
                sp.wait_ge(S(f"{other}_stage_done"), MOE_STAGE)

            def body(i, e):
                for q in range(NPIECE):
                    sp.wait_ge(S("m_lo"), NPIECE * i + q + 1)
                    if q < 16:
                        k = q % 8
                        w = t["moe_w1" if q < 8 else "moe_w3"][0, bass.ds(e, 1), P * k:P * k + P, :]
                        src = w.rearrange("a p n -> p (a n)")
                    else:
                        w = t["moe_w2"][0, bass.ds(e, 1), :, :].rearrange("a (p c) n -> p (a c n)", p=P)
                        src = w[:, D_FF * (q - 16):D_FF * (q - 15)]
                    sp.dma_start(RAW[q % NRAW], src).then_inc(S(f"m_raw{q % NRAW}"), 16)
            rounds(sp, body)

        def pe_gather(pe, i):
            pe.wait_ge(S("m_onehot"), 2 * i + 2)
            for k in range(KC):
                for n, (part, x) in enumerate(((XLH, 0), (XLH, 1), (XLL, 0), (XLL, 1))):
                    mm = pe.matmul(B(6 + k // 4)[:, P * (k % 4):P * (k % 4) + P], part[:, x, P * k:P * k + P],
                                   PH[:, x, :], start=n == 0, stop=n == 3)
                if k % 4 == 3:
                    mm.then_inc(S("m_gathered"), 1)

        def pe_scatter(pe, x):
            for h in range(2):
                pe.matmul(B(6 + h), PT[:, x, :], YE[:, 512 * h:512 * h + 512], start=True,
                          stop=True).then_inc(S("m_scattered"), 1)

        def pe_moe_first(pe):
            pe.sem_inc(S("m_used"), 22)
            for h in range(2):
                mm = pe.matmul(B(2 + h)[:, 0:256], PT[:, 0, :], PT.rearrange("p x s -> p (x s)"), start=True, stop=True)
                mm = pe.matmul(B(2 + h)[:, 256:512], PT[:, 0, :], PT.rearrange("p x s -> p (x s)"), start=True, stop=True)
            pe_gather(pe, 0)

        def pe_moe(pe):
            def matrix(i, first, banks, order, done):
                for k in range(KC):
                    q = first + k
                    pe.wait_ge(S("m_lo"), NPIECE * i + q + 1 + NRAW)
                    hi, lo = WHI[q % NSPLIT], WLO[q % NSPLIT]
                    passes = ((HEH, hi), (HEH, lo), (HEL, hi))

                    def product(j, n, a, b):
                        f0, w = FT[j]
                        return pe.matmul(B(banks[j])[:, 0:w], a[:, k, :], b[:, f0:f0 + w], start=k == 0 and n == 0,
                                         stop=k == KC - 1 and n == 2)
                    if k == 0:
                        for j in order:
                            yield j
                            product(j, 0, *passes[0])
                        for n in (1, 2):
                            for j in order:
                                mm = product(j, n, *passes[n])
                        mm.then_inc(S("m_used"), 1)
                    elif k < KC - 1:
                        for n in range(3):
                            for j in order:
                                mm = product(j, n, *passes[n])
                        mm.then_inc(S("m_used"), 1)
                    else:
                        for j in order:
                            for n in range(3):
                                mm = product(j, n, *passes[n])
                            mm.then_inc(S(done), 1)
                    if first == 0 and k in (2, 5):
                        if k == 2:
                            pe.wait_ge(S("m_ye"), 2 * i + 2)
                            pe.wait_ge(S("m_pt"), i + 1)
                        else:
                            pe.wait_ge(S("m_added"), 4 * i + 2)
                        pe_scatter(pe, (k - 2) // 3)

            def body(i, e):
                pe.wait_ge(S("m_he_lo"), 2 * i + 2)
                pe.wait_ge(S("m_pt"), i + 1)
                for j in matrix(i, 0, range(6), UORD, "m_u_full"):
                    if j == 2:
                        pe.wait_ge(S("m_ye"), 2 * i + 2)
                for j in matrix(i, 8, VB, range(6), "m_v_full"):
                    if j == 0:
                        pe.wait_ge(S("m_added"), 4 * i + 4)
                    elif j >= 2:
                        pe.wait_ge(S("m_u"), 6 * i + UORD.index(VB[j]) + 1)
                pe.wait_ge(S("m_u"), 6 * i + 6)
                pe.wait_ge(S("m_hidden"), 6 * i + 6)
                turned = UA.rearrange("p (f c) -> p c f", c=FC)
                for g in range(6):
                    for c in range(4 * g, min(4 * g + 4, FC)):
                        mm = pe.transpose(B(TBK[g])[:, P * (c % 4):P * (c % 4) + P], turned[:, c, :], ident)
                    mm.then_inc(S("m_turned"), 1)
                pe.wait_ge(S("m_ae_lo"), 6 * i + 1)
                pe.wait_ge(S("m_gated"), 2 * i + 2)
                for x in range(2):
                    mm = pe.transpose(B(4)[:, P * x:P * x + P], PG[:, x, :], ident)
                mm.then_inc(S("m_gt"), 1)
                for q in range(16, NPIECE):
                    pe.wait_ge(S("m_lo"), NPIECE * i + q + 1 + NRAW)
                    segs = [g for g in YSEG if g[0] == q]
                    hi, lo = WHI[q % NSPLIT], WLO[q % NSPLIT]
                    pe.wait_ge(S("m_ae_lo"), 6 * i + segs[-1][2] // 4 + 1)
                    for _, a, c, h, o, w in segs:
                        for n, (x, y) in enumerate(((AEH, hi), (AEH, lo), (AEL, hi))):
                            mm = pe.matmul(B(2 + h)[:, o:o + w], x[:, c, :], y[:, a:a + w], start=c == 0 and n == 0,
                                           stop=c == FC - 1 and n == 2)
                    mm.then_inc(S("m_used"), 1)
                    if q == NEXT_AFTER:
                        pe.wait_ge(S("m_ae_lo"), 6 * i + 6)
                        pe_gather(pe, i + 1)
            rounds(pe, body)

        def act_tokens(act, i):
            for h in range(2):
                act.wait_ge(S("m_gathered"), 2 * i + h + 1)
                act.activation(HEH[:, 4 * h:4 * h + 4, :], B(6 + h).rearrange("p (k s) -> p k s", s=P),
                               ACT.Copy).then_inc(S("m_he_hi"), 1)

        def dve_tokens(dve, i):
            for h in range(2):
                dve.wait_ge(S("m_he_hi"), 2 * i + h + 1)
                dve.tensor_tensor(HEL[:, 4 * h:4 * h + 4, :], B(6 + h).rearrange("p (k s) -> p k s", s=P),
                                  HEH[:, 4 * h:4 * h + 4, :], ALU.subtract).then_inc(S("m_he_lo"), 1)

        def dve_onehot(dve, i):
            for x in range(2):
                dve.tensor_scalar(PH[:, x, :], kc(K_IOTA), POS[:, x, bass.ds(i, 1)], None,
                                  ALU.is_equal).then_inc(S("m_onehot"), 1)

        def act_output(act):
            for h in range(2):
                act.activation(YE[:, 512 * h:512 * h + 512], B(2 + h), ACT.Copy).then_inc(S("m_ye"), 1)

        def dve_add(dve, x, count):
            for h in range(2):
                dve.wait_ge(S("m_scattered"), count + h + 1)
                v = Y[:, x, 512 * h:512 * h + 512]
                dve.tensor_tensor(v, B(6 + h), v, ALU.add).then_inc(S("m_added"), 1)

        def act_moe(act):
            def body(i, e):
                for q in range(NPIECE):
                    act.wait_ge(S(f"m_raw{q % NRAW}"), 16 * (6 * i + q // NRAW + 1))
                    if q < 8:
                        act.wait_ge(S("m_used"), 22 * i + 15 + q)
                    elif q == 15:
                        act.wait_ge(S("m_u_full"), 6 * i + 6)
                    elif q == 23:
                        act.wait_ge(S("m_v_full"), 6 * i + 6)
                    else:
                        act.wait_ge(S("m_used"), 22 * i + 22 + q - 7 - (q > 15))
                    act.activation(WHI[q % NSPLIT], RAW[q % NRAW], ACT.Copy).then_inc(S("m_hi"), 1)
                    if q == 0:
                        act.wait_ge(S("m_used"), 22 * i + 22)
                        act_output(act)
                    if q == INSERT_U:
                        for n, j in enumerate(UORD):
                            f0, w = FT[j]
                            act.wait_ge(S("m_u_full"), 6 * i + n + 1)
                            act.activation(UA[:, f0:f0 + w], B(j)[:, 0:w], ACT.Silu).then_inc(S("m_u"), 1)
                    if q == INSERT_V:
                        for g in range(6):
                            n = min(4, FC - 4 * g)
                            act.wait_ge(S("m_turned"), 6 * i + g + 1)
                            act.activation(AEH[:, 4 * g:4 * g + n, :], B(TBK[g])[:, 0:n * P].rearrange(
                                "p (a b) -> p a b", b=P), ACT.Copy).then_inc(S("m_ae_hi"), 1)
                    if q == INSERT_NEXT:
                        act_tokens(act, i + 1)
            rounds(act, body)
            act.drain()
            n = act.value_load(NROUND[0:1, 0:1], min_val=1, max_val=2)
            act.wait_ge(S("m_used"), n * (22 * N_EXP) + 22)
            act_output(act)

        def dve_moe(dve):
            def body(i, e):
                for q in range(NPIECE):
                    dve.wait_ge(S("m_hi"), NPIECE * i + q + 1)
                    dve.tensor_tensor(WLO[q % NSPLIT], RAW[q % NRAW], WHI[q % NSPLIT],
                                      ALU.subtract).then_inc(S("m_lo"), 1)
                    if q == 3:
                        dve_add(dve, 0, 4 * i)
                    if q == 6:
                        dve_add(dve, 1, 4 * i + 2)
                    if q == INSERT_ONEHOT:
                        dve_onehot(dve, i + 1)
                        for x in range(2):
                            dve.tensor_scalar(PG[:, x, :], kc(K_IOTA), POS[:, x, bass.ds(i, 1)], GT[:, x, bass.ds(i, 1)],
                                              ALU.is_equal, ALU.mult).then_inc(S("m_gated"), 1)
                        dve.wait_ge(S("m_added"), 4 * i + 4)
                    if q == INSERT_V:
                        for j, (f0, w) in enumerate(FT):
                            dve.wait_ge(S("m_v_full"), 6 * i + j + 1)
                            dve.wait_ge(S("m_u"), 6 * i + UORD.index(j) + 1)
                            dve.tensor_tensor(UA[:, f0:f0 + w], B(VB[j])[:, 0:w], UA[:, f0:f0 + w],
                                              ALU.mult).then_inc(S("m_hidden"), 1)
                        for g in range(6):
                            n = min(4, FC - 4 * g)
                            dve.wait_ge(S("m_ae_hi"), 6 * i + g + 1)
                            dve.tensor_tensor(AEL[:, 4 * g:4 * g + n, :], B(TBK[g])[:, 0:n * P].rearrange(
                                "p (a b) -> p a b", b=P), AEH[:, 4 * g:4 * g + n, :], ALU.subtract).then_inc(S("m_ae_lo"), 1)
                        dve.wait_ge(S("m_gt"), i + 1)
                        dve.tensor_copy(PT, B(4)[:, 0:256].rearrange("p (a b) -> p a b", b=P)).then_inc(S("m_pt"), 1)
                    if q == INSERT_NEXT:
                        dve_tokens(dve, i + 1)
            rounds(dve, body)

        def pe_moe_last(pe):
            for x in range(2):
                for h in range(2):
                    pe.matmul(B(4 + 2 * x + h), PT[:, x, :], YE[:, 512 * h:512 * h + 512], start=True, stop=True)

        def dve_moe_last(dve):
            for j in range(4):
                v = Y[:, j // 2, 512 * (j % 2):512 * (j % 2) + 512]
                dve.tensor_tensor(v, B(4 + j), v, ALU.add).then_inc(S("y_added"), 1)
            dve.wait_ge(S("y_added"), 4)

        def dve_last(dve):
            dve.tensor_tensor(Y, Y, GATE[:, 1, 1:2, :].to_broadcast([P, 2, D]), ALU.mult).then_inc(S("y_gated"), 1)
            dve.wait_ge(S("y_gated"), 1)
            dve.tensor_tensor(X[:, 2:4, :], X[:, 2:4, :], Y, ALU.add).then_inc(S("x_done"), 1)

        SMALL = [(K[:, :], t["consts"]), (MASKF, t["masks"]),
                 (X[:, 0:2, :], t["ctx"][0].rearrange("(a p) n -> p a n", p=P)),
                 (X[:, 2:4, :], t["x"][0].rearrange("(a p) n -> p a n", p=P)),
                 (CIN[:, :, 0:1], t["c_ctx"].rearrange("(k p a) -> p k a", p=P, a=1)),
                 (CIN[:, :, 1:2], t["c"].rearrange("a (k p) -> p k a", p=P)),
                 (ROUT[:, :, :], t["moe_router"][0].rearrange("(k p) e -> p k e", p=P)),
                 (QKG[:, :, :, :], t["diff_qk_norm_g"].partition_broadcast(P)),
                 (LAMV[:, :, :, :], t["diff_lambda"].partition_broadcast(P)),
                 (SUBG[:, :, :], t["diff_subln_g"].partition_broadcast(P)),
                 (HNG[:, :, :], t["hgrn_norm_g"].partition_broadcast(P)),
                 (SQKG[:, :, :, :], t["swa_qk_norm_g"].partition_broadcast(P)),
                 (SINK[:, :, :], t["swa_sink"].partition_broadcast(P))]
        for L in range(DEPTH):
            SMALL.append((GMIX[:, L, :].unsqueeze(2), t["norm_mix_g"][L].rearrange("(k p a) -> p k a", p=P, a=1)))
            SMALL.append((GFFN[:, L, :].unsqueeze(2), t["norm_ffn_g"][L].rearrange("(k p a) -> p k a", p=P, a=1)))
            for d in range(2):
                SMALL.append((LBL[:, d, L, :].unsqueeze(2),
                              t["hgrn_lb_logits"][d, L].rearrange("(k p a) -> p k a", p=P, a=1)))

        def dve_setup(dve):
            step = [0]

            def then(ins):
                step[0] += 1
                ins.then_inc(S("setup_step"), 1)
                dve.wait_ge(S("setup_step"), step[0])

            then(dve.memset(NEGH[:, :], -0.5))
            dve.wait_ge(S("small_loaded"), 16 * len(SMALL))
            then(dve.tensor_copy(M8.rearrange("p a b c -> p (a b c)"), MASKF))
            then(dve.tensor_scalar(NSINK[:, :, :], SINK[:, :, :], -1.0, None, ALU.mult))
            l0, l1 = LBL[:, :, 0, :], LBL[:, :, 1, :]
            then(dve.tensor_tensor(LBT[:, 0, :, :], l0, l1, ALU.max))
            then(dve.tensor_tensor(LBT[:, 1, :, :], l0, LBT[:, 0, :, :], ALU.subtract))
            dve.tensor_tensor(LBT[:, 2, :, :], l1, LBT[:, 0, :, :], ALU.subtract).then_inc(S("lb_ready"), 1)
            for L in range(DEPTH):
                for j in range(2):
                    then(dve.tensor_tensor(LAMV[:, L, 2 * j, :], LAMV[:, L, 2 * j, :], LAMV[:, L, 2 * j + 1, :], ALU.mult))
                    then(dve.tensor_reduce(LAM[:, L, j:j + 1], LAMV[:, L, 2 * j, :], AX.X, ALU.add))
            dve.sem_inc(S("lam_ready"), 1)
            dve.wait_ge(S("setup_exp"), 1)
            then(dve.tensor_tensor(LBT[:, 3, :, :], LBT[:, 1, :, :], LBT[:, 2, :, :], ALU.add))
            then(dve.reciprocal(LBT[:, 3, :, :], LBT[:, 3, :, :]))
            then(dve.tensor_tensor(LBT[:, 1, :, :], LBT[:, 1, :, :], LBT[:, 3, :, :], ALU.mult))
            then(dve.tensor_tensor(LBT[:, 2, :, :], LBT[:, 2, :, :], LBT[:, 3, :, :], ALU.mult))
            then(dve.tensor_tensor(LBT[:, 2, :, :], LBT[:, 2, :, :], LBT[:, 1, :, :], ALU.add))
            then(dve.tensor_tensor(LBT[:, 4, :, :], LBT[:, 2, :, :], LBT[:, 1, :, :], ALU.subtract))
            then(dve.tensor_scalar(LBT[:, 5, :, :], LBT[:, 4, :, :], -1.0, 1.0, ALU.mult, ALU.add))
            for L in range(DEPTH):
                lam_init = 0.8 - 0.6 * math.exp(-0.3 * L)
                then(dve.tensor_tensor(LAM[:, L, 4:5], LAM[:, L, 3:4], LAM[:, L, 2:3], ALU.subtract))
                then(dve.tensor_scalar(LAM[:, L, 5:6], LAM[:, L, 4:5], -lam_init, None, ALU.add))

        def act_setup(act):
            act.wait_ge(S("small_loaded"), 16 * len(SMALL))
            act.activation(SC[:, :, :], CIN[:, :, :], ACT.Silu)
            act.wait_ge(S("lb_ready"), 1)
            act.wait_ge(S("lam_ready"), 1)
            act.activation(LAM[:, :, 2:4], LAM[:, :, 0:2], ACT.Exp)
            act.activation(LBT[:, 1:3, :, :], LBT[:, 1:3, :, :], ACT.Exp).then_inc(S("setup_exp"), 1)

        def ADA_STAGE(L):
            return 1 + 9 * L

        MOE_STAGE = 1 + 9 * DEPTH

        @block.sync
        def _(sp):
            for dst, src in SMALL:
                sp.dma_start(dst, src, allow_slow_non_contiguous=True).then_inc(S("small_loaded"), 16)
            for n, (pieces, _) in enumerate(plan):
                key = next(k for k, v in index.items() if v == n)
                if key[0] == "ada" and key[2] == 0:
                    L = key[1]
                    for other in ENG:
                        sp.wait_ge(S(f"{other}_stage_done"), ADA_STAGE(L))
                    sp.dma_start(ADAB[0:12, :], t["ada_b"][L].rearrange("(a n) -> a n", n=512)).then_inc(
                        S("adab_loaded"), 16)
                if n >= 2:
                    sp.wait_ge(S(plan[n - 2][1][0]), plan[n - 2][1][1])
                for where, src in pieces:
                    if where is None:
                        rows = min(4, FC - 4 * src)
                        dst = RING[n % 2].rearrange("p k n -> p (k n)")[:, 0:rows * D].rearrange("p (c n) -> p c n", n=D)
                        w = t["ffn_w2"][0][4 * P * src:4 * P * src + rows * P, :].rearrange("(c p) n -> p c n", p=P)
                    else:
                        dst, w = RING[n % 2][:, :, where], src
                    sp.dma_start(dst, w).then_inc(S(f"ring_full{n % 2}"), 16)
            sp_moe(sp)
            sp.wait_ge(S("x_done"), 1)
            sp.dma_start(t["out"][0].rearrange("(a p) n -> p a n", p=P), X[:, 2:4, :]).then_inc(S("stored"), 16)
            sp.wait_ge(S("stored"), 16)

        @block.tensor
        def _(pe):
            stage_end(pe, "pe")
            for L in range(DEPTH):
                for stage in (pe_ada, lambda e, l: pe_norm(e, l, 0), pe_mix_in, pe_states, pe_qkt,
                              pe_att, None, pe_out):
                    if stage:
                        stage(pe, L)
                    stage_end(pe, "pe")
                pe_norm(pe, L, 1)
                if L == 0:
                    pe.wait_ge(S("norm_ht_act"), 16)
                    pe.wait_ge(S("norm_ht_dve"), 16)
                    pe_ffn(pe)
                else:
                    pe.wait_ge(S("norm_ht_act"), 28)
                    pe.wait_ge(S("norm_ht_dve"), 28)
                    pe_route(pe)
                stage_end(pe, "pe")
            pe_moe_first(pe)
            stage_end(pe, "pe")
            pe_moe(pe)
            stage_end(pe, "pe")
            pe_moe_last(pe)
            stage_end(pe, "pe")

        @block.scalar
        def _(act):
            act_setup(act)
            stage_end(act, "act")
            for L in range(DEPTH):
                for stage in (act_ada, lambda e, l: act_norm(e, l, 0), act_proj, act_states, act_qkt,
                              act_att, None, act_out):
                    if stage:
                        stage(act, L)
                    stage_end(act, "act")
                act_norm(act, L, 1)
                if L == 0:
                    act_ffn(act)
                else:
                    act_route(act)
                stage_end(act, "act")
            act_tokens(act, 0)
            stage_end(act, "act")
            act_moe(act)
            stage_end(act, "act")
            stage_end(act, "act")

        @block.gpsimd
        def _(pool):
            stage_end(pool, "pool")
            for L in range(DEPTH):
                for stage in (None, lambda e, l: pool_norm(e, l, 0), pool_mix_in, None,
                              lambda e, l: pool_post(e, l, "hp", 128), None, lambda e, l: pool_post(e, l, "dp", 64), None):
                    if stage:
                        stage(pool, L)
                    stage_end(pool, "pool")
                pool_norm(pool, L, 1)
                stage_end(pool, "pool")
            for _ in range(3):
                stage_end(pool, "pool")

        @block.vector
        def _(dve):
            dve_setup(dve)
            stage_end(dve, "dve")
            for L in range(DEPTH):
                lam_init = 0.8 - 0.6 * math.exp(-0.3 * L)
                dve_ada(dve, L)
                stage_end(dve, "dve")
                dve_norm(dve, L, 0)
                stage_end(dve, "dve")
                dve_proj(dve, L, ("aqk", "c"))
                dve_qk(dve, L)
                dve_proj(dve, L, ("bi",))
                hgrn_gates(dve, L, 0)
                dve_proj(dve, L, ("av",))
                dve_levels(dve, L)
                stage_end(dve, "dve")
                dve_states(dve, L)
                stage_end(dve, "dve")
                dve_qkt(dve, L)
                dve_post(dve, L, "hp", 256, 128, HNG[:, L, :], None)
                stage_end(dve, "dve")
                dve_att(dve, L)
                stage_end(dve, "dve")
                dve_post(dve, L, "dp", 0, 64, SUBG[:, L, :], 1.0 - lam_init)
                stage_end(dve, "dve")
                dve_out(dve, L)
                stage_end(dve, "dve")
                dve_norm(dve, L, 1)
                if L == 0:
                    dve_ffn(dve)
                else:
                    dve_route(dve)
                stage_end(dve, "dve")
            dve.sem_inc(S("m_lo"), NRAW)
            dve.sem_inc(S("m_pt"), 1)
            dve_onehot(dve, 0)
            dve_tokens(dve, 0)
            stage_end(dve, "dve")
            dve_moe(dve)
            stage_end(dve, "dve")
            stage_end(dve, "dve")
            dve_moe_last(dve)
            dve_last(dve)


_INS = ['x', 'c', 'ctx', 'c_ctx', 'ada_w', 'ada_b', 'norm_mix_g', 'norm_ffn_g', 'w_in', 'w_out',
        'diff_qk_norm_g', 'diff_lambda', 'diff_subln_g', 'hgrn_lb_logits', 'hgrn_norm_g',
        'swa_qk_norm_g', 'swa_sink', 'ffn_w1', 'ffn_w3', 'ffn_w2', 'moe_router', 'moe_w1', 'moe_w3', 'moe_w2']


def kernel(**inputs):
    import concourse.bacc as bacc
    from concourse.bass_utils import run_bass_kernel_spmd

    nc = bacc.Bacc("TRN2", target_bir_lowering=False, num_devices=1)
    arrays, t = {}, {}
    k, masks = constants()
    for name, a in [(n, inputs[n]) for n in _INS] + [("consts", k), ("masks", masks)]:
        a = np.ascontiguousarray(a)
        arrays["in_" + name] = a
        t[name] = nc.dram_tensor("in_" + name, a.shape, mybir.dt.from_np(a.dtype), kind="ExternalInput").ap()
    t["out"] = nc.dram_tensor("out_x", (1, 256, D), F32, kind="ExternalOutput").ap()
    trunk(nc, t)
    r = run_bass_kernel_spmd(nc, [arrays], core_ids=[0])
    return r.results[0]["out_x"]
```

```python
from contextlib import ExitStack
import math

import numpy as np
import concourse.bass as bass
import concourse.mybir as mybir

F32 = mybir.dt.float32
U8 = mybir.dt.uint8
BF16 = mybir.dt.bfloat16
I32 = mybir.dt.int32
ALU = mybir.AluOpType
ACT = mybir.ActivationFunctionType
AX = mybir.AxisListType

P = 128
D = 1024
KC = D // P
NT = 4
CTX_TILES, LAT_TILES = (0, 1), (2, 3)
DEPTH = 2
D_IN = 3840
D_FF = 2816
FC = D_FF // P
N_EXP = 8
EPS = 1e-6
GRID_W = 64
WINDOW = 128
NH = 4
C_AQK, C_AV, C_BQ, C_BI, C_BFF, C_BFB, C_BG, C_C = 0, 512, 768, 1280, 1792, 2304, 2816, 3328
LEVELS = [1, 2, 4, 8, 16, 32, 64]
FT = [(0, 512), (512, 512), (1024, 512), (1536, 512), (2048, 512), (2560, 256)]

K_ID, K_TRI, K_ONE, K_IOTA, K_C32, K_S32, K_C64, K_S64, K_SWA, K_REV, K_SELT, K_E12 = range(12)
K_WIDTH = {K_ID: 128, K_TRI: 128, K_ONE: 128, K_IOTA: 128, K_C32: 64, K_S32: 64, K_C64: 128,
           K_S64: 128, K_SWA: 256, K_REV: 16, K_SELT: 256, K_E12: 24}
K_AT = {k: sum(K_WIDTH[j] for j in range(k)) for k in K_WIDTH}
K_ALL = sum(K_WIDTH.values())


def constants():
    k = np.zeros((P, K_ALL), np.float32)

    def put(name, a):
        a = np.asarray(a, np.float32)
        k[:a.shape[0], K_AT[name]:K_AT[name] + a.shape[1]] = a

    i = np.arange(P)
    put(K_ID, np.eye(P))
    put(K_TRI, i[:, None] < i[None, :])
    put(K_ONE, np.ones((P, P)))
    put(K_IOTA, np.broadcast_to(i, (P, P)))
    tok = np.arange(2 * P)
    row, col = tok // GRID_W, tok % GRID_W
    for dim, kc, ks in ((32, K_C32, K_S32), (64, K_C64, K_S64)):
        nf = dim // 4
        inv = (np.float32(10000.0) ** (-np.arange(nf, dtype=np.float32) / np.float32(nf))).astype(np.float32)
        c, s = np.zeros((2 * P, dim)), np.zeros((2 * P, dim))
        for half, pos in enumerate((row, col)):
            ang = (pos.astype(np.float32)[:, None] * inv[None, :]).astype(np.float32).astype(np.float64)
            a = half * 2 * nf
            c[:, a:a + nf] = c[:, a + nf:a + 2 * nf] = np.cos(ang)
            s[:, a:a + nf] = -np.sin(ang)
            s[:, a + nf:a + 2 * nf] = np.sin(ang)
        put(kc, c.reshape(2, P, dim).transpose(1, 0, 2).reshape(P, 2 * dim))
        put(ks, s.reshape(2, P, dim).transpose(1, 0, 2).reshape(P, 2 * dim))
    swa = np.zeros((P, 2, P), np.float32)
    for b in range(2):
        swa[:, b] = np.where(np.abs((b * P + i)[:, None] - ((1 - b) * P + i)[None, :]) <= WINDOW, 0.0, -1e30)
    put(K_SWA, swa.reshape(P, -1))
    put(K_REV, np.broadcast_to(np.tile(8.0 - np.arange(8), 2), (P, 16)))
    sel = np.zeros((2, 2, P))
    sel[0, 0] = sel[1, 1] = 1
    put(K_SELT, sel.reshape(2, -1))
    e12 = np.zeros((12, 12, 2))
    e12[np.arange(12), np.arange(12)] = 1
    put(K_E12, e12.reshape(12, -1))
    m8 = np.zeros((P, 2, len(LEVELS), P), np.float32)
    s, t = i[:, None], i[None, :]
    for n, m in enumerate(LEVELS):
        same = s // (2 * m) == t // (2 * m)
        m8[:, 0, n] = same & (s % (2 * m) < m) & (t % (2 * m) >= m)
        m8[:, 1, n] = same & (s % (2 * m) >= m) & (t % (2 * m) < m)
    return k, m8.reshape(P, -1)


def bc(ap, axis, n):
    ap = ap.unsqueeze(axis)
    shape = list(ap.shape)
    shape[axis] = n
    return ap.to_broadcast(shape)


def trunk(nc, t):
    ctx = ExitStack()
    with ctx:
        def sb(name, shape, dt=F32):
            return ctx.enter_context(nc.sbuf_tensor(name, shape, dt))

        sems = {}

        def S(name):
            if name not in sems:
                sems[name] = ctx.enter_context(nc.semaphore(name))
            return sems[name]

        X = sb("X", [P, NT, D])
        GATE = sb("GATE", [P, 2, 2, D])
        K = sb("K", [P, K_ALL])
        M8 = sb("M8", [P, 2, len(LEVELS), P], U8)
        ARENA = sb("ARENA", [P, 161 * 256])
        MT = sb("MT", [P, DEPTH, 6, KC, 2])
        SC = sb("SC", [P, KC, 2])
        CIN = sb("CIN", [P, KC, 2])
        GMIX = sb("GMIX", [P, DEPTH, KC])
        GFFN = sb("GFFN", [P, DEPTH, KC])
        QKG = sb("QKG", [P, DEPTH, 2, 32])
        SUBG = sb("SUBG", [P, DEPTH, 64])
        HNG = sb("HNG", [P, DEPTH, 128])
        SQKG = sb("SQKG", [P, DEPTH, 2, 64])
        SINK = sb("SINK", [P, DEPTH, NH])
        NSINK = sb("NSINK", [P, DEPTH, NH])
        LBL = sb("LBL", [P, 2, DEPTH, NH])
        LBT = sb("LBT", [P, 6, 2, NH])
        LAM = sb("LAM", [P, DEPTH, 6])
        ROUT = sb("ROUT", [P, KC, N_EXP])
        NEGH = sb("NEGH", [P, 64])
        STAT = sb("STAT", [P, 4, 96])
        PS = ctx.enter_context(nc.psum_tensor("PS", [P, 8, 512], F32))

        def B(i):
            return PS[:, i, :]

        def kc(name, w=None):
            return K[:, K_AT[name]:K_AT[name] + (w or K_WIDTH[name])]

        ident = kc(K_ID)

        def A(at, *shape):
            n = int(np.prod(shape))
            a = int(at * 256)
            v = ARENA[:, a:a + n]
            names = "abcde"[:len(shape)]
            if len(shape) == 1:
                return v
            return v.rearrange(f"p ({' '.join(names)}) -> p {' '.join(names)}", **dict(zip(names[1:], shape[1:])))

        ST = [A(0, NH, 512), A(8, NH, 512)]
        Q = A(16, NH, 512)
        QP = [A(24, NH, 512), A(32, NH, 512)]
        KE = [A(40, NH, 512), A(48, NH, 512)]
        FG = [A(56, NH, 512), A(64, NH, 512)]
        TB = [A(108, 1024), A(112, 1024)]
        SST = A(56, 3, 2, NH, P)
        KDT = A(68, 2, NH, P)
        V = A(72, NT, 512)
        G = A(80, NT, 512)
        AQK = A(88, NT, 512)
        AV = A(96, NT, 256)
        CQKV = A(100, NT, 512)
        MIX = A(108, NT, D)
        XN = A(24, NT, D)
        HT = A(0, KC, 512)
        TMP = A(108, NT, 512)
        TMP2 = A(116, NT, 512)
        QKT = A(0, 4, 512)
        CT = A(8, 3, 512)
        EX = A(24, 4, 2, 512)
        AT = A(40, 2, 512)
        MSK = A(44, 2, 512)
        OT = A(48, NT, 512)
        AST = A(56, 6, 32, 2)
        LAMV = A(0, DEPTH, 4, 32)
        MASKF = A(60, 2 * len(LEVELS) * P)
        YT = A(24, 2, 512)
        ADAB = A(101, 512)
        MROW = A(103, 2, 512)

        def parts(at, kib, *shape):
            v = ARENA[:, 256 * at:256 * (at + kib)].bitcast(BF16).rearrange(
                "p (h a b) -> p h a b", h=2, b=shape[-1])
            return v[:, 0], v[:, 1]

        ACTH, ACTL = parts(16, 44, FC, 512)
        HTH, HTL = parts(113, 16, KC, 512)
        MTH, MTL = parts(0, 16, KC, 512)
        WSPLIT = [parts(61 + 16 * i, 16, KC, 512) for i in range(2)]
        HSPLIT = [parts(145 + 8 * i, 8, KC // 2, 512) for i in range(2)]
        UT = A(93, 4, 512)
        FTMP = A(61, 8, 512)

        in_layer0 = {
            "adab_loaded": 16, "ada_mm": 12, "ada_row": 12, "ada_spread": 12, "ada_cp": 12,
            "proj_mm": 8 * NT, "proj_act": 4 * NT, "proj_dve": 4 * NT,
            "qk_sq": 2, "qk_ss": 2, "qk_ms": 2, "qk_rstd": 2, "qk_x": 1 + NT, "qk_gained": 4, "qk_turned": 12,
            "qk_rotated": 4,
            "s_kt": 6, "s_kd": 6, "s_kv": 6, "s_st": 6 * NH, "s_o": NT, "t_tp": 7,
            "a_msk": 2 * 2 * NH, "o_gated": 2 * NT,
            "o_added": 2 * NT, "out_mm": 2 * NT}
        for d in range(2):
            in_layer0.update({f"h{d}_f": 0, f"h{d}_qp": 1, f"h{d}_mm": 1 + len(LEVELS), f"h{d}_taken": 1 + len(LEVELS),
                              f"h{d}_upd": 3 * len(LEVELS)})
        for step in ("s", "mx", "nb", "exp", "r", "ratio", "p", "pt", "at", "pv", "o"):
            in_layer0["a_" + step] = 2 * NH * NT

        def since(L, name):
            return L * in_layer0[name]

        RAW_AT = {"R0": A(129, KC, 512), "R1": A(145, KC, 512), "E0": A(0, KC, 512), "E1": A(16, KC, 512),
                  "H0": A(129, KC // 2, 512), "H1": A(137, KC // 2, 512)}
        BLOCKS = {"R0": (0, 1), "R1": (2, 3), "E0": (4,), "E1": (5,), "H0": (0,), "H1": (1,)}
        free = {}
        loads = {place: 0 for place in RAW_AT}
        slot_users = {"W": [], "H": []}
        items = {}

        def rows_of(v):
            return v.rearrange("p k n -> p (k n)").rearrange("p (c n) -> p c n", n=D)

        def item(key, place, pieces, used, split=False, part=lambda v: v):
            loads[place] += 16 * len(pieces)
            it = dict(place=place, full=loads[place], raw=part(RAW_AT[place]),
                      place_free=sorted({free[b] for b in BLOCKS[place] if b in free}),
                      loads=[(RAW_AT[place][:, :, where] if where else rows_of(part(RAW_AT[place])), src)
                             for where, src in pieces])
            items[key] = it
            for b in BLOCKS[place]:
                free[b] = used
            if split:
                kind = "H" if place[0] == "H" else "W"
                users = slot_users[kind]
                hi, lo = (HSPLIT if kind == "H" else WSPLIT)[len(users) % 2]
                it["number"] = len(slot_users["H"]) + len(slot_users["W"]) + 1
                it["hi"], it["lo"] = part(hi), part(lo)
                it["slot_free"] = users[-2] if len(users) >= 2 else None
                for b in BLOCKS[place]:
                    free[b] = ("split_lo", it["number"])
                if kind == "H":
                    free[2 + len(users) % 2] = used
                users.append(used)

        def cols(w, a, n):
            return w.rearrange("(k p) n -> p k n", p=P)[:, :, a:a + n]

        def proj_units(L):
            out = []
            lat = LAT_TILES if L == DEPTH - 1 else range(NT)
            for key, kind, c0, w, eng in (
                    ("bff", "T", C_BFF, 512, "act"), ("aqk", "N", C_AQK, 512, "dve"),
                    ("bfb", "T", C_BFB, 512, "act"), ("c", "N", C_C, 512, "dve"),
                    ("bq", "T", C_BQ, 512, "act"), ("bi", "N", C_BI, 512, "dve"),
                    ("bg", "N", C_BG, 512, "act"), ("av", "N", C_AV, 256, "dve")):
                for u in (lat if key == "bg" else range(4)):
                    out.append((key, u, kind, c0, w, eng))
            return out

        def ada_item(L, j, place):
            item(("ada", L, j), place, [(slice(0, 512), cols(t["ada_w"][L], 512 * j, 512))], ("ada_mm", 12 * L + j + 1))

        FFN_ITEMS = []
        for n in range(len(FT)):
            FFN_ITEMS += [("w1", n), ("ada", 1, 2 * n), ("w3", n), ("ada", 1, 2 * n + 1)]
        FFN_ITEMS += [("w2", n) for n in range(6)]
        SPLIT_ITEMS = [key for key in FFN_ITEMS if key[0] != "ada"]
        FFN_LOADS = [SPLIT_ITEMS[0], ("ada", 1, 0), SPLIT_ITEMS[1]]
        for j in range(1, 12):
            FFN_LOADS += [SPLIT_ITEMS[j + 1], ("ada", 1, j)]
        FFN_LOADS += SPLIT_ITEMS[13:]

        for L in range(DEPTH):
            if L == 0:
                for j in range(12):
                    ada_item(0, j, ("R0", "R1", "E0", "E1")[j % 4])
            units = proj_units(L)
            for g, key in enumerate(dict.fromkeys(u[0] for u in units)):
                c0, w = next((u[3], u[4]) for u in units if u[0] == key)
                last = max(i for i, u in enumerate(units) if u[0] == key)
                if key == "c":
                    pieces = [(slice(64 * n, 64 * n + 64), cols(t["w_in"][L], C_C + 64 * h, 64))
                              for n, h in enumerate((0, 2, 1, 3))]
                    pieces.append((slice(256, 512), cols(t["w_in"][L], C_C + 256, 256)))
                else:
                    pieces = [(slice(0, w), cols(t["w_in"][L], c0, w))]
                item((key, L), f"R{g % 2}", pieces, ("proj_mm", since(L, "proj_mm") + last + 1))
            n_out = NT if L == 0 else 2
            for h in range(2):
                for half in range(2):
                    item(("out", L, h, half), f"H{half}",
                         [(slice(0, 512), cols(t["w_out"][L], 512 * h, 512)[:, 4 * half:4 * half + 4, :])],
                         ("out_half", 2 * L + h + 1) if half == 0 else ("out_mm", since(L, "out_mm") + n_out * (h + 1)),
                         split=True)
            if L == 0:
                for key in FFN_LOADS:
                    n = key[-1]
                    place = {"w1": "R0", "w3": "R0", "ada": "R1", "w2": f"R{n % 2}"}[key[0]]
                    if key[0] == "ada":
                        ada_item(1, n, place)
                    elif key[0] == "w2":
                        rows = min(4 * P, D_FF - 4 * P * n)
                        src = t["ffn_w2"][0][4 * P * n:4 * P * n + rows, :].rearrange("(c p) n -> p c n", p=P)
                        item(key, place, [(None, src)], ("ffn_y_mm", n + 1), split=True,
                             part=lambda v, r=rows // P: v[:, 0:2 * r, :])
                    else:
                        f0, w = FT[n]
                        item(key, place, [(slice(0, w), cols(t["ffn_" + key[0]][0], f0, w))],
                             ("ffn_u_mm" if key[0] == "w1" else "ffn_v_mm", 4 * n + w // P),
                             split=True, part=lambda v, w=w: v[:, :, 0:w])

        def raw_full(eng, key):
            it = items[key]
            eng.wait_ge(S(f"ring_full_{it['place']}"), it["full"])
            return it["raw"]

        def act_split(act, key):
            it, raw = items[key], raw_full(act, key)
            if it["slot_free"]:
                act.wait_ge(S(it["slot_free"][0]), it["slot_free"][1])
            act.activation(it["hi"], raw, ACT.Copy).then_inc(S("split_hi"), 1)

        def dve_split(dve, key):
            it = items[key]
            dve.wait_ge(S("split_hi"), it["number"])
            dve.tensor_tensor(it["lo"], it["raw"], it["hi"], ALU.subtract).then_inc(S("split_lo"), 1)

        def pe_parts(pe, key):
            it = items[key]
            pe.wait_ge(S("split_lo"), it["number"])
            return it["hi"], it["lo"]

        def gate(L, which, r):
            return GATE[:, which, r, :] if L == 0 else GATE[:, 0, 1 - which, :]

        ENG = ("pe", "act", "dve", "pool")
        stage_count = {e: 0 for e in ENG}

        def stage_end(eng, me):
            eng.drain().then_inc(S(f"{me}_stage_done"), 1)
            stage_count[me] += 1
            for other in ENG:
                if other != me:
                    eng.wait_ge(S(f"{other}_stage_done"), stage_count[me])

        def rng(L):
            return (0, 1) if L < DEPTH - 1 else (1,)

        def tiles(L):
            return range(NT) if L < DEPTH - 1 else LAT_TILES

        block = ctx.enter_context(nc.Block())

        def ada_banks(L, j):
            return (j % 2, 2) if L == 0 else (6, 7)

        def pe_ada_mm(pe, L, j):
            w = raw_full(pe, ("ada", L, j))
            if j == 0:
                pe.wait_ge(S("adab_loaded"), 16 * (L + 1))
            if j >= 2 - L:
                pe.wait_ge(S("ada_row"), 12 * L + j - 1 + L)
            ps = B(ada_banks(L, j)[0])[0:2, :]
            e12 = K[0:12, K_AT[K_E12] + 2 * j:K_AT[K_E12] + 2 * j + 2]
            pe.matmul(ps, e12, ADAB[0:12, :], start=True, stop=False)
            for k in range(KC):
                mm = pe.matmul(ps, SC[:, k, :], w[:, k, :], start=False, stop=k == KC - 1)
            mm.then_inc(S("ada_mm"), 1)

        def pe_ada_spread(pe, L, j):
            pe.wait_ge(S("ada_row"), 12 * L + j + 1)
            if j >= 1:
                pe.wait_ge(S("ada_cp"), 12 * L + j)
            b = ada_banks(L, j)[1]
            if j // 2 in (2, 5):
                for r in rng(L):
                    sel = K[0:2, K_AT[K_SELT] + P * r:K_AT[K_SELT] + P * r + P]
                    mm = pe.matmul(B(b + r * (1 - L)), sel, MROW[0:2, j % 2, :], start=True, stop=True)
            else:
                for c in range(4):
                    mm = pe.matmul(B(b)[:, 2 * c:2 * c + 2], MROW[0:2, j % 2, P * c:P * c + P],
                                   ident[0:2, 0:2], start=True, stop=True)
            mm.then_inc(S("ada_spread"), 1)

        def act_ada_row(act, L, j):
            act.wait_ge(S("ada_mm"), 12 * L + j + 1)
            if j >= 2:
                act.wait_ge(S("ada_spread"), 12 * L + j - 1)
            act.activation(MROW[0:2, j % 2, :], B(ada_banks(L, j)[0])[0:2, :], ACT.Copy).then_inc(S("ada_row"), 1)

        def dve_ada_cp(dve, L, j):
            m, half = j // 2, j % 2
            c = slice(512 * half, 512 * half + 512)
            b = ada_banks(L, j)[1]
            dve.wait_ge(S("ada_spread"), 12 * L + j + 1)
            if m in (2, 5) and L == 0:
                dve.tensor_copy(GATE[:, m // 3, :, c], PS[:, b:b + 2, :]).then_inc(S("ada_cp"), 1)
            elif m in (2, 5):
                dve.tensor_copy(gate(L, m // 3, 1)[:, c], B(b)).then_inc(S("ada_cp"), 1)
            else:
                dve.tensor_copy(MT[:, L, m, 4 * half:4 * half + 4, :],
                                B(b)[:, 0:8].rearrange("p (c r) -> p c r", r=2)).then_inc(S("ada_cp"), 1)

        def dve_ada_gain(dve, L):
            dve.wait_ge(S("ada_cp"), 12 * L + 12)
            for m, g in ((1, GMIX), (4, GFFN)):
                dve.scalar_tensor_tensor(out=MT[:, L, m, :, :], in0=MT[:, L, m, :, :], scalar=1.0,
                                         in1=bc(g[:, L, :], 2, 2), op0=ALU.add, op1=ALU.mult)

        def pe_ada(pe):
            for j in range(13):
                if j < 12:
                    pe_ada_mm(pe, 0, j)
                if j >= 1:
                    pe_ada_spread(pe, 0, j - 1)

        def act_ada(act):
            for j in range(12):
                act_ada_row(act, 0, j)

        def dve_ada(dve):
            for j in range(12):
                dve_ada_cp(dve, 0, j)
            dve_ada_gain(dve, 0)

        def norm_tiles(L, which):
            return list(range(NT)) if which == 0 else list(tiles(L))

        def act_norm(act, L, which):
            n, tt, v = "norm_", norm_tiles(L, which), 2 * L + which
            for x in tt:
                act.activation(A(0, D), X[:, x, :], ACT.Square,
                               accum_out=STAT[:, 0, x:x + 1]).then_inc(S(n + "ss"), 1)
                act.wait_ge(S(n + "ss"), 4 * v + tt.index(x) + 1)
            if v == 1:
                act_split(act, SPLIT_ITEMS[0])
            for k in range(1, KC, 2):
                act.wait_ge(S(n + "tp"), KC * v + k + 1)
                for r in sorted({x // 2 for x in tt}):
                    act.activation(HT[:, k, 256 * r:256 * r + 256], B(k % 4)[:, 256 * r:256 * r + 256], ACT.Identity,
                                   bias=MT[:, L, 3 * which, k, r:r + 1],
                                   scale=MT[:, L, 3 * which + 1, k, r:r + 1]).then_inc(S(n + "ht_act"), 1)

        def pool_norm(pool, L, which):
            n, tt, v = "norm_", norm_tiles(L, which), 2 * L + which
            a, b = tt[0], tt[-1] + 1
            pool.wait_ge(S(n + "ss"), 4 * v + len(tt))
            pool.tensor_scalar(STAT[:, 1, a:b], STAT[:, 0, a:b], 1.0 / D, EPS, ALU.mult, ALU.add).then_inc(S(n + "ms"), 1)
            pool.wait_ge(S(n + "ms"), v + 1)
            pool.tensor_tensor(STAT[:, 2, a:b], STAT[:, 1, a:b], NEGH[:, 0:b - a], ALU.pow).then_inc(S(n + "rstd"), 1)

        def dve_norm(dve, L, which):
            n, tt, v = "norm_", norm_tiles(L, which), 2 * L + which
            dve.wait_ge(S(n + "rstd"), v + 1)
            for x in tt:
                dve.tensor_scalar(XN[:, x, :], X[:, x, :], STAT[:, 2, x:x + 1], None, ALU.mult).then_inc(S(n + "xn"), 1)
            if v == 1:
                dve_split(dve, SPLIT_ITEMS[0])
            for k in range(0, KC, 2):
                dve.wait_ge(S(n + "tp"), KC * v + k + 1)
                for r in sorted({x // 2 for x in tt}):
                    dve.tensor_scalar(HT[:, k, 256 * r:256 * r + 256], B(k % 4)[:, 256 * r:256 * r + 256],
                                      MT[:, L, 3 * which + 1, k, r:r + 1], MT[:, L, 3 * which, k, r:r + 1],
                                      ALU.mult, ALU.add).then_inc(S(n + "ht_dve"), 1)

        def pe_norm(pe, L, which):
            n, tt, v = "norm_", norm_tiles(L, which), 2 * L + which
            nr = len({x // 2 for x in tt})
            pe.wait_ge(S(n + "xn"), 4 * v + len(tt))
            for k in range(KC):
                if k >= 4:
                    pe.wait_ge(S(n + ("ht_act" if k % 2 else "ht_dve")), 8 * v + nr * ((k - 4) // 2 + 1))
                for x in tt:
                    mm = pe.transpose(B(k % 4)[:, P * x:P * x + P], XN[:, x, P * k:P * k + P], ident)
                mm.then_inc(S(n + "tp"), 1)

        def proj_places(L):
            seen = {"act": 0, "dve": 0}
            for key, u, kind, c0, w, eng in proj_units(L):
                i = seen[eng]
                seen[eng] += 1
                yield key, u, kind, w, eng, (0 if eng == "act" else 4) + i % 4, i

        def pe_proj(pe, L):
            last = None
            for key, u, kind, w, eng, bank, i in proj_places(L):
                if key != last:
                    slot = raw_full(pe, (key, L))
                    last = key
                if i >= 4:
                    pe.wait_ge(S(f"proj_{eng}"), since(L, f"proj_{eng}") + i - 3)
                for k in range(KC):
                    if kind == "T":
                        mm = pe.matmul(B(bank), slot[:, k, P * u:P * u + P], HT[:, k, :], start=k == 0, stop=k == KC - 1)
                    else:
                        mm = pe.matmul(B(bank)[:, 0:w], HT[:, k, P * u:P * u + P], slot[:, k, 0:w],
                                       start=k == 0, stop=k == KC - 1)
                mm.then_inc(S("proj_mm"), 1)

        def act_proj(act, L):
            for n, (key, u, kind, w, eng, bank, i) in enumerate(proj_places(L)):
                if eng != "act":
                    continue
                act.wait_ge(S("proj_mm"), since(L, "proj_mm") + n + 1)
                if key == "bq":
                    act.activation(Q[:, u, :], B(bank), ACT.Silu).then_inc(S("proj_act"), 1)
                elif key == "bg":
                    act.activation(G[:, u, :], B(bank), ACT.Silu).then_inc(S("proj_act"), 1)
                else:
                    d = 0 if key == "bff" else 1
                    act.activation(FG[d][:, u, :], B(bank), ACT.Sigmoid)
                    act.activation(KE[d][:, u, :], B(bank), ACT.Sigmoid, scale=-1.0).then_inc(S("proj_act"), 1)

        def dve_proj(dve, L, keys):
            dst = {"aqk": AQK, "c": CQKV, "bi": V, "av": AV}
            for n, (key, u, kind, w, eng, bank, i) in enumerate(proj_places(L)):
                if key not in keys:
                    continue
                dve.wait_ge(S("proj_mm"), since(L, "proj_mm") + n + 1)
                dve.tensor_copy(dst[key][:, u, :], B(bank)[:, 0:w]).then_inc(S("proj_dve"), 1)

        def dve_qk(dve, L):
            n = "qk_"
            c3 = CQKV[:, :, 0:384]
            a3 = AQK.rearrange("p a (g d) -> p (a g) d", d=32)
            dve.wait_ge(S("proj_dve"), since(L, "proj_dve") + 2 * NT)
            dve.tensor_tensor(TMP, AQK, AQK, ALU.mult).then_inc(S(n + "sq"), 1)
            dve.tensor_tensor(TMP2[:, :, 0:384], c3, c3, ALU.mult).then_inc(S(n + "sq"), 1)
            dve.wait_ge(S(n + "sq"), since(L, n + "sq") + 2)
            dve.tensor_reduce(STAT[:, 0, 0:64], TMP.rearrange("p a (g d) -> p (a g) d", d=32), AX.X, ALU.add).then_inc(S(n + "ss"), 1)
            dve.tensor_reduce(STAT[:, 0, 64:88].rearrange("p (a g) -> p a g", g=6),
                              TMP2[:, :, 0:384].rearrange("p a (g d) -> p a g d", d=64), AX.X, ALU.add).then_inc(S(n + "ss"), 1)
            dve.wait_ge(S(n + "rstd"), since(L, n + "rstd") + 2)
            dve.tensor_tensor(a3, a3, bc(STAT[:, 2, 0:64], 2, 32), ALU.mult).then_inc(S(n + "x"), 1)
            for x in range(NT):
                v = CQKV[:, x, 0:384].rearrange("p (g d) -> p g d", d=64)
                dve.tensor_tensor(v, v, bc(STAT[:, 2, 64 + 6 * x:70 + 6 * x], 2, 64), ALU.mult).then_inc(S(n + "x"), 1)
            dve.wait_ge(S(n + "x"), since(L, n + "x") + 1 + NT)
            for j in range(2):
                v = AQK[:, :, 256 * j:256 * j + 256].rearrange("p a (g d) -> p a g d", d=32)
                g = bc(bc(QKG[:, L, j, :], 1, 8), 1, NT)
                dve.tensor_tensor(v, v, g, ALU.mult).then_inc(S(n + "gained"), 1)
            for j, (a, b) in enumerate(((0, 256), (256, 384))):
                v = CQKV[:, :, a:b].rearrange("p a (g d) -> p a g d", d=64)
                g = bc(bc(SQKG[:, L, j, :], 1, (b - a) // 64), 1, NT)
                dve.tensor_tensor(v, v, g, ALU.mult).then_inc(S(n + "gained"), 1)

        def pool_qk(pool, L):
            n = "qk_"
            pool.wait_ge(S(n + "ss"), since(L, n + "ss") + 2)
            pool.tensor_scalar(STAT[:, 1, 0:64], STAT[:, 0, 0:64], 1.0 / 32, EPS, ALU.mult, ALU.add).then_inc(S(n + "ms"), 1)
            pool.tensor_scalar(STAT[:, 1, 64:88], STAT[:, 0, 64:88], 1.0 / 64, EPS, ALU.mult, ALU.add).then_inc(S(n + "ms"), 1)
            pool.wait_ge(S(n + "ms"), since(L, n + "ms") + 2)
            pool.tensor_tensor(STAT[:, 2, 0:64], STAT[:, 1, 0:64], NEGH[:, :], ALU.pow).then_inc(S(n + "rstd"), 1)
            pool.tensor_tensor(STAT[:, 2, 64:88], STAT[:, 1, 64:88], NEGH[:, 0:24], ALU.pow).then_inc(S(n + "rstd"), 1)
            pool.wait_ge(S(n + "gained"), since(L, n + "gained") + 4)
            for x in LAT_TILES:
                for src, dim, g, kcos, ksin in ((AQK[:, x, :], 32, 16, K_C32, K_S32),
                                                (CQKV[:, x, 0:384], 64, 6, K_C64, K_S64)):
                    c = kc(kcos)[:, dim * (x - 2):dim * (x - 1)]
                    s = kc(ksin)[:, dim * (x - 2):dim * (x - 1)]
                    nf = dim // 4
                    w = g * dim
                    v = src.rearrange("p (g d) -> p g d", d=dim)
                    turned = TMP2[:, x, 0:w].rearrange("p (g h b f) -> p g h b f", h=2, b=2, f=nf)
                    halves = src.rearrange("p (g h b f) -> p g h b f", h=2, b=2, f=nf)
                    sh = s.rearrange("p (h b f) -> p h b f", h=2, b=2)
                    for b in range(2):
                        pool.tensor_tensor(turned[:, :, :, b, :], halves[:, :, :, 1 - b, :],
                                           bc(sh[:, :, b, :], 1, g), ALU.mult).then_inc(S(n + "turned"), 1)
                    pool.tensor_tensor(TMP[:, x, 0:w].rearrange("p (g d) -> p g d", d=dim), v, bc(c, 1, g),
                                       ALU.mult).then_inc(S(n + "turned"), 1)
                    k = 3 * (2 * (x - 2) + (0 if dim == 32 else 1) + 1)
                    pool.wait_ge(S(n + "turned"), since(L, n + "turned") + k)
                    pool.tensor_tensor(src, TMP[:, x, 0:w], TMP2[:, x, 0:w], ALU.add).then_inc(S(n + "rotated"), 1)
                    pool.wait_ge(S(n + "rotated"), since(L, n + "rotated") + k // 3)

        def hgrn_gates(eng, L, d):
            n = f"h{d}_"
            eng.wait_ge(S("proj_act"), since(L, "proj_act") + 3 * NH)
            if L > 0:
                for h in range(NH):
                    eng.tensor_scalar(FG[d][:, h, :], FG[d][:, h, :], LBT[:, 5, d, h:h + 1], LBT[:, 4, d, h:h + 1],
                                      ALU.mult, ALU.add).then_inc(S(n + "f"), 1)
                    eng.tensor_scalar(KE[d][:, h, :], KE[d][:, h, :], LBT[:, 5, d, h:h + 1], None,
                                      ALU.mult).then_inc(S(n + "f"), 1)
                eng.wait_ge(S(n + "f"), since(L, n + "f") + 2 * NH)
            eng.tensor_tensor(QP[d], Q, FG[d], ALU.mult).then_inc(S(n + "qp"), 1)
            eng.wait_ge(S(n + "qp"), since(L, n + "qp") + 1)

        def hgrn_double(eng, L, d, n_level):
            n = f"h{d}_"
            m = LEVELS[n_level]
            nb = NH * 512 // m
            tot = FG[d].rearrange("p a b -> p (a b)") if n_level == 0 else (
                TB[d][:, 0:nb] if n_level % 2 else FG[d].rearrange("p a b -> p (a b)")[:, 0:nb])
            new = TB[d][:, 0:nb // 2] if n_level % 2 == 0 else FG[d].rearrange("p a b -> p (a b)")[:, 0:nb // 2]
            tv = tot.rearrange("p (b h) -> p b h", h=2)
            early, late = (0, 1) if d == 0 else (1, 0)
            qv = QP[d].rearrange("p a b -> p (a b)").rearrange("p (b h m) -> p b h m", h=2, m=m)
            kv = KE[d].rearrange("p a b -> p (a b)").rearrange("p (b h m) -> p b h m", h=2, m=m)
            eng.wait_ge(S(n + "mm"), since(L, n + "mm") + n_level + 2)
            eng.tensor_tensor(qv[:, :, late, :], qv[:, :, late, :], bc(tv[:, :, early], 2, m), ALU.mult).then_inc(S(n + "upd"), 1)
            eng.tensor_tensor(kv[:, :, early, :], kv[:, :, early, :], bc(tv[:, :, late], 2, m), ALU.mult).then_inc(S(n + "upd"), 1)
            eng.tensor_tensor(new, tv[:, :, 0], tv[:, :, 1], ALU.mult).then_inc(S(n + "upd"), 1)
            eng.wait_ge(S(n + "upd"), since(L, n + "upd") + 3 * (n_level + 1))

        def pe_levels(pe, L):
            ts = list(tiles(L))
            pe.wait_ge(S("proj_act"), since(L, "proj_act") + 3 * NH + len(ts))
            pe.wait_ge(S("proj_dve"), since(L, "proj_dve") + 4 * NT)
            for n_level in range(-1, len(LEVELS)):
                for d in range(2):
                    n = f"h{d}_"
                    pe.wait_ge(S(n + "qp"), since(L, n + "qp") + 1)
                    if n_level >= 1:
                        pe.wait_ge(S(n + "upd"), since(L, n + "upd") + 3 * n_level)
                    if n_level >= 0:
                        pe.wait_ge(S(n + "taken"), since(L, n + "taken") + n_level + 1)
                    for h in range(NH):
                        for x in ts:
                            c = slice(P * x, P * x + P)
                            q = Q if n_level < 0 else QP[d]
                            mm = pe.matmul(B(4 * d + h)[:, c], KE[d][:, h, c], q[:, h, c], start=True, stop=True)
                    mm.then_inc(S(n + "mm"), 1)

        def dve_take(dve, L, d, n_level):
            n = f"h{d}_"
            ts = list(tiles(L))
            a, nt = P * ts[0], len(ts)
            dve.wait_ge(S(n + "mm"), since(L, n + "mm") + n_level + 2)
            if n_level < 0:
                for h in range(NH):
                    src = B(4 * d + h)[:, a:].rearrange("p (x t) -> p x t", t=P)
                    dst = ST[d][:, h, a:].rearrange("p (x t) -> p x t", t=P)
                    ins = dve.tensor_tensor(dst, src, bc(ident, 1, nt), ALU.mult)
            else:
                for h in range(NH):
                    src = B(4 * d + h)[:, a:].rearrange("p (x t) -> p x t", t=P)
                    dst = ST[d][:, h, a:].rearrange("p (x t) -> p x t", t=P)
                    dve.wait_ge(S(n + "taken"), since(L, n + "taken") + n_level + 1)
                    ins = dve.copy_predicated(dst, bc(M8[:, d, n_level, :], 1, nt), src)
            ins.then_inc(S(n + "taken"), 1)

        def dve_levels(dve, L):
            dve.wait_ge(S("qk_rotated"), since(L, "qk_rotated") + 4)
            dve_take(dve, L, 0, -1)
            dve_take(dve, L, 1, -1)
            for n_level in range(len(LEVELS)):
                dve_take(dve, L, 0, n_level)
                hgrn_double(dve, L, 0, n_level)
                dve_take(dve, L, 1, n_level)

        def pool_levels(pool, L):
            hgrn_gates(pool, L, 1)
            for n_level in range(len(LEVELS)):
                hgrn_double(pool, L, 1, n_level)

        def pe_mix_in(pe, L):
            pe_proj(pe, L)
            pe_levels(pe, L)

        def dve_mix_in(dve, L):
            dve_proj(dve, L, ("aqk", "c"))
            dve_qk(dve, L)
            dve_proj(dve, L, ("bi",))
            hgrn_gates(dve, L, 0)
            dve_proj(dve, L, ("av",))
            dve_levels(dve, L)

        def pool_mix_in(pool, L):
            pool_qk(pool, L)
            pool_levels(pool, L)

        ORDER = [(0, 1, 2, 3), (1, 0, 3, 2)]

        def pe_states(pe, L):
            n = "s_"
            for i in range(3):
                b0 = 4 * (i % 2)
                for d in range(2):
                    x = ORDER[d][i]
                    for h in range(NH):
                        mm = pe.transpose(B(b0 + d)[:, P * h:P * h + P], KE[d][:, h, P * x:P * x + P], ident)
                    mm.then_inc(S(n + "kt"), 1)
                for d in range(2):
                    x = ORDER[d][i]
                    pe.wait_ge(S(n + "kd"), since(L, n + "kd") + 2 * i + d + 1)
                    if i >= 2:
                        pe.wait_ge(S(n + "st"), since(L, n + "st") + 2 * NH * (i - 1))
                    for h in range(NH):
                        mm = pe.matmul(B(b0 + 2 + d)[:, P * h:P * h + P], KDT[:, d, h, :], V[:, x, P * h:P * h + P],
                                       start=True, stop=True)
                    mm.then_inc(S(n + "kv"), 1)
            pe.wait_ge(S(n + "st"), since(L, n + "st") + 6 * NH)
            for j, x in enumerate(tiles(L)):
                c = slice(P * x, P * x + P)
                for h in range(NH):
                    o = B(j)[:, P * h:P * h + P]
                    v = V[:, x, P * h:P * h + P]
                    pairs = [(ST[0][:, h, c], v), (ST[1][:, h, c], v)]
                    for d in range(2):
                        i = ORDER[d].index(x)
                        if i:
                            pairs.append((QP[d][:, h, c], SST[:, i - 1, d, h, :]))
                    for k, (a, b) in enumerate(pairs):
                        mm = pe.matmul(o, a, b, start=k == 0, stop=k == len(pairs) - 1)
                mm.then_inc(S(n + "o"), 1)

        def act_states(act, L):
            n = "s_"
            for i in range(3):
                for d in range(2):
                    act.wait_ge(S(n + "kt"), since(L, n + "kt") + 2 * i + d + 1)
                    if i:
                        act.wait_ge(S(n + "kv"), since(L, n + "kv") + 2 * (i - 1) + d + 1)
                    act.activation(KDT[:, d, :, :], B(4 * (i % 2) + d).rearrange("p (h k) -> p h k", k=P),
                                   ACT.Copy).then_inc(S(n + "kd"), 1)

        def dve_states(dve, L):
            n = "s_"
            for i in range(3):
                for d in range(2):
                    x = ORDER[d][i]
                    dve.wait_ge(S(n + "kv"), since(L, n + "kv") + 2 * i + d + 1)
                    if i:
                        dve.wait_ge(S(n + "st"), since(L, n + "st") + 2 * NH * i)
                    for h in range(NH):
                        ps = B(4 * (i % 2) + 2 + d)[:, P * h:P * h + P]
                        if i == 0:
                            dve.tensor_copy(SST[:, 0, d, h, :], ps).then_inc(S(n + "st"), 1)
                        else:
                            total = TB[d][:, NT * h + x:NT * h + x + 1]
                            dve.scalar_tensor_tensor(out=SST[:, i, d, h, :], in0=SST[:, i - 1, d, h, :], scalar=total,
                                                     in1=ps, op0=ALU.mult, op1=ALU.add).then_inc(S(n + "st"), 1)
            for j, x in enumerate(tiles(L)):
                dve.wait_ge(S(n + "o"), since(L, n + "o") + j + 1)
                dve.tensor_copy(MIX[:, x, 256:768], B(j)).then_inc(S(n + "mix"), 1)

        def out_rows(L):
            ts = list(tiles(L))
            return slice(ts[0], ts[-1] + 1), len(ts)

        POST_STEPS = 5

        def dve_post(dve, L, name, step):
            n, v = "post_", 2 * L + (name == "dp")
            rows, nt = out_rows(L)
            c0, dim, w, gain = (256, 128, 512, HNG[:, L, :]) if name == "hp" else (0, 64, 256, SUBG[:, L, :])
            hs = w // dim
            o = MIX[:, rows, c0:c0 + w]
            sq = OT[:, rows, 0:w]
            if step == 0:
                dve.tensor_tensor(sq, o, o, ALU.mult).then_inc(S(n + "sq"), 1)
            elif step == 1:
                dve.wait_ge(S(n + "sq"), v + 1)
                st = STAT[:, 0, 0:nt * hs]
                dve.tensor_reduce(st.rearrange("p (a g) -> p a g", g=hs), sq.rearrange("p a (g d) -> p a g d", d=dim),
                                  AX.X, ALU.add).then_inc(S(n + "ss"), 1)
            elif step == 2:
                dve.wait_ge(S(n + "rstd"), v + 1)
                for j, x in enumerate(tiles(L)):
                    mv = MIX[:, x, c0:c0 + w].rearrange("p (g d) -> p g d", d=dim)
                    dve.tensor_tensor(mv, mv, bc(STAT[:, 2, hs * j:hs * j + hs], 2, dim), ALU.mult).then_inc(S(n + "x"), 1)
            elif step == 3:
                dve.wait_ge(S(n + "x"), (0, 4, 8, 10)[v] + nt)
                ov = o.rearrange("p a (g d) -> p a g d", d=dim)
                dve.tensor_tensor(ov, ov, bc(bc(gain, 1, hs), 1, nt), ALU.mult).then_inc(S(n + "g"), 1)
            else:
                dve.wait_ge(S(n + "g"), v + 1)
                if name == "hp":
                    dve.tensor_tensor(o, o, G[:, rows, :], ALU.mult)
                else:
                    dve.tensor_scalar(o, o, 0.2 + 0.6 * math.exp(-0.3 * L), None, ALU.mult)

        def pool_post(pool, L, name, dim):
            n, v = "post_", 2 * L + (name == "dp")
            nt = out_rows(L)[1]
            w = nt * ((512 if name == "hp" else 256) // dim)
            pool.wait_ge(S(n + "ss"), v + 1)
            pool.tensor_scalar(STAT[:, 1, 0:w], STAT[:, 0, 0:w], 1.0 / dim, EPS, ALU.mult, ALU.add).then_inc(S(n + "ms"), 1)
            pool.wait_ge(S(n + "ms"), v + 1)
            pool.tensor_tensor(STAT[:, 2, 0:w], STAT[:, 1, 0:w], NEGH[:, 0:w], ALU.pow).then_inc(S(n + "rstd"), 1)

        def units(L):
            return [(kind, h, x) for x in tiles(L) for h in range(NH) for kind in "DW"]

        def keys(x):
            return 256 if x in CTX_TILES else 512

        def masked(L, u):
            return sum(k == "W" and x in LAT_TILES for k, _, x in units(L)[:u])

        def pe_qkt(pe, L):
            n = "t_"
            for b in range(7):
                for x in range(NT):
                    src = AQK[:, x, P * b:P * b + P] if b < 4 else CQKV[:, x, P * (b - 4):P * (b - 3)]
                    mm = pe.transpose(B(b)[:, P * x:P * x + P], src, ident)
                mm.then_inc(S(n + "tp"), 1)

        def act_qkt(act, L):
            for b in range(0, 7, 2):
                act.wait_ge(S("t_tp"), since(L, "t_tp") + b + 1)
                act.activation(QKT[:, b, :] if b < 4 else CT[:, b - 4, :], B(b), ACT.Copy)

        def dve_qkt(dve, L):
            for b in range(1, 7, 2):
                dve.wait_ge(S("t_tp"), since(L, "t_tp") + b + 1)
                dve.tensor_copy(QKT[:, b, :] if b < 4 else CT[:, b - 4, :], B(b))

        def pe_att(pe, L):
            n, us = "a_", units(L)
            for s in range(len(us) + 3):
                if s < len(us):
                    kind, h, x = us[s]
                    if s >= 2:
                        pe.wait_ge(S(n + "exp"), since(L, n + "exp") + s - 1)
                    c, nk = slice(P * x, P * x + P), keys(x)
                    if kind == "D":
                        for m in range(2):
                            g = 2 * h + m
                            r = slice(32 * (g % 4), 32 * (g % 4) + 32)
                            mm = pe.matmul(B(2 * (s % 2) + m)[:, 0:nk], QKT[r, g // 4, c], QKT[r, 2 + g // 4, 0:nk],
                                           start=True, stop=True)
                    else:
                        r = slice(64 * (h // 2), 64 * (h // 2) + 64)
                        mm = pe.matmul(B(2 * (s % 2))[:, 0:nk], CT[r, h % 2, c], CT[r, 2, 0:nk], start=True, stop=True)
                    mm.then_inc(S(n + "s"), 1)
                if 2 <= s < len(us) + 2:
                    u = s - 2
                    pe.wait_ge(S(n + "p"), since(L, n + "p") + u + 1)
                    if u >= 2:
                        pe.wait_ge(S(n + "at"), since(L, n + "at") + u - 1)
                    for k in range(keys(us[u][2]) // P):
                        mm = pe.transpose(B(4 + u % 2)[:, P * k:P * k + P], EX[:, u % 4, 0, P * k:P * k + P], ident)
                    mm.then_inc(S(n + "pt"), 1)
                if s >= 3:
                    u = s - 3
                    kind, h, x = us[u]
                    pe.wait_ge(S(n + "at"), since(L, n + "at") + u + 1)
                    if u >= 2:
                        pe.wait_ge(S(n + "o"), since(L, n + "o") + u - 1)
                    nk = keys(x) // P
                    for k in range(nk):
                        v = AV[:, k, 64 * h:64 * h + 64] if kind == "D" else CQKV[:, k, 384 + 64 * (h // 2):448 + 64 * (h // 2)]
                        mm = pe.matmul(B(6 + u % 2)[:, 0:64], AT[:, u % 2, P * k:P * k + P], v, start=k == 0, stop=k == nk - 1)
                    mm.then_inc(S(n + "pv"), 1)

        def act_att(act, L):
            n, us = "a_", units(L)
            for s in range(len(us) + 2):
                if s < len(us):
                    kind, h, x = us[s]
                    nk = keys(x)
                    act.wait_ge(S(n + "nb"), since(L, n + "nb") + s + 1)
                    if s >= 4:
                        act.wait_ge(S(n + "pt"), since(L, n + "pt") + s - 3)
                    if kind == "D":
                        for m in range(2):
                            ins = act.activation(EX[:, s % 4, m, 0:nk], B(2 * (s % 2) + m)[:, 0:nk], ACT.Exp,
                                                 bias=AST[:, 1, s, m:m + 1], scale=32 ** -0.5,
                                                 accum_out=AST[:, 2, s, m:m + 1])
                    else:
                        src = MSK[:, masked(L, s) % 2, :] if x in LAT_TILES else B(2 * (s % 2))[:, 0:nk]
                        act.activation(AST[:, 3, s, 0:1], SINK[:, L, h:h + 1], ACT.Exp, bias=AST[:, 1, s, 0:1])
                        ins = act.activation(EX[:, s % 4, 0, 0:nk], src, ACT.Exp, bias=AST[:, 1, s, 0:1],
                                             scale=64 ** -0.5, accum_out=AST[:, 2, s, 0:1])
                    ins.then_inc(S(n + "exp"), 1)
                if s >= 2:
                    u = s - 2
                    nk = keys(us[u][2])
                    act.wait_ge(S(n + "pt"), since(L, n + "pt") + u + 1)
                    if u >= 2:
                        act.wait_ge(S(n + "pv"), since(L, n + "pv") + u - 1)
                    act.activation(AT[:, u % 2, 0:nk], B(4 + u % 2)[:, 0:nk], ACT.Copy).then_inc(S(n + "at"), 1)

        def dve_att(dve, L):
            n, us = "a_", units(L)
            for s in range(len(us) + 4):
                if s < len(us):
                    kind, h, x = us[s]
                    nk = keys(x)
                    dve.wait_ge(S(n + "s"), since(L, n + "s") + s + 1)
                    if kind == "D":
                        dve.tensor_reduce(AST[:, 0, s, :], PS[:, 2 * (s % 2):2 * (s % 2) + 2, 0:nk], AX.X,
                                          ALU.max).then_inc(S(n + "mx"), 1)
                        dve.wait_ge(S(n + "mx"), since(L, n + "mx") + s + 1)
                        dve.tensor_scalar(AST[:, 1, s, :], AST[:, 0, s, :], -(32 ** -0.5), None,
                                          ALU.mult).then_inc(S(n + "nb"), 1)
                    else:
                        src = B(2 * (s % 2))[:, 0:nk]
                        if x in LAT_TILES:
                            w = masked(L, s)
                            if w >= 2:
                                before = [i for i, (k, _, y) in enumerate(us) if k == "W" and y in LAT_TILES][w - 2]
                                dve.wait_ge(S(n + "exp"), since(L, n + "exp") + before + 1)
                            dst = MSK[:, w % 2, :]
                            o = 384 if x == 2 else 256
                            dve.tensor_tensor(dst[:, o:o + P], src[:, o:o + P], kc(K_SWA)[:, P * (x - 2):P * (x - 1)],
                                              ALU.add).then_inc(S(n + "msk"), 1)
                            if x == 2:
                                dve.tensor_copy(dst[:, 0:384], src[:, 0:384]).then_inc(S(n + "msk"), 1)
                            else:
                                dve.tensor_copy(dst[:, 0:256], src[:, 0:256])
                                dve.tensor_copy(dst[:, 384:512], src[:, 384:512]).then_inc(S(n + "msk"), 1)
                            dve.wait_ge(S(n + "msk"), since(L, n + "msk") + 2 * (w + 1))
                            src = dst
                        dve.tensor_reduce(AST[:, 0, s, 0:1], src, AX.X, ALU.max).then_inc(S(n + "mx"), 1)
                        dve.wait_ge(S(n + "mx"), since(L, n + "mx") + s + 1)
                        dve.tensor_scalar(AST[:, 1, s, 0:1], AST[:, 0, s, 0:1], -(64 ** -0.5), NSINK[:, L, h:h + 1],
                                          ALU.mult, ALU.min).then_inc(S(n + "nb"), 1)
                if 1 <= s <= len(us):
                    u = s - 1
                    kind, h, x = us[u]
                    nk = keys(x)
                    dve.wait_ge(S(n + "exp"), since(L, n + "exp") + u + 1)
                    if kind == "D":
                        dve.reciprocal(AST[:, 4, u, :], AST[:, 2, u, :]).then_inc(S(n + "r"), 1)
                        dve.wait_ge(S(n + "r"), since(L, n + "r") + u + 1)
                        dve.tensor_scalar(AST[:, 5, u, 0:1], AST[:, 4, u, 1:2], AST[:, 2, u, 0:1], LAM[:, L, 5:6],
                                          ALU.mult, ALU.mult).then_inc(S(n + "ratio"), 1)
                        dve.wait_ge(S(n + "ratio"), since(L, n + "ratio") + u + 1)
                        e = EX[:, u % 4, 0, 0:nk]
                        dve.scalar_tensor_tensor(out=e, in0=EX[:, u % 4, 1, 0:nk], scalar=AST[:, 5, u, 0:1], in1=e,
                                                 op0=ALU.mult, op1=ALU.add).then_inc(S(n + "p"), 1)
                    else:
                        dve.tensor_tensor(AST[:, 5, u, 0:1], AST[:, 2, u, 0:1], AST[:, 3, u, 0:1], ALU.add).then_inc(S(n + "ratio"), 1)
                        dve.wait_ge(S(n + "ratio"), since(L, n + "ratio") + u + 1)
                        dve.reciprocal(AST[:, 4, u, 0:1], AST[:, 5, u, 0:1]).then_inc(S(n + "r"), 1)
                        dve.wait_ge(S(n + "r"), since(L, n + "r") + u + 1)
                        dve.tensor_copy(AST[:, 3, u, 1:2], AST[:, 4, u, 0:1]).then_inc(S(n + "p"), 1)
                if s >= 4:
                    u = s - 4
                    kind, h, x = us[u]
                    dve.wait_ge(S(n + "pv"), since(L, n + "pv") + u + 1)
                    c = (0 if kind == "D" else 768) + 64 * h
                    dve.tensor_scalar(MIX[:, x, c:c + 64], B(6 + u % 2)[:, 0:64], AST[:, 4, u, 0:1], None,
                                      ALU.mult).then_inc(S(n + "o"), 1)
                if s % 2 == 0 and 4 <= s < 4 + 2 * POST_STEPS:
                    dve_post(dve, L, "hp", s // 2 - 2)

        def pe_out(pe, L):
            n, ts = "o_", list(tiles(L))
            for k in range(KC):
                if k >= 4:
                    pe.wait_ge(S(n + "mt_lo"), KC * L + k - 3)
                for x in ts:
                    mm = pe.transpose(B(k % 4)[:, P * x:P * x + P], MIX[:, x, P * k:P * k + P], ident)
                mm.then_inc(S(n + "tp"), 1)
            pe.wait_ge(S(n + "mt_lo"), KC * L + KC)
            for h in range(2):
                for half in range(2):
                    hi, lo = pe_parts(pe, ("out", L, h, half))
                    for i, x in enumerate(ts):
                        for j in range(KC // 2):
                            k = 4 * half + j
                            for m, (a, b) in enumerate(((MTH, hi), (MTH, lo), (MTL, hi))):
                                mm = pe.matmul(B(len(ts) * h + i), a[:, k, P * x:P * x + P], b[:, j, :],
                                               start=k == 0 and m == 0, stop=k == KC - 1 and m == 2)
                        if half == 1:
                            mm.then_inc(S("out_mm"), 1)
                    if half == 0:
                        mm.then_inc(S("out_half"), 1)

        def act_out(act, L):
            n, a = "o_", P * tiles(L)[0]
            for half in range(2):
                act_split(act, ("out", L, 0, half))
            for k in range(KC):
                act.wait_ge(S(n + "tp"), KC * L + k + 1)
                act.activation(MTH[:, k, a:], B(k % 4)[:, a:], ACT.Copy).then_inc(S(n + "mt_hi"), 1)
            for half in range(2):
                act_split(act, ("out", L, 1, half))

        def dve_out(dve, L):
            n, ts = "o_", list(tiles(L))
            a = P * ts[0]
            for half in range(2):
                dve_split(dve, ("out", L, 0, half))
            for k in range(KC):
                dve.wait_ge(S(n + "mt_hi"), KC * L + k + 1)
                dve.tensor_tensor(MTL[:, k, a:], B(k % 4)[:, a:], MTH[:, k, a:],
                                  ALU.subtract).then_inc(S(n + "mt_lo"), 1)
            for half in range(2):
                dve_split(dve, ("out", L, 1, half))
            for h in range(2):
                for j, x in enumerate(ts):
                    i = len(ts) * h + j
                    dve.wait_ge(S("out_mm"), since(L, "out_mm") + i + 1)
                    if i >= 2:
                        dve.wait_ge(S(n + "added"), since(L, n + "added") + i - 1)
                    c = slice(512 * h, 512 * h + 512)
                    dve.tensor_tensor(YT[:, i % 2, :], B(i), gate(L, 0, x // 2)[:, c], ALU.mult).then_inc(S(n + "gated"), 1)
                    dve.wait_ge(S(n + "gated"), since(L, n + "gated") + i + 1)
                    dve.tensor_tensor(X[:, x, c], X[:, x, c], YT[:, i % 2, :], ALU.add).then_inc(S(n + "added"), 1)

        def pe_ffn(pe):
            pending = None
            for key in FFN_ITEMS:
                if key[0] == "ada":
                    pe_ada_mm(pe, 1, key[2])
                    pending = key[2]
                elif key[0] == "w2":
                    if key[1] == 0:
                        pe_ada_spread(pe, 1, 11)
                        pe.wait_ge(S("ada_cp"), 24)
                    hi, lo = (v.rearrange("p k n -> p (k n)") for v in pe_parts(pe, key))
                    for c in range(4 * key[1], min(4 * key[1] + 4, FC)):
                        if c == 0 or c >= 20:
                            pe.wait_ge(S("ffn_lo"), FC - 2 if c == 0 else c + 1)
                        for x in range(NT):
                            for n, (a, w) in enumerate(((ACTH, hi), (ACTH, lo), (ACTL, hi))):
                                for h in range(2):
                                    at = D * (c - 4 * key[1]) + 512 * h
                                    mm = pe.matmul(B(2 * x + h), a[:, c, P * x:P * x + P], w[:, at:at + 512],
                                                   start=c == 0 and n == 0, stop=c == FC - 1 and n == 2)
                    mm.then_inc(S("ffn_y_mm"), 1)
                else:
                    b0, sem, ev = (0, "ffn_u_mm", "ffn_u") if key[0] == "w1" else (3, "ffn_v_mm", "ffn_act")
                    hi, lo, number = items[key]["hi"], items[key]["lo"], items[key]["number"]
                    pe.wait_ge(S("split_hi"), number)
                    for c in range(FT[key[1]][1] // P):
                        i = 4 * key[1] + c
                        if i >= 3:
                            pe.wait_ge(S(ev), i - 2)
                        for w in (hi, lo):
                            if c == 0 and w is lo:
                                pe.wait_ge(S("split_lo"), number)
                            for k in range(KC):
                                if i == 0 and key[0] == "w1" and w is hi:
                                    pe.wait_ge(S("in_lo"), k + 1)
                                for x in (HTH, HTL) if w is hi else (HTH,):
                                    mm = pe.matmul(B(b0 + i % 3), w[:, k, P * c:P * c + P], x[:, k, :],
                                                   start=k == 0 and w is hi and x is HTH,
                                                   stop=k == KC - 1 and w is lo)
                        mm.then_inc(S(sem), 1)
                        if pending is not None:
                            pe_ada_spread(pe, 1, pending)
                            pending = None

        def act_ffn(act):
            for k in range(KC):
                act.wait_ge(S("norm_ht_act" if k % 2 else "norm_ht_dve"), 8 + 2 * (k // 2 + 1))
                act.activation(HTH[:, k, :], HT[:, k, :], ACT.Copy).then_inc(S("in_hi"), 1)
            for key in FFN_ITEMS:
                if key in SPLIT_ITEMS[:-1]:
                    act_split(act, SPLIT_ITEMS[SPLIT_ITEMS.index(key) + 1])
                if key[0] == "ada":
                    act_ada_row(act, 1, key[2])
                elif key[0] != "w2":
                    for i in range(4 * key[1], min(4 * key[1] + 4, FC)):
                        if key[0] == "w1":
                            act.wait_ge(S("ffn_u_mm"), i + 1)
                            if i >= 4:
                                act.wait_ge(S("ffn_lo"), i - 3)
                            act.activation(UT[:, i % 4, :], B(i % 3), ACT.Silu).then_inc(S("ffn_u"), 1)
                        else:
                            act.wait_ge(S("ffn_act"), i + 1)
                            act.activation(ACTH[:, i, :], UT[:, i % 4, :], ACT.Copy).then_inc(S("ffn_hi"), 1)

        def dve_ffn(dve):
            for k in range(KC):
                dve.wait_ge(S("in_hi"), k + 1)
                dve.tensor_tensor(HTL[:, k, :], HT[:, k, :], HTH[:, k, :], ALU.subtract).then_inc(S("in_lo"), 1)
            pending = None
            for key in FFN_ITEMS:
                if key in SPLIT_ITEMS[:-1]:
                    dve_split(dve, SPLIT_ITEMS[SPLIT_ITEMS.index(key) + 1])
                if key[0] == "ada":
                    pending = key[2]
                    if pending == 11:
                        dve_ada_cp(dve, 1, pending)
                        dve_ada_gain(dve, 1)
                elif key[0] != "w2":
                    if pending is not None:
                        dve_ada_cp(dve, 1, pending)
                        pending = None
                    if key[0] == "w3":
                        chunks = range(4 * key[1], min(4 * key[1] + 4, FC))
                        for i in chunks:
                            dve.wait_ge(S("ffn_u"), i + 1)
                            dve.wait_ge(S("ffn_v_mm"), i + 1)
                            dve.tensor_tensor(UT[:, i % 4, :], B(3 + i % 3), UT[:, i % 4, :],
                                              ALU.mult).then_inc(S("ffn_act"), 1)
                        for i in chunks:
                            dve.wait_ge(S("ffn_hi"), i + 1)
                            dve.tensor_tensor(ACTL[:, i, :], UT[:, i % 4, :], ACTH[:, i, :],
                                              ALU.subtract).then_inc(S("ffn_lo"), 1)
            dve.wait_ge(S("ffn_y_mm"), 6)
            for i in range(8):
                x, h = i // 2, i % 2
                dve.tensor_tensor(FTMP[:, i, :], B(i), gate(0, 1, x // 2)[:, 512 * h:512 * h + 512],
                                  ALU.mult).then_inc(S("ffn_gated"), 1)
            for i in range(8):
                x, c = i // 2, slice(512 * (i % 2), 512 * (i % 2) + 512)
                dve.wait_ge(S("ffn_gated"), i + 1)
                dve.tensor_tensor(X[:, x, c], X[:, x, c], FTMP[:, i, :], ALU.add)

        NPIECE, NRAW, NSPLIT = 24, 4, 8
        RAW = [A(11 * s, D_FF) for s in range(NRAW)]
        SPLIT = [ARENA[:, 256 * (44 + 11 * s):256 * (55 + 11 * s)].bitcast(BF16) for s in range(NSPLIT)]
        WHI = [v[:, 0:D_FF] for v in SPLIT]
        WLO = [v[:, D_FF:2 * D_FF] for v in SPLIT]
        UA = A(132, D_FF)
        AEP = ARENA[:, 256 * 143:256 * 154].bitcast(BF16).rearrange("p (h c s) -> p h c s", h=2, c=FC)
        AEH, AEL = AEP[:, 0], AEP[:, 1]
        HEP = ARENA[:, 256 * 154:256 * 158].bitcast(BF16).rearrange("p (h k s) -> p h k s", h=2, k=KC)
        HEH, HEL = HEP[:, 0], HEP[:, 1]
        PG = A(158, 2, P)
        PT = A(159, 2, P)
        PH = ARENA[:, 256 * 160:256 * 160 + P].bitcast(BF16).rearrange("p (x s) -> p x s", x=2)
        XLP = GATE[:, 1, :, :].rearrange("p a n -> p (a n)").bitcast(BF16).rearrange("p (h x n) -> p h x n", h=2, x=2)
        XLH, XLL = XLP[:, 0], XLP[:, 1]
        YE = GATE[:, 0, 1, :]
        Y = X[:, 0:2, :]
        RT = A(16, 9, 2, N_EXP)
        RV = A(17, 8, 2)
        NIT = 2 * N_EXP + 1
        POS = sb("POS", [P, 2, NIT])
        GT = sb("GT", [P, 2, NIT])
        CNT = sb("CNT", [P, 4])
        NROUND = sb("NROUND", [P, 1], I32)

        def pe_route(pe):
            for x in range(2):
                for k in range(KC):
                    mm = pe.matmul(B(0)[:, 8 * x:8 * x + 8], HT[:, k, 256 + P * x:384 + P * x], ROUT[:, k, :],
                                   start=k == 0, stop=k == KC - 1)
            mm.then_inc(S("r_logits"), 1)
            for x in range(2):
                for k in range(KC):
                    mm = pe.transpose(B(4 + 2 * x + k // 4)[:, P * (k % 4):P * (k % 4) + P],
                                      HT[:, k, 256 + P * x:384 + P * x], ident)
            mm.then_inc(S("r_rows"), 1)
            pe.wait_ge(S("r_sel"), 1)
            one, tri = kc(K_ONE), kc(K_TRI)
            pe.matmul(B(1)[:, 0:8], tri, RT[:, 8, 0, :], start=True, stop=True)
            pe.matmul(B(1)[:, 8:16], one, RT[:, 8, 0, :], start=True, stop=False)
            pe.matmul(B(1)[:, 8:16], tri, RT[:, 8, 1, :], start=False, stop=True)
            pe.matmul(B(1)[:, 16:24], one, RT[:, 8, 0, :], start=True, stop=False)
            pe.matmul(B(1)[:, 16:24], one, RT[:, 8, 1, :], start=False, stop=True).then_inc(S("r_pos"), 1)

        def dve_route(dve):
            step = [0]

            def then(ins):
                step[0] += 1
                ins.then_inc(S("r_step"), 1)
                dve.wait_ge(S("r_step"), step[0])

            dve.wait_ge(S("r_logits"), 1)
            lg, rev = RT[:, 0, :, :], kc(K_REV).rearrange("p (x e) -> p x e", e=8)
            then(dve.tensor_copy(lg, B(0)[:, 0:16].rearrange("p (x e) -> p x e", e=8)))
            for r in range(2):
                then(dve.tensor_reduce(RV[:, r, :], lg, AX.X, ALU.max))
                then(dve.tensor_tensor(RT[:, 1, :, :], lg, bc(RV[:, r, :], 2, 8), ALU.is_equal))
                then(dve.tensor_tensor(RT[:, 2, :, :], RT[:, 1, :, :], rev, ALU.mult))
                then(dve.tensor_reduce(RV[:, 2 + r, :], RT[:, 2, :, :], AX.X, ALU.max))
                then(dve.tensor_tensor(RT[:, 3 + r, :, :], RT[:, 2, :, :], bc(RV[:, 2 + r, :], 2, 8), ALU.is_equal))
                if r == 0:
                    then(dve.scalar_tensor_tensor(out=lg, in0=RT[:, 3, :, :], scalar=-3.0e38, in1=lg,
                                                  op0=ALU.mult, op1=ALU.add))
            then(dve.tensor_tensor(RV[:, 4, :], RV[:, 1, :], RV[:, 0, :], ALU.subtract))
            dve.tensor_tensor(RT[:, 8, :, :], RT[:, 3, :, :], RT[:, 4, :, :], ALU.add).then_inc(S("r_sel"), 1)
            dve.wait_ge(S("r_exp"), 1)
            then(dve.tensor_scalar(RV[:, 6, :], RV[:, 5, :], 1.0, None, ALU.add))
            then(dve.reciprocal(RV[:, 6, :], RV[:, 6, :]))
            then(dve.tensor_tensor(RV[:, 7, :], RV[:, 5, :], RV[:, 6, :], ALU.mult))
            then(dve.tensor_tensor(RT[:, 5, :, :], RT[:, 3, :, :], bc(RV[:, 6, :], 2, 8), ALU.mult))
            then(dve.tensor_tensor(RT[:, 6, :, :], RT[:, 4, :, :], bc(RV[:, 7, :], 2, 8), ALU.mult))
            then(dve.memset(POS[:, :, 2 * N_EXP:NIT], -1.0))
            for c in range(2):
                then(dve.tensor_tensor(GT[:, :, N_EXP * c:N_EXP * c + N_EXP], RT[:, 5, :, :], RT[:, 6, :, :], ALU.add))
            dve.wait_ge(S("r_pos"), 1)
            pos = B(1)[:, 0:16].rearrange("p (x e) -> p x e", e=8)
            then(dve.scalar_tensor_tensor(out=RT[:, 7, :, :], in0=pos, scalar=1.0, in1=RT[:, 8, :, :],
                                          op0=ALU.add, op1=ALU.mult))
            for c in range(2):
                then(dve.tensor_scalar(POS[:, :, N_EXP * c:N_EXP * c + N_EXP], RT[:, 7, :, :], -1.0 - P * c, None, ALU.add))
            then(dve.tensor_reduce(CNT[:, 0:1], B(1)[:, 16:24], AX.X, ALU.max))
            then(dve.tensor_scalar(CNT[:, 1:2], CNT[:, 0:1], float(P), None, ALU.is_gt))
            then(dve.tensor_scalar(CNT[:, 2:3], CNT[:, 1:2], 1.0, None, ALU.add))
            then(dve.tensor_copy(NROUND[:, :], CNT[:, 2:3]))
            dve.wait_ge(S("r_high"), 4)
            for j in range(4):
                x, c = j // 2, slice(512 * (j % 2), 512 * (j % 2) + 512)
                dve.tensor_tensor(XLL[:, x, c], B(4 + j), XLH[:, x, c], ALU.subtract)
            dve.memset(Y, 0.0)
            dve.memset(PT, 0.0)

        def act_route(act):
            act.wait_ge(S("r_sel"), 1)
            act.activation(RV[:, 5, :], RV[:, 4, :], ACT.Exp).then_inc(S("r_exp"), 1)
            act.wait_ge(S("r_rows"), 1)
            for j in range(4):
                act.activation(XLH[:, j // 2, 512 * (j % 2):512 * (j % 2) + 512], B(4 + j),
                               ACT.Copy).then_inc(S("r_high"), 1)

        VB = [6, 7, 0, 1, 2, 3]
        TBK = [4, 5, 6, 7, 0, 1]
        UORD = [0, 1, 4, 5, 2, 3]
        YSEG = []
        for blk in range(2 * FC):
            a, left = 512 * blk, 512
            while left:
                w = min(left, D_FF - a % D_FF)
                YSEG.append((16 + a // D_FF, a % D_FF, blk // 2, blk % 2, 512 - left, w))
                a, left = a + w, left - w
        NEXT_AFTER = 20
        INSERT_U, INSERT_V, INSERT_NEXT, INSERT_ONEHOT = 9, 17, 22, 12

        def rounds(eng, body):
            n = eng.value_load(NROUND[0:1, 0:1], min_val=1, max_val=2)
            with eng.Fori(0, n) as c:
                with eng.Fori(0, N_EXP) as e:
                    body(c * N_EXP + e, e)

        def sp_moe(sp):
            for other in ENG:
                sp.wait_ge(S(f"{other}_stage_done"), MOE_STAGE)

            def body(i, e):
                for q in range(NPIECE):
                    sp.wait_ge(S("m_lo"), NPIECE * i + q + 1)
                    if q < 16:
                        k = q % 8
                        w = t["moe_w1" if q < 8 else "moe_w3"][0, bass.ds(e, 1), P * k:P * k + P, :]
                        src = w.rearrange("a p n -> p (a n)")
                    else:
                        w = t["moe_w2"][0, bass.ds(e, 1), :, :].rearrange("a (p c) n -> p (a c n)", p=P)
                        src = w[:, D_FF * (q - 16):D_FF * (q - 15)]
                    sp.dma_start(RAW[q % NRAW], src).then_inc(S(f"m_raw{q % NRAW}"), 16)
            rounds(sp, body)

        def pe_gather(pe, i):
            pe.wait_ge(S("m_onehot"), 2 * i + 2)
            for k in range(KC):
                for n, (part, x) in enumerate(((XLH, 0), (XLH, 1), (XLL, 0), (XLL, 1))):
                    mm = pe.matmul(B(6 + k // 4)[:, P * (k % 4):P * (k % 4) + P], part[:, x, P * k:P * k + P],
                                   PH[:, x, :], start=n == 0, stop=n == 3)
                if k % 4 == 3:
                    mm.then_inc(S("m_gathered"), 1)

        def pe_scatter(pe, x):
            for h in range(2):
                pe.matmul(B(6 + h), PT[:, x, :], YE[:, 512 * h:512 * h + 512], start=True,
                          stop=True).then_inc(S("m_scattered"), 1)

        def pe_moe_first(pe):
            pe.sem_inc(S("m_used"), 22)
            for h in range(2):
                mm = pe.matmul(B(2 + h)[:, 0:256], PT[:, 0, :], PT.rearrange("p x s -> p (x s)"), start=True, stop=True)
                mm = pe.matmul(B(2 + h)[:, 256:512], PT[:, 0, :], PT.rearrange("p x s -> p (x s)"), start=True, stop=True)
            pe_gather(pe, 0)

        def pe_moe(pe):
            def matrix(i, first, banks, order, done):
                for k in range(KC):
                    q = first + k
                    pe.wait_ge(S("m_lo"), NPIECE * i + q + 1 + NRAW)
                    hi, lo = WHI[q % NSPLIT], WLO[q % NSPLIT]
                    passes = ((HEH, hi), (HEH, lo), (HEL, hi))

                    def product(j, n, a, b):
                        f0, w = FT[j]
                        return pe.matmul(B(banks[j])[:, 0:w], a[:, k, :], b[:, f0:f0 + w], start=k == 0 and n == 0,
                                         stop=k == KC - 1 and n == 2)
                    if k == 0:
                        for j in order:
                            yield j
                            product(j, 0, *passes[0])
                        for n in (1, 2):
                            for j in order:
                                mm = product(j, n, *passes[n])
                        mm.then_inc(S("m_used"), 1)
                    elif k < KC - 1:
                        for n in range(3):
                            for j in order:
                                mm = product(j, n, *passes[n])
                        mm.then_inc(S("m_used"), 1)
                    else:
                        for j in order:
                            for n in range(3):
                                mm = product(j, n, *passes[n])
                            mm.then_inc(S(done), 1)
                    if first == 0 and k in (2, 5):
                        if k == 2:
                            pe.wait_ge(S("m_ye"), 2 * i + 2)
                            pe.wait_ge(S("m_pt"), i + 1)
                        else:
                            pe.wait_ge(S("m_added"), 4 * i + 2)
                        pe_scatter(pe, (k - 2) // 3)

            def body(i, e):
                pe.wait_ge(S("m_he_lo"), 2 * i + 2)
                pe.wait_ge(S("m_pt"), i + 1)
                for j in matrix(i, 0, range(6), UORD, "m_u_full"):
                    if j == 2:
                        pe.wait_ge(S("m_ye"), 2 * i + 2)
                for j in matrix(i, 8, VB, range(6), "m_v_full"):
                    if j == 0:
                        pe.wait_ge(S("m_added"), 4 * i + 4)
                    elif j >= 2:
                        pe.wait_ge(S("m_u"), 6 * i + UORD.index(VB[j]) + 1)
                pe.wait_ge(S("m_u"), 6 * i + 6)
                pe.wait_ge(S("m_hidden"), 6 * i + 6)
                turned = UA.rearrange("p (f c) -> p c f", c=FC)
                for g in range(6):
                    for c in range(4 * g, min(4 * g + 4, FC)):
                        mm = pe.transpose(B(TBK[g])[:, P * (c % 4):P * (c % 4) + P], turned[:, c, :], ident)
                    mm.then_inc(S("m_turned"), 1)
                pe.wait_ge(S("m_ae_lo"), 6 * i + 1)
                pe.wait_ge(S("m_gated"), 2 * i + 2)
                for x in range(2):
                    mm = pe.transpose(B(4)[:, P * x:P * x + P], PG[:, x, :], ident)
                mm.then_inc(S("m_gt"), 1)
                for q in range(16, NPIECE):
                    pe.wait_ge(S("m_lo"), NPIECE * i + q + 1 + NRAW)
                    segs = [g for g in YSEG if g[0] == q]
                    hi, lo = WHI[q % NSPLIT], WLO[q % NSPLIT]
                    pe.wait_ge(S("m_ae_lo"), 6 * i + segs[-1][2] // 4 + 1)
                    for _, a, c, h, o, w in segs:
                        for n, (x, y) in enumerate(((AEH, hi), (AEH, lo), (AEL, hi))):
                            mm = pe.matmul(B(2 + h)[:, o:o + w], x[:, c, :], y[:, a:a + w], start=c == 0 and n == 0,
                                           stop=c == FC - 1 and n == 2)
                    mm.then_inc(S("m_used"), 1)
                    if q == NEXT_AFTER:
                        pe.wait_ge(S("m_ae_lo"), 6 * i + 6)
                        pe_gather(pe, i + 1)
            rounds(pe, body)

        def act_tokens(act, i):
            for h in range(2):
                act.wait_ge(S("m_gathered"), 2 * i + h + 1)
                act.activation(HEH[:, 4 * h:4 * h + 4, :], B(6 + h).rearrange("p (k s) -> p k s", s=P),
                               ACT.Copy).then_inc(S("m_he_hi"), 1)

        def dve_tokens(dve, i):
            for h in range(2):
                dve.wait_ge(S("m_he_hi"), 2 * i + h + 1)
                dve.tensor_tensor(HEL[:, 4 * h:4 * h + 4, :], B(6 + h).rearrange("p (k s) -> p k s", s=P),
                                  HEH[:, 4 * h:4 * h + 4, :], ALU.subtract).then_inc(S("m_he_lo"), 1)

        def dve_onehot(dve, i):
            for x in range(2):
                dve.tensor_scalar(PH[:, x, :], kc(K_IOTA), POS[:, x, bass.ds(i, 1)], None,
                                  ALU.is_equal).then_inc(S("m_onehot"), 1)

        def act_output(act):
            for h in range(2):
                act.activation(YE[:, 512 * h:512 * h + 512], B(2 + h), ACT.Copy).then_inc(S("m_ye"), 1)

        def dve_add(dve, x, count):
            for h in range(2):
                dve.wait_ge(S("m_scattered"), count + h + 1)
                v = Y[:, x, 512 * h:512 * h + 512]
                dve.tensor_tensor(v, B(6 + h), v, ALU.add).then_inc(S("m_added"), 1)

        def act_moe(act):
            def body(i, e):
                for q in range(NPIECE):
                    act.wait_ge(S(f"m_raw{q % NRAW}"), 16 * (6 * i + q // NRAW + 1))
                    if q < 8:
                        act.wait_ge(S("m_used"), 22 * i + 15 + q)
                    elif q == 15:
                        act.wait_ge(S("m_u_full"), 6 * i + 6)
                    elif q == 23:
                        act.wait_ge(S("m_v_full"), 6 * i + 6)
                    else:
                        act.wait_ge(S("m_used"), 22 * i + 22 + q - 7 - (q > 15))
                    act.activation(WHI[q % NSPLIT], RAW[q % NRAW], ACT.Copy).then_inc(S("m_hi"), 1)
                    if q == 0:
                        act.wait_ge(S("m_used"), 22 * i + 22)
                        act_output(act)
                    if q == INSERT_U:
                        for n, j in enumerate(UORD):
                            f0, w = FT[j]
                            act.wait_ge(S("m_u_full"), 6 * i + n + 1)
                            act.activation(UA[:, f0:f0 + w], B(j)[:, 0:w], ACT.Silu).then_inc(S("m_u"), 1)
                    if q == INSERT_V:
                        for g in range(6):
                            n = min(4, FC - 4 * g)
                            act.wait_ge(S("m_turned"), 6 * i + g + 1)
                            act.activation(AEH[:, 4 * g:4 * g + n, :], B(TBK[g])[:, 0:n * P].rearrange(
                                "p (a b) -> p a b", b=P), ACT.Copy).then_inc(S("m_ae_hi"), 1)
                    if q == INSERT_NEXT:
                        act_tokens(act, i + 1)
            rounds(act, body)
            act.drain()
            n = act.value_load(NROUND[0:1, 0:1], min_val=1, max_val=2)
            act.wait_ge(S("m_used"), n * (22 * N_EXP) + 22)
            act_output(act)

        def dve_moe(dve):
            def body(i, e):
                for q in range(NPIECE):
                    dve.wait_ge(S("m_hi"), NPIECE * i + q + 1)
                    dve.tensor_tensor(WLO[q % NSPLIT], RAW[q % NRAW], WHI[q % NSPLIT],
                                      ALU.subtract).then_inc(S("m_lo"), 1)
                    if q == 3:
                        dve_add(dve, 0, 4 * i)
                    if q == 6:
                        dve_add(dve, 1, 4 * i + 2)
                    if q == INSERT_ONEHOT:
                        dve_onehot(dve, i + 1)
                        for x in range(2):
                            dve.tensor_scalar(PG[:, x, :], kc(K_IOTA), POS[:, x, bass.ds(i, 1)], GT[:, x, bass.ds(i, 1)],
                                              ALU.is_equal, ALU.mult).then_inc(S("m_gated"), 1)
                        dve.wait_ge(S("m_added"), 4 * i + 4)
                    if q == INSERT_V:
                        for j, (f0, w) in enumerate(FT):
                            dve.wait_ge(S("m_v_full"), 6 * i + j + 1)
                            dve.wait_ge(S("m_u"), 6 * i + UORD.index(j) + 1)
                            dve.tensor_tensor(UA[:, f0:f0 + w], B(VB[j])[:, 0:w], UA[:, f0:f0 + w],
                                              ALU.mult).then_inc(S("m_hidden"), 1)
                        for g in range(6):
                            n = min(4, FC - 4 * g)
                            dve.wait_ge(S("m_ae_hi"), 6 * i + g + 1)
                            dve.tensor_tensor(AEL[:, 4 * g:4 * g + n, :], B(TBK[g])[:, 0:n * P].rearrange(
                                "p (a b) -> p a b", b=P), AEH[:, 4 * g:4 * g + n, :], ALU.subtract).then_inc(S("m_ae_lo"), 1)
                        dve.wait_ge(S("m_gt"), i + 1)
                        dve.tensor_copy(PT, B(4)[:, 0:256].rearrange("p (a b) -> p a b", b=P)).then_inc(S("m_pt"), 1)
                    if q == INSERT_NEXT:
                        dve_tokens(dve, i + 1)
            rounds(dve, body)

        def pe_moe_last(pe):
            for x in range(2):
                for h in range(2):
                    pe.matmul(B(4 + 2 * x + h), PT[:, x, :], YE[:, 512 * h:512 * h + 512], start=True, stop=True)

        def dve_moe_last(dve):
            for j in range(4):
                v = Y[:, j // 2, 512 * (j % 2):512 * (j % 2) + 512]
                dve.tensor_tensor(v, B(4 + j), v, ALU.add).then_inc(S("y_added"), 1)
            dve.wait_ge(S("y_added"), 4)

        def dve_last(dve):
            dve.tensor_tensor(Y, Y, gate(1, 1, 1).unsqueeze(1).to_broadcast([P, 2, D]), ALU.mult).then_inc(S("y_gated"), 1)
            dve.wait_ge(S("y_gated"), 1)
            dve.tensor_tensor(X[:, 2:4, :], X[:, 2:4, :], Y, ALU.add).then_inc(S("x_done"), 1)

        SMALL = [(K[:, :], t["consts"]), (MASKF, t["masks"]),
                 (X[:, 0:2, :], t["ctx"][0].rearrange("(a p) n -> p a n", p=P)),
                 (X[:, 2:4, :], t["x"][0].rearrange("(a p) n -> p a n", p=P)),
                 (CIN[:, :, 0:1], t["c_ctx"].rearrange("(k p a) -> p k a", p=P, a=1)),
                 (CIN[:, :, 1:2], t["c"].rearrange("a (k p) -> p k a", p=P)),
                 (ROUT[:, :, :], t["moe_router"][0].rearrange("(k p) e -> p k e", p=P)),
                 (QKG[:, :, :, :], t["diff_qk_norm_g"].partition_broadcast(P)),
                 (LAMV[:, :, :, :], t["diff_lambda"].partition_broadcast(P)),
                 (SUBG[:, :, :], t["diff_subln_g"].partition_broadcast(P)),
                 (HNG[:, :, :], t["hgrn_norm_g"].partition_broadcast(P)),
                 (SQKG[:, :, :, :], t["swa_qk_norm_g"].partition_broadcast(P)),
                 (SINK[:, :, :], t["swa_sink"].partition_broadcast(P))]
        for L in range(DEPTH):
            SMALL.append((GMIX[:, L, :].unsqueeze(2), t["norm_mix_g"][L].rearrange("(k p a) -> p k a", p=P, a=1)))
            SMALL.append((GFFN[:, L, :].unsqueeze(2), t["norm_ffn_g"][L].rearrange("(k p a) -> p k a", p=P, a=1)))
            for d in range(2):
                SMALL.append((LBL[:, d, L, :].unsqueeze(2),
                              t["hgrn_lb_logits"][d, L].rearrange("(k p a) -> p k a", p=P, a=1)))

        def dve_setup(dve):
            step = [0]

            def then(ins):
                step[0] += 1
                ins.then_inc(S("setup_step"), 1)
                dve.wait_ge(S("setup_step"), step[0])

            then(dve.memset(NEGH[:, :], -0.5))
            dve.wait_ge(S("small_loaded"), 16 * len(SMALL))
            then(dve.tensor_copy(M8.rearrange("p a b c -> p (a b c)"), MASKF))
            then(dve.tensor_scalar(NSINK[:, :, :], SINK[:, :, :], -1.0, None, ALU.mult))
            l0, l1 = LBL[:, :, 0, :], LBL[:, :, 1, :]
            then(dve.tensor_tensor(LBT[:, 0, :, :], l0, l1, ALU.max))
            then(dve.tensor_tensor(LBT[:, 1, :, :], l0, LBT[:, 0, :, :], ALU.subtract))
            dve.tensor_tensor(LBT[:, 2, :, :], l1, LBT[:, 0, :, :], ALU.subtract).then_inc(S("lb_ready"), 1)
            for L in range(DEPTH):
                for j in range(2):
                    then(dve.tensor_tensor(LAMV[:, L, 2 * j, :], LAMV[:, L, 2 * j, :], LAMV[:, L, 2 * j + 1, :], ALU.mult))
                    then(dve.tensor_reduce(LAM[:, L, j:j + 1], LAMV[:, L, 2 * j, :], AX.X, ALU.add))
            dve.sem_inc(S("lam_ready"), 1)
            dve.wait_ge(S("setup_exp"), 1)
            then(dve.tensor_tensor(LBT[:, 3, :, :], LBT[:, 1, :, :], LBT[:, 2, :, :], ALU.add))
            then(dve.reciprocal(LBT[:, 3, :, :], LBT[:, 3, :, :]))
            then(dve.tensor_tensor(LBT[:, 1, :, :], LBT[:, 1, :, :], LBT[:, 3, :, :], ALU.mult))
            then(dve.tensor_tensor(LBT[:, 2, :, :], LBT[:, 2, :, :], LBT[:, 3, :, :], ALU.mult))
            then(dve.tensor_tensor(LBT[:, 2, :, :], LBT[:, 2, :, :], LBT[:, 1, :, :], ALU.add))
            then(dve.tensor_tensor(LBT[:, 4, :, :], LBT[:, 2, :, :], LBT[:, 1, :, :], ALU.subtract))
            then(dve.tensor_scalar(LBT[:, 5, :, :], LBT[:, 4, :, :], -1.0, 1.0, ALU.mult, ALU.add))
            for L in range(DEPTH):
                lam_init = 0.8 - 0.6 * math.exp(-0.3 * L)
                then(dve.tensor_tensor(LAM[:, L, 4:5], LAM[:, L, 3:4], LAM[:, L, 2:3], ALU.subtract))
                then(dve.tensor_scalar(LAM[:, L, 5:6], LAM[:, L, 4:5], -lam_init, None, ALU.add))

        def act_setup(act):
            act.wait_ge(S("small_loaded"), 16 * len(SMALL))
            act.activation(SC[:, :, :], CIN[:, :, :], ACT.Silu)
            act.wait_ge(S("lb_ready"), 1)
            act.wait_ge(S("lam_ready"), 1)
            act.activation(LAM[:, :, 2:4], LAM[:, :, 0:2], ACT.Exp)
            act.activation(LBT[:, 1:3, :, :], LBT[:, 1:3, :, :], ACT.Exp).then_inc(S("setup_exp"), 1)

        ADA_STAGE = (1, 9)
        MOE_STAGE = 9 * DEPTH

        @block.sync
        def _(sp):
            for dst, src in SMALL:
                sp.dma_start(dst, src, allow_slow_non_contiguous=True).then_inc(S("small_loaded"), 16)
            for key, it in items.items():
                if key[0] == "ada" and key[2] == 0:
                    L = key[1]
                    for other in ENG:
                        sp.wait_ge(S(f"{other}_stage_done"), ADA_STAGE[L])
                    sp.dma_start(ADAB[0:12, :], t["ada_b"][L].rearrange("(a n) -> a n", n=512)).then_inc(
                        S("adab_loaded"), 16)
                for sem, value in it["place_free"]:
                    sp.wait_ge(S(sem), value)
                for dst, src in it["loads"]:
                    sp.dma_start(dst, src).then_inc(S(f"ring_full_{it['place']}"), 16)
            sp_moe(sp)
            sp.wait_ge(S("x_done"), 1)
            sp.dma_start(t["out"][0].rearrange("(a p) n -> p a n", p=P), X[:, 2:4, :]).then_inc(S("stored"), 16)
            sp.wait_ge(S("stored"), 16)

        @block.tensor
        def _(pe):
            stage_end(pe, "pe")
            pe_ada(pe)
            stage_end(pe, "pe")
            for L in range(DEPTH):
                for stage in (lambda e, l: pe_norm(e, l, 0), pe_mix_in, pe_states, pe_qkt,
                              pe_att, None, pe_out):
                    if stage:
                        stage(pe, L)
                    stage_end(pe, "pe")
                pe_norm(pe, L, 1)
                if L == 0:
                    pe_ffn(pe)
                else:
                    pe.wait_ge(S("norm_ht_act"), 28)
                    pe.wait_ge(S("norm_ht_dve"), 28)
                    pe_route(pe)
                stage_end(pe, "pe")
            pe_moe_first(pe)
            stage_end(pe, "pe")
            pe_moe(pe)
            stage_end(pe, "pe")
            pe_moe_last(pe)
            stage_end(pe, "pe")

        @block.scalar
        def _(act):
            act_setup(act)
            stage_end(act, "act")
            act_ada(act)
            stage_end(act, "act")
            for L in range(DEPTH):
                for stage in (lambda e, l: act_norm(e, l, 0), act_proj, act_states, act_qkt,
                              act_att, None, act_out):
                    if stage:
                        stage(act, L)
                    stage_end(act, "act")
                act_norm(act, L, 1)
                if L == 0:
                    act_ffn(act)
                else:
                    act_route(act)
                stage_end(act, "act")
            act_tokens(act, 0)
            stage_end(act, "act")
            act_moe(act)
            stage_end(act, "act")
            stage_end(act, "act")

        @block.gpsimd
        def _(pool):
            stage_end(pool, "pool")
            stage_end(pool, "pool")
            for L in range(DEPTH):
                for stage in (lambda e, l: pool_norm(e, l, 0), pool_mix_in, None,
                              None, lambda e, l: pool_post(e, l, "hp", 128), lambda e, l: pool_post(e, l, "dp", 64), None):
                    if stage:
                        stage(pool, L)
                    stage_end(pool, "pool")
                pool_norm(pool, L, 1)
                stage_end(pool, "pool")
            for _ in range(3):
                stage_end(pool, "pool")

        @block.vector
        def _(dve):
            dve_setup(dve)
            stage_end(dve, "dve")
            dve_ada(dve)
            stage_end(dve, "dve")
            for L in range(DEPTH):
                dve_norm(dve, L, 0)
                stage_end(dve, "dve")
                dve_mix_in(dve, L)
                stage_end(dve, "dve")
                dve_states(dve, L)
                stage_end(dve, "dve")
                dve_qkt(dve, L)
                stage_end(dve, "dve")
                dve_att(dve, L)
                stage_end(dve, "dve")
                for step in range(POST_STEPS):
                    dve_post(dve, L, "dp", step)
                stage_end(dve, "dve")
                dve_out(dve, L)
                stage_end(dve, "dve")
                dve_norm(dve, L, 1)
                if L == 0:
                    dve_ffn(dve)
                else:
                    dve_route(dve)
                stage_end(dve, "dve")
            dve.sem_inc(S("m_lo"), NRAW)
            dve.sem_inc(S("m_pt"), 1)
            dve_onehot(dve, 0)
            dve_tokens(dve, 0)
            stage_end(dve, "dve")
            dve_moe(dve)
            stage_end(dve, "dve")
            stage_end(dve, "dve")
            dve_moe_last(dve)
            dve_last(dve)


_INS = ['x', 'c', 'ctx', 'c_ctx', 'ada_w', 'ada_b', 'norm_mix_g', 'norm_ffn_g', 'w_in', 'w_out',
        'diff_qk_norm_g', 'diff_lambda', 'diff_subln_g', 'hgrn_lb_logits', 'hgrn_norm_g',
        'swa_qk_norm_g', 'swa_sink', 'ffn_w1', 'ffn_w3', 'ffn_w2', 'moe_router', 'moe_w1', 'moe_w3', 'moe_w2']


def kernel(**inputs):
    import concourse.bacc as bacc
    from concourse.bass_utils import run_bass_kernel_spmd

    nc = bacc.Bacc("TRN2", target_bir_lowering=False, num_devices=1)
    arrays, t = {}, {}
    k, masks = constants()
    for name, a in [(n, inputs[n]) for n in _INS] + [("consts", k), ("masks", masks)]:
        a = np.ascontiguousarray(a)
        arrays["in_" + name] = a
        t[name] = nc.dram_tensor("in_" + name, a.shape, mybir.dt.from_np(a.dtype), kind="ExternalInput").ap()
    t["out"] = nc.dram_tensor("out_x", (1, 256, D), F32, kind="ExternalOutput").ap()
    trunk(nc, t)
    r = run_bass_kernel_spmd(nc, [arrays], core_ids=[0])
    return r.results[0]["out_x"]
```
